# Optimizing a Trainium2 kernel written in Bass

```python
import math
import jax, jax.numpy as jnp
from jax import lax
import numpy as np

D_MODEL = 1024
BATCH = 1
SEQ = 1024
DEPTH = 1
DEC_BATCH = 8
DEC_SEQ = 1
PAST_LEN = 8192
PAGE_SIZE = 128

D_MIX = D_MODEL
D_HGRN = D_MIX // 2
D_S5 = D_MIX - D_HGRN
HGRN_HEAD_DIM = 128
HGRN_HEADS = D_HGRN // HGRN_HEAD_DIM
HGRN_CHUNK = 64
S5_GROUP_CH = 16
S5_GROUPS = D_S5 // S5_GROUP_CH
S5_STATE = 64
D_FF = ((8 * D_MODEL // 3 + 127) // 128) * 128
CONV_W = 3
D_IN_PROJ = 4 * D_HGRN + D_S5
ALPHA = (2 * DEPTH) ** 0.25
BETA = (8 * DEPTH) ** -0.25
LN_EPS = 1e-5
RMS_EPS = 1e-6
F_FLOOR = 1e-20

kernel_name = "hymba_hgrn2_s5_convffn_deepnorm_step"

def layer_norm(x, g, b):
    xf = x.astype(jnp.float32)
    mu = jnp.mean(xf, axis=-1, keepdims=True)
    xc = xf - mu
    var = jnp.mean(xc * xc, axis=-1, keepdims=True)
    return (xc * lax.rsqrt(var + LN_EPS) * g.astype(jnp.float32) + b.astype(jnp.float32)).astype(x.dtype)

def hgrn2_chunked(q, log_f, k, v, s0):
    B, T, H, DK = q.shape
    DV = v.shape[-1]
    c = min(HGRN_CHUNK, T)
    n = -(-T // c)
    pad = n * c - T

    def to_chunks(a):
        a = jnp.pad(a, ((0, 0), (0, pad), (0, 0), (0, 0)))
        return a.reshape(B, n, c, H, a.shape[-1]).transpose(1, 0, 2, 3, 4)

    causal = jnp.tril(jnp.ones((c, c), dtype=bool))[None, :, :, None, None]

    def step(S, inp):
        qc, lfc, kc, vc = inp
        b = jnp.cumsum(lfc, axis=1)
        diff = b[:, :, None] - b[:, None]
        decay = jnp.where(causal, jnp.exp(jnp.where(causal, diff, 0.0)), 0.0)
        scores = jnp.einsum('bthd,btshd,bshd->btsh', qc, decay, kc)
        o = (jnp.einsum('btsh,bshe->bthe', scores, vc)
             + jnp.einsum('bthd,bhde->bthe', qc * jnp.exp(b), S))
        b_last = b[:, -1]
        S_new = (jnp.exp(b_last)[..., None] * S
                 + jnp.einsum('bshd,bshe->bhde', kc * jnp.exp(b_last[:, None] - b), vc))
        return S_new, o

    S, o = lax.scan(step, s0, (to_chunks(q), to_chunks(log_f), to_chunks(k), to_chunks(v)))
    o = o.transpose(1, 0, 2, 3, 4).reshape(B, n * c, H, DV)[:, :T]
    return o, S

def hgrn2_mixer(q, fz, iv, g, lb, norm_g, s0):
    B, T, _ = q.shape
    f32 = jnp.float32
    fz32 = fz.astype(f32)
    lb32 = lb.astype(f32)
    f = lb32 + (1.0 - lb32) * jax.nn.sigmoid(fz32)
    log_f = jnp.log(jnp.maximum(f, F_FLOOR))
    k = (1.0 - lb32) * jax.nn.sigmoid(-fz32)
    heads = lambda a: a.reshape(B, T, HGRN_HEADS, HGRN_HEAD_DIM)
    o, s_new = hgrn2_chunked(heads(q.astype(f32)), heads(log_f), heads(k),
                             heads(iv.astype(f32)), s0.astype(f32))
    o = o * lax.rsqrt(jnp.mean(o * o, axis=-1, keepdims=True) + RMS_EPS) * norm_g.astype(f32)
    o = o.reshape(B, T, D_HGRN) * jax.nn.sigmoid(g.astype(f32))
    return o, s_new

def _complex_affine_combine(e1, e2):
    a1r, a1i, b1r, b1i = e1
    a2r, a2i, b2r, b2i = e2
    return (a2r * a1r - a2i * a1i,
            a2r * a1i + a2i * a1r,
            a2r * b1r - a2i * b1i + b2r,
            a2r * b1i + a2i * b1r + b2i)

def s5_mixer(u, lam_re, lam_im, log_dt, b_re, b_im, c_re, c_im, d_skip, w_glu, h_re0, h_im0):
    B, T, _ = u.shape
    f32 = jnp.float32
    u32 = u.astype(f32)
    ug = u32.reshape(B, T, S5_GROUPS, S5_GROUP_CH)
    lr = jnp.minimum(lam_re.astype(f32), -1e-4)
    li = lam_im.astype(f32)
    dt = jnp.exp(log_dt.astype(f32))[:, None]
    mag = jnp.exp(lr * dt)
    ab_re = mag * jnp.cos(li * dt)
    ab_im = mag * jnp.sin(li * dt)
    den = lr * lr + li * li
    nr = ab_re - 1.0
    coef_re = (nr * lr + ab_im * li) / den
    coef_im = (ab_im * lr - nr * li) / den
    br = b_re.astype(f32)
    bi = b_im.astype(f32)
    bb_re = coef_re[..., None] * br - coef_im[..., None] * bi
    bb_im = coef_re[..., None] * bi + coef_im[..., None] * br
    bu_re = jnp.einsum('btgj,gpj->tbgp', ug, bb_re)
    bu_im = jnp.einsum('btgj,gpj->tbgp', ug, bb_im)
    hr = h_re0.astype(f32)
    hi = h_im0.astype(f32)
    bu_re = bu_re.at[0].add(ab_re * hr - ab_im * hi)
    bu_im = bu_im.at[0].add(ab_re * hi + ab_im * hr)
    a_re = jnp.broadcast_to(ab_re, (T, 1, S5_GROUPS, S5_STATE))
    a_im = jnp.broadcast_to(ab_im, (T, 1, S5_GROUPS, S5_STATE))
    _, _, xr, xi = lax.associative_scan(_complex_affine_combine, (a_re, a_im, bu_re, bu_im), axis=0)
    y = (jnp.einsum('tbgp,gjp->btgj', xr, c_re.astype(f32))
         - jnp.einsum('tbgp,gjp->btgj', xi, c_im.astype(f32)))
    y = y.reshape(B, T, D_S5) + d_skip.astype(f32) * u32
    y = jax.nn.gelu(y, approximate=False)
    y = y * jax.nn.sigmoid(y @ w_glu.astype(f32))
    return y, xr[-1], xi[-1]

def conv_ffn(x, w_up, conv_w, conv_b, w_down, buf):
    T = x.shape[1]
    up = x @ w_up
    padded = jnp.concatenate([buf.astype(up.dtype), up], axis=1)
    h = conv_b + padded[:, 0:T] * conv_w[0]
    for j in range(1, CONV_W):
        h = h + padded[:, j:j + T] * conv_w[j]
    val, gate = jnp.split(h, 2, axis=-1)
    out = (jax.nn.silu(gate) * val) @ w_down
    return out, padded[:, -(CONV_W - 1):]

def trunk(x, s_hgrn, s_re, s_im, buf, params):
    (w_in, lb_logits, hgrn_norm_g, lam_re, lam_im, log_dt, b_re, b_im, c_re, c_im, d_skip,
     w_glu, w_out, ln1_g, ln1_b, w_up, conv_w, conv_b, w_down, ln2_g, ln2_b) = params
    sm = jax.nn.softmax(lb_logits.astype(jnp.float32), axis=0)
    lower_bounds = jnp.cumsum(sm, axis=0) - sm[0:1]
    new_h, new_re, new_im, new_buf = [], [], [], []
    for l in range(DEPTH):
        proj = x @ w_in[l]
        q, fz, iv, g, u = jnp.split(proj, [D_HGRN, 2 * D_HGRN, 3 * D_HGRN, 4 * D_HGRN], axis=-1)
        o_a, sa = hgrn2_mixer(q, fz, iv, g, lower_bounds[l], hgrn_norm_g[l], s_hgrn[l])
        o_b, sr, si = s5_mixer(u, lam_re[l], lam_im[l], log_dt[l], b_re[l], b_im[l],
                               c_re[l], c_im[l], d_skip[l], w_glu[l], s_re[l], s_im[l])
        mix = jnp.concatenate([o_a.astype(x.dtype), o_b.astype(x.dtype)], axis=-1) @ w_out[l]
        x = layer_norm(ALPHA * x + mix, ln1_g[l], ln1_b[l])
        ff, nb = conv_ffn(x, w_up[l], conv_w[l], conv_b[l], w_down[l], buf[l])
        x = layer_norm(ALPHA * x + ff, ln2_g[l], ln2_b[l])
        new_h.append(sa)
        new_re.append(sr)
        new_im.append(si)
        new_buf.append(nb)
    return x, jnp.stack(new_h), jnp.stack(new_re), jnp.stack(new_im), jnp.stack(new_buf)

def setup_inputs(seed: int = 0) -> dict:
    key = jax.random.key(seed)
    ks = jax.random.split(key, 32)
    f32 = jnp.float32
    nrm = lambda k, shape, s: jax.random.normal(k, shape, f32) * s
    lam_im_base = math.pi * jnp.arange(S5_STATE, dtype=f32)
    return {
        "x_prompt": nrm(ks[0], (BATCH, SEQ, D_MODEL), 1.0),
        "x_sample": nrm(ks[1], (DEC_BATCH, DEC_SEQ, D_MODEL), 1.0),
        "state_hgrn": nrm(ks[2], (DEPTH, DEC_BATCH, HGRN_HEADS, HGRN_HEAD_DIM, HGRN_HEAD_DIM), 0.5),
        "state_s5_re": nrm(ks[3], (DEPTH, DEC_BATCH, S5_GROUPS, S5_STATE), 0.5),
        "state_s5_im": nrm(ks[4], (DEPTH, DEC_BATCH, S5_GROUPS, S5_STATE), 0.5),
        "cache_ffn_conv": nrm(ks[5], (DEPTH, DEC_BATCH, CONV_W - 1, 2 * D_FF), 1.0),
        "w_in": nrm(ks[6], (DEPTH, D_MODEL, D_IN_PROJ), D_MODEL ** -0.5),
        "hgrn_lb_logits": nrm(ks[7], (DEPTH, D_HGRN), 0.1),
        "hgrn_norm_g": 1.0 + nrm(ks[8], (DEPTH, HGRN_HEAD_DIM), 0.02),
        "s5_lambda_re": -0.5 + nrm(ks[9], (DEPTH, S5_GROUPS, S5_STATE), 0.01),
        "s5_lambda_im": lam_im_base + nrm(ks[10], (DEPTH, S5_GROUPS, S5_STATE), 0.01),
        "s5_log_dt": jax.random.uniform(ks[11], (DEPTH, S5_GROUPS), f32,
                                        math.log(0.001), math.log(0.1)),
        "s5_b_re": nrm(ks[12], (DEPTH, S5_GROUPS, S5_STATE, S5_GROUP_CH), (2 * S5_GROUP_CH) ** -0.5),
        "s5_b_im": nrm(ks[13], (DEPTH, S5_GROUPS, S5_STATE, S5_GROUP_CH), (2 * S5_GROUP_CH) ** -0.5),
        "s5_c_re": nrm(ks[14], (DEPTH, S5_GROUPS, S5_GROUP_CH, S5_STATE), (2 * S5_STATE) ** -0.5),
        "s5_c_im": nrm(ks[15], (DEPTH, S5_GROUPS, S5_GROUP_CH, S5_STATE), (2 * S5_STATE) ** -0.5),
        "s5_d": nrm(ks[16], (DEPTH, D_S5), 1.0),
        "w_glu": nrm(ks[17], (DEPTH, D_S5, D_S5), D_S5 ** -0.5),
        "w_out": nrm(ks[18], (DEPTH, D_MIX, D_MODEL), BETA * D_MIX ** -0.5),
        "ln1_g": 1.0 + nrm(ks[19], (DEPTH, D_MODEL), 0.02),
        "ln1_b": nrm(ks[20], (DEPTH, D_MODEL), 0.01),
        "w_ffn_up": nrm(ks[21], (DEPTH, D_MODEL, 2 * D_FF), D_MODEL ** -0.5),
        "ffn_conv_w": nrm(ks[22], (DEPTH, CONV_W, 2 * D_FF), CONV_W ** -0.5),
        "ffn_conv_b": nrm(ks[23], (DEPTH, 2 * D_FF), 0.01),
        "w_ffn_down": nrm(ks[24], (DEPTH, D_FF, D_MODEL), BETA * D_FF ** -0.5),
        "ln2_g": 1.0 + nrm(ks[25], (DEPTH, D_MODEL), 0.02),
        "ln2_b": nrm(ks[26], (DEPTH, D_MODEL), 0.01),
    }

def reference(x_prompt, x_sample, state_hgrn, state_s5_re, state_s5_im, cache_ffn_conv,
              w_in, hgrn_lb_logits, hgrn_norm_g, s5_lambda_re, s5_lambda_im, s5_log_dt,
              s5_b_re, s5_b_im, s5_c_re, s5_c_im, s5_d, w_glu, w_out, ln1_g, ln1_b,
              w_ffn_up, ffn_conv_w, ffn_conv_b, w_ffn_down, ln2_g, ln2_b):
    params = (w_in, hgrn_lb_logits, hgrn_norm_g, s5_lambda_re, s5_lambda_im, s5_log_dt,
              s5_b_re, s5_b_im, s5_c_re, s5_c_im, s5_d, w_glu, w_out, ln1_g, ln1_b,
              w_ffn_up, ffn_conv_w, ffn_conv_b, w_ffn_down, ln2_g, ln2_b)
    bp = x_prompt.shape[0]
    f32 = jnp.float32
    zero_h = jnp.zeros((DEPTH, bp, HGRN_HEADS, HGRN_HEAD_DIM, HGRN_HEAD_DIM), f32)
    zero_s = jnp.zeros((DEPTH, bp, S5_GROUPS, S5_STATE), f32)
    zero_buf = jnp.zeros((DEPTH, bp, CONV_W - 1, 2 * D_FF), x_prompt.dtype)
    y_prompt, h_p, re_p, im_p, buf_p = trunk(x_prompt, zero_h, zero_s, zero_s, zero_buf, params)
    y_sample, h_s, re_s, im_s, buf_s = trunk(x_sample, state_hgrn, state_s5_re, state_s5_im,
                                             cache_ffn_conv, params)
    return (y_prompt, y_sample, h_p, re_p, im_p, buf_p, h_s, re_s, im_s, buf_s)


_drawn_inputs = setup_inputs


def setup_inputs(seed=0):
    import zlib

    import numpy as np

    out = dict(_drawn_inputs(seed))
    spreads = {}
    factors = {'hgrn_norm_g': 8.0,
     's5_lambda_re': 4.075,
     'ln1_g': 2.715,
     'ln1_b': 5.65,
     'ffn_conv_b': 8.0,
     'ln2_g': 2.804,
     'ln2_b': 5.605}
    for name, (base, spread) in spreads.items():
        noise = np.random.default_rng([zlib.crc32(name.encode()), seed]).standard_normal(out[name].shape)
        drawn = base * np.exp(spread * noise) if base else spread * noise
        out[name] = __import__('jax').numpy.asarray(drawn.astype(out[name].dtype))
    for name, factor in factors.items():
        out[name] = (out[name] * factor).astype(out[name].dtype)
    return out
```

```python
import concourse.bass as bass
from concourse import mybir
from contextlib import ExitStack

F32 = mybir.dt.float32
F32R = mybir.dt.float32r
ALU = mybir.AluOpType
ACT = mybir.ActivationFunctionType

P = 128
D = 1024
KD = D // P
TP = 1024
NS = 8
T = TP + NS
NB = 3
CW = T // NB
HEADS = 4
CH = 128
NC = TP // CH
FF = 2816
JT = FF // P
G = 32
GC = G // HEADS
PR = GC // 2
SS = 64
L = 8
NL = TP // L
UC = NS + NL + NS
HC = NS + 1 + NL
ALPHA = 2.0 ** 0.25
LN_EPS = 1e-5
RMS_EPS = 1e-6
F_FLOOR = 1e-20
TWO60 = 2.0 ** 60
PARTS = [(0, 8), (8, 7), (15, 7)]
TWO_PI_1 = 6.28125
TWO_PI_2 = 0.0019350051879882812
TWO_PI_3 = 3.019916050e-07
INV_TWO_PI = 0.15915494309189535
ROUND = 12582912.0
PI_SAFE = 3.1415925
U_N, F_N, GLU_N, OUT_N, FFN_N = 0, 4, 16, 20, 28
Y_GROUPS = [(0, 2, 4), (6,), (1, 3, 5), (7,)]
LEVELS = [1, 2, 4, 8, 16, 32, 64]


def unit_of(kind, h):
    return F_N + 3 * h + kind


def order():
    o = [("s5_prep", 0)] + [("unit", n) for n in range(2)] + [("values", 0)]
    o += [("unit", 2), ("unit", 3)]
    units = list(range(F_N, OUT_N))
    take = lambda: [("unit", units.pop(0))]
    for c in range(HEADS):
        if c:
            o += [("s5_prep", c)] + take()
        o += [("s5_in", c)] + take() + [("s5_out", c)]
    for h in range(HEADS):
        if h == 2:
            while units[0] < GLU_N:
                o += take()
            o += [("gelu", c) for c in range(HEADS)]
        o += [("h_prep", h), ("level_prep", h, 1)]
        for l in range(len(LEVELS) + 1):
            if 1 <= l < len(LEVELS):
                o += [("level_prep", h, l + 1)]
            o += [("level", h, l)]
            if l in (2, 5) and units and (units[0] < GLU_N or h >= 2):
                o += take()
        o += [("state", h), ("h_out", h)]
    assert not units
    o += [("mix", h) for h in range(HEADS)]
    o += [("unit", n) for n in range(OUT_N, FFN_N)]
    return o


ORDER = order()


def bank_uses():
    names = []
    for s in ORDER:
        if s[0] == "s5_in":
            names += [(s[0], s[1], x) for x in ("wre", "wim", "k0", "k1", "dre0", "dim0", "dre1", "dim1")]
        elif s[0] == "s5_out":
            names += [(s[0], s[1], x) for x in range(4)]
        elif s[0] == "level":
            names += [(s[0], s[1], s[2], b) for b in range(2)]
        elif s[0] == "state":
            names += [(s[0], s[1], x) for x in ("t0", "t1", "kv0", "kv1", "vb0", "vb1")]
        elif s[0] == "h_out":
            names += [(s[0], s[1], x) for x in ("o0", "o1", "os", "m0", "m1", "m2")]
    names += [("ln", w, x, i) for w in range(2) for x in ("mean",) for i in range(NB)]
    return {name: (i % 2, i // 2) for i, name in enumerate(names)}


USES = bank_uses()


class Lane:

    def __init__(self, eng, own):
        self.eng, self.own, self.count, self.last = eng, own, {}, None

    def __call__(self, ins, event=None, by=1):
        if isinstance(event, tuple):
            ins.then_inc(event[0], by)
            self.last = event
            return event
        sem = self.own if event is None else event
        ins.then_inc(sem, by)
        key = id(sem)
        self.count[key] = self.count.get(key, 0) + by
        self.last = (sem, self.count[key])
        return self.last

    def sync(self, token=None):
        token = token or self.last
        if token:
            self.eng.wait_ge(*token)


def layer(nc, xT, w_units, w_v, w_glu, w_out, w_up, w_dn, s5p, dskip, lbl, normg, lnp, convp, s0, cache_old,
          yT, hp, s5st, cache_new, hs, cache_row0):
    ctx = ExitStack()
    with ctx:
        def sb(name, shape, dt=F32, c=ctx):
            return c.enter_context(nc.sbuf_tensor(name, shape, dt))

        def sem(name):
            return ctx.enter_context(nc.semaphore(name))

        XH, XL = sb("XH", [P, KD, T], F32R), sb("XL", [P, KD, T], F32R)
        raw = [sb(f"raw{i}", [P, KD * P]) for i in range(2)]
        wh = [sb(f"wh{i}", [P, KD * P], F32R) for i in range(2)]
        wl = [sb(f"wl{i}", [P, KD * P], F32R) for i in range(2)]
        ident = sb("ident", [P, P])
        ones_rms = sb("ones_rms", [P, P])
        ones_ln = sb("ones_ln", [P, P])
        one = sb("one", [P, 1])
        eps_rms, eps_ln = sb("eps_rms", [P, 1]), sb("eps_ln", [P, 1])
        lb, oml, lbt = sb("lb", [P, HEADS]), sb("oml", [P, HEADS]), sb("lbt", [P, 3, HEADS])
        ng, ln_sb = sb("ng", [P, 1]), sb("ln_sb", [P, 4, KD])
        psum = ctx.enter_context(nc.psum_tensor("psum", [P, 8, 512], F32))

        ph1 = ExitStack()
        masks = sb("masks", [P, len(LEVELS) + 1, P], mybir.dt.int8, ph1)
        V, Vs = sb("V", [P, NC, 512], F32, ph1), sb("Vs", [NS, 512], F32, ph1)
        st = [sb(f"st{i}", [P, GC * (NS + NL)], F32, ph1) for i in range(3)]
        pa = ExitStack()
        WVH, WVL = sb("WVH", [P, KD, 512], F32R, pa), sb("WVL", [P, KD, 512], F32R, pa)
        U = sb("U", [P, GC, UC], F32, pa)
        TM = sb("TM", [P, GC, P], F32, pa)
        BT = [sb(f"BT{i}", [P, PR, P], F32, pa) for i in range(2)]
        prm = sb("prm", [P, 332], F32, pa)
        CA = [sb(f"CA{i}", [P, PR, L + 1, 16], F32, pa) for i in range(2)]
        E = sb("E", [P, 2, PR, NL], F32, pa)
        PW = sb("PW", [P, 2, PR, L + 1], F32, pa)
        G5 = [sb(f"G5{i}", [P, PR, NL], F32, pa) for i in range(2)]
        H5 = [sb(f"H5{i}", [P, PR, HC], F32, pa) for i in range(2)]
        ds_ = [sb(f"ds{i}", [P, PR, NS], F32, pa) for i in range(2)]
        KS = sb("KS", [16, GC, P], F32, pa)
        Ysb = sb("Ysb", [P, GC, NS + NL], F32, pa)
        dk = sb("dk", [16, G], F32, pa)
        sm = sb("sm", [P, 40, PR], F32, pa)
        bb = [sb(f"bb{i}", [P, PR, 16], F32, pa) for i in range(2)]
        s5o = sb("s5o", [P, 2, PR, NS + 1], F32, pa)
        ta5, tb5 = sb("ta5", [P, 1024], F32, pa), sb("tb5", [P, 1024], F32, pa)
        WB = [H5[i][:, :, NS + 1:NS + 1 + NL] for i in range(2)]
        pa.close()
        pb = ExitStack()
        FZ, Q = [sb(f"FZ{i}", [P, T], F32, pb) for i in range(2)], [sb(f"Q{i}", [P, T], F32, pb) for i in range(2)]
        SG, K, B = sb("SG", [P, T], F32, pb), sb("K", [P, T], F32, pb), sb("B", [P, T], F32, pb)
        tA, tB = sb("tA", [P, T], F32, pb), sb("tB", [P, T], F32, pb)
        EL = [sb(f"EL{i}", [P, T], F32, pb) for i in range(3)]
        Qs = sb("Qs", [P, TP], F32, pb)
        SC = sb("SC", [P, NC, CH], F32, pb)
        KT = sb("KT", [P, NC, CH], F32, pb)
        S_all = sb("S_all", [P, NC + 1, P], F32, pb)
        S0 = sb("S0", [P, NS, P], F32, pb)
        O = sb("O", [P, T], F32, pb)
        A8 = sb("A8", [P, NC], F32, pb)
        sel = sb("sel", [NS, NS, P], F32, pb)
        pb.close()
        ph1.close()
        R = sb("R", [P, KD, T])
        p2 = ExitStack()
        xt = [sb(f"xt{i}", [P, T], F32, p2) for i in range(2)]
        racc = sb("racc", [P, T], F32, p2)
        sq = [sb(f"sq{i}", [P, T], F32, p2) for i in range(2)]
        rstd = sb("rstd", [P, T], F32, p2)
        p2.close()
        AH, AL = sb("AH", [P, PARTS[0][1], T], F32R), sb("AL", [P, PARTS[0][1], T], F32R)
        ub = [sb(f"ub{i}", [P, 2 + T]) for i in range(2)]
        hb = [sb(f"hb{i}", [P, T]) for i in range(2)]
        cp = [sb(f"cp{i}", [P, 20]) for i in range(2)]

        uscr = nc.dram_tensor("uscr", [HEADS, P, T], F32).ap()
        fscr = nc.dram_tensor("fscr", [3 * HEADS, P, T], F32).ap()
        yscr = nc.dram_tensor("yscr", [HEADS, P, GC * (NS + NL)], F32).ap()
        oscr = nc.dram_tensor("oscr", [HEADS, P, T], F32).ap()

        def sems(names):
            return (sem(x) for x in names.split())

        def two(name):
            return [sem(f"{name}{i}") for i in range(2)]

        loaded = two("loaded")
        hi_done, lo_done = sems("hi_done lo_done")
        mm_done = sem("mm_done")
        evac = two("evac")
        fill, free = two("fill"), two("free")
        act_own, dve_own, pool_own = sems("act_own dve_own pool_own")
        small_in, consts, dconsts, lbd, lbe = sems("small_in consts dconsts lbd lbe")
        x_in, (x_hi, x_lo) = two("x_in"), sems("x_hi x_lo")
        wv_in, (wv_hi, wv_lo) = two("wv_in"), sems("wv_hi wv_lo")
        v_mm, v_ev = two("v_mm"), two("v_ev")
        st_out = [sem(f"st_out{i}") for i in range(3)]
        prm_in, u_in, t_in = sems("prm_in u_in t_in")
        p_dt, p_e, p_ang, p_sin, wb_ready, ca_ready, k_ready = sems("p_dt p_e p_ang p_sin wb_ready ca_ready k_ready")
        h5_ready, ys_out, s5_full, s5_out = sems("h5_ready ys_out s5_full s5_out")
        fq_in, (sg_in, s0_in) = two("fq_in"), sems("sg_in s0_in")
        sig_done, sig_g, lnarg, ln_done, b_ready = sems("sig_done sig_g lnarg ln_done b_ready")
        ex_arg, ex_done, ex_a8, lv_ready, qs_ready = sems("ex_arg ex_done ex_a8 lv_ready qs_ready")
        sn_ready, sq_ready, rms_e, o_full, o_out, st_saved = sems("sn_ready sq_ready rms_e o_full o_out st_saved")
        y_in, g_ready, g_hi, g_lo = sems("y_in g_ready g_hi g_lo")
        z_ready, z_hi, z_lo, oa_in, m_hi, m_lo = sems("z_ready z_hi z_lo oa_in m_hi m_lo")
        xt_in, (racc_ready, xc_ready, sq_done, sq_mm) = two("xt_in"), sems("racc_ready xc_ready sq_done sq_mm")
        var_e, t_ready, x1_hi, x1_lo, y_out = sems("var_e t_ready x1_hi x1_lo y_out")
        cp_in, cache_out = two("cp_in"), two("cache_out")
        halo, u_full, h0_ready, conv_done, silu_done = sems("halo u_full h0_ready conv_done silu_done")
        a_ready, a_hi, a_lo, row0_out = sems("a_ready a_hi a_lo row0_out")
        block = ctx.enter_context(nc.Block())

        def banks(slot):
            return psum[:, 3 * slot:3 * slot + 3, 0:CW]

        def b3(ap):
            return ap.rearrange("p (b n) -> p b n", b=NB)

        def evacuated(n):
            return evac[n % 2], n // 2 + 1

        def filled(name):
            b, k = USES[name]
            return fill[b], k + 1

        def freed(name):
            b, k = USES[name]
            return free[b], k + 1

        def static_source(n):
            if n < GLU_N:
                return w_units[n], KD * P
            if n < OUT_N:
                return w_glu[n - GLU_N], HEADS * P
            return w_out[n - OUT_N], KD * P

        def after_unit(n):
            return n + 2 if n + 2 < FFN_N else None

        @block.sync
        def _(sp):
            def load_weights(n, half, slot, src, width):
                if not isinstance(n, int) or n >= 2:
                    sp.wait_ge(lo_done, n - 1)
                sp.dma_start(raw[slot][:, 0:width], src).then_inc(loaded[slot], 16)

            def load_x(k):
                if k >= 2:
                    sp.wait_ge(x_lo, k - 1)
                sp.dma_start(st[k % 2][:, 0:T], xT[k]).then_inc(x_in[k % 2], 16)

            def load_wv(k):
                s = k % 2
                if k >= 2:
                    sp.wait_ge(wv_lo, k - 1)
                sp.dma_start(G5[s][:, :, :].rearrange("p r n -> p (r n)"), w_v[k]).then_inc(wv_in[s], 16)

            def store_unit(n):
                sp.wait_ge(*evacuated(n))
                dst = uscr[n] if n < F_N else fscr[n - F_N]
                sp.dma_start(dst, st[n % 3][:, 0:T]).then_inc(st_out[n % 3], 16)

            def load_u(c):
                sp.wait_ge(st_out[c % 3], 16 * (c // 3 + 1))
                if c == 0:
                    sp.wait_ge(consts, 1)
                else:
                    sp.wait_ge(*filled(("s5_out", c - 1, 3)))
                v = uscr[c].rearrange("(g j) n -> j g n", j=16)
                for s in range(L):
                    sp.dma_start(U[16 * s:16 * s + 16, :, NS:NS + NL], v[:, :, NL * (7 - s):NL * (8 - s)]).then_inc(u_in, 16)
                sp.dma_start(U[16 * 7:16 * 8, :, 0:NS], v[:, :, TP:T]).then_inc(u_in, 16)
                sp.dma_start(U[0:16, :, NS + NL:UC], v[:, :, TP:T]).then_inc(u_in, 16)

            for src, dst in ((lbl, lbt[:, 0, :]), (normg, ng[:, :]), (lnp, ln_sb[:, :, :]), (dskip, dk[:, :])):
                sp.dma_start(dst, src).then_inc(small_in, 16)
            sp.dma_start(prm[:, :], s5p[0]).then_inc(prm_in, 16)
            load_x(0)
            load_x(1)
            load_weights(0, 0, 0, w_units[0], KD * P)
            for k in range(2, KD):
                load_x(k)
            load_weights(1, 0, 1, w_units[1], KD * P)
            sp.dma_start(cache_row0, cache_old[:, 1, :]).then_inc(row0_out, 16)
            for step in ORDER:
                kind, c = step[0], step[1]
                if kind == "unit":
                    if c < GLU_N:
                        store_unit(c)
                    if after_unit(c) is not None:
                        src, width = static_source(c + 2)
                        load_weights(c + 2, 0, c % 2, src, width)
                    if c >= OUT_N and c - OUT_N + 2 < KD:
                        m = c - OUT_N + 2
                        sp.wait_ge(*evacuated(c))
                        sp.dma_start(xt[m % 2][:, :], xT[m]).then_inc(xt_in[m % 2], 16)
                elif kind == "values":
                    for k in range(KD):
                        load_wv(k)
                elif kind == "s5_prep" and c:
                    sp.wait_ge(s5_full, c)
                    sp.dma_start(prm[:, :], s5p[c]).then_inc(prm_in, 16)
                elif kind == "s5_in":
                    load_u(c)
                    sp.wait_ge(k_ready, 2 * (c + 1))
                    if c:
                        sp.wait_ge(*filled(("s5_out", c - 1, 3)))
                    for s in range(L):
                        sp.dma_start(TM[16 * (7 - s):16 * (8 - s), :, 16 * s:P], KS[:, :, 0:P - 16 * s]).then_inc(t_in, 16)
                elif kind == "s5_out":
                    sp.wait_ge(s5_full, c + 1)
                    sp.dma_start(s5st[c], s5o[:, :, :, :]).then_inc(s5_out, 16)
                    sp.wait_ge(*freed(("s5_out", c, 3)))
                    sp.wait_ge(*freed(("s5_out", c, 2)))
                    sp.dma_start(yscr[c], Ysb[:, :, :].rearrange("p g n -> p (g n)")).then_inc(ys_out, 16)
                elif kind == "h_prep":
                    for i in range(3):
                        sp.wait_ge(st_out[unit_of(i, c) % 3], 16 * (unit_of(i, c) // 3 + 1))
                    if c == 0:
                        sp.wait_ge(ys_out, 16 * HEADS)
                        sp.wait_ge(s5_out, 16 * HEADS)
                    else:
                        sp.wait_ge(o_full, c)
                        sp.wait_ge(st_saved, 32 * c)
                    sp.dma_start(FZ[c % 2][:, :], fscr[3 * c]).then_inc(fq_in[c % 2], 16)
                    sp.dma_start(Q[c % 2][:, :], fscr[3 * c + 1]).then_inc(fq_in[c % 2], 16)
                    sp.dma_start(SG[:, :], fscr[3 * c + 2]).then_inc(sg_in, 16)
                    sp.dma_start(S0[:, :, :], s0[:, c].rearrange("b d e -> d b e")).then_inc(s0_in, 16)
                elif kind == "h_out":
                    sp.wait_ge(*freed(("state", c, "kv1")))
                    sp.dma_start(hp[c], S_all[:, NC, :]).then_inc(st_saved, 16)
                    sp.wait_ge(sn_ready, c + 1)
                    sp.dma_start(hs[:, c].rearrange("b d e -> d b e"), S0[:, :, :]).then_inc(st_saved, 16)
                    sp.wait_ge(o_full, c + 1)
                    sp.dma_start(oscr[c], O[:, :]).then_inc(o_out, 16)
                elif kind == "gelu":
                    if c == 0:
                        for i in range(3):
                            sp.wait_ge(st_out[i], 16 * len([n for n in range(GLU_N) if n % 3 == i]))
                        sp.wait_ge(ys_out, 16 * HEADS)
                    else:
                        sp.wait_ge(g_ready, c)
                    v = yscr[c].rearrange("(t j) (g n) -> j g t n", j=16, g=GC)
                    for g in range(GC):
                        sp.dma_start(st[0][16 * g:16 * g + 16, :].rearrange("p (t n) -> p t n", t=L), v[:, g]).then_inc(y_in, 16)
                elif kind == "mix":
                    if c == 0:
                        sp.wait_ge(z_lo, HEADS)
                    sp.wait_ge(o_out, 16 * (c + 1))
                    if c >= 1:
                        sp.wait_ge(m_lo, c)
                    sp.dma_start(st[0][:, 0:T], oscr[c]).then_inc(oa_in, 16)
                    if c == HEADS - 1:
                        sp.wait_ge(m_lo, HEADS)
                        sp.wait_ge(st_saved, 32 * HEADS)
                        for m in range(2):
                            sp.dma_start(xt[m][:, :], xT[m]).then_inc(xt_in[m], 16)
            def conv_params(j0, i, s, first):
                if not first:
                    sp.wait_ge(conv_done, 2 * (j0 + i) + s - 1)
                sp.dma_start(cp[s][:, :], convp[bass.ds(2 * (j0 + i) + s, 1)].rearrange("a p n -> p (a n)")).then_inc(cp_in[s], 16)

            def store_cache(j):
                for s in range(2):
                    sp.wait_ge(u_full, 2 * j + s + 1)
                    sp.dma_start(cache_new[bass.ds(2 * j + s, 1)].rearrange("a p n -> p (a n)"), ub[s][:, TP:2 + T]).then_inc(cache_out[s], 16)

            n0 = FFN_N
            for j0, nk in PARTS:
                def pair(i, first=False):
                    for s in range(2):
                        load_weights(n0 + 2 * i + s, 0, s, w_up[bass.ds(2 * (j0 + i) + s, 1)].rearrange("a p n -> p (a n)"), KD * P)
                        conv_params(j0, i, s, first)
                    if not first:
                        store_cache(j0 + i - 1)
                if j0 == 0:
                    pair(0, True)
                    with sp.Fori(1, nk) as i:
                        pair(i)
                else:
                    with sp.Fori(0, nk) as i:
                        pair(i)
                n0 += 2 * nk
                with sp.Fori(0, KD // 2) as i:
                    for s in range(2):
                        load_weights(n0 + 2 * i + s, 0, s,
                                     w_dn[bass.ds(2 * i + s, 1), :, j0 * P:(j0 + nk) * P].rearrange("a p n -> p (a n)"), nk * P)
                n0 += KD
            store_cache(JT - 1)
            for m in range(KD):
                sp.wait_ge(x1_hi, KD + m + 1)
                sp.dma_start(yT[m], R[:, m, :]).then_inc(y_out, 16)
            sp.wait_ge(y_out, 16 * KD)
            sp.wait_ge(row0_out, 16)
            sp.wait_ge(s5_out, 16 * HEADS)
            sp.wait_ge(st_saved, 32 * HEADS)
            for s in range(2):
                sp.wait_ge(cache_out[s], 16 * JT)

        @block.scalar
        def _(act):
            me = Lane(act, act_own)

            def split_hi(n, count, slot, width):
                act.wait_ge(loaded[slot], 16 * count)
                if not isinstance(n, int) or n >= 2:
                    act.wait_ge(mm_done, n - 1)
                me(act.activation(wh[slot][:, 0:width], raw[slot][:, 0:width], ACT.Copy), hi_done)

            act.wait_ge(small_in, 64)
            act.wait_ge(lbd, 1)
            me(act.activation(lbt[:, 1, :], lbt[:, 1, :], ACT.Exp), lbe)
            for k in range(KD):
                act.wait_ge(x_in[k % 2], 16 * (k // 2 + 1))
                me(act.activation(XH[:, k, :], st[k % 2][:, 0:T], ACT.Copy), x_hi)
                if k == 1:
                    split_hi(0, 1, 0, KD * P)
            split_hi(1, 1, 1, KD * P)
            nx = {}

            def use(name):
                b, k = USES[name]
                act.wait_ge(fill[b], k + 1)
                return psum[:, 6 + b, :], (free[b], k + 1)

            for step in ORDER:
                kind, c = step[0], step[1]
                if kind == "unit":
                    s, h = c % 2, c // 2
                    act_unit = c < OUT_N
                    if act_unit:
                        act.wait_ge(mm_done, c + 1)
                    if c < GLU_N:
                        if c >= 3:
                            act.wait_ge(st_out[c % 3], 16 * (c // 3))
                        elif c < 2:
                            act.wait_ge(x_lo, KD)
                        dst = st[c % 3][:, 0:T]
                        if c < F_N:
                            for b in range(NB):
                                nn = min(CW, TP - b * CW) // L
                                me(act.activation(dst[:, 0:TP].rearrange("p (t n) -> p n t", t=L)[:, 43 * b:43 * b + nn, :],
                                                  psum[:, 3 * s + b, 0:nn * L].rearrange("p (n t) -> p n t", t=L), ACT.Copy))
                            me(act.activation(dst[:, TP:T], psum[:, 3 * s + 2, CW - NS:CW], ACT.Copy), evacuated(c))
                        else:
                            me(act.activation(b3(dst), banks(s), ACT.Copy), evacuated(c))
                    elif c < OUT_N:
                        m = c - GLU_N
                        if m:
                            act.wait_ge(z_lo, m)
                        else:
                            act.wait_ge(g_lo, HEADS)
                        me(act.activation(b3(st[1][:, 0:T]), banks(s), ACT.Sigmoid), evacuated(c))
                        act.wait_ge(z_ready, m + 1)
                        me(act.activation(XH[:, HEADS + m, :], st[2][:, 0:T], ACT.Copy), z_hi)
                    if after_unit(c) is not None:
                        _, width = static_source(c + 2)
                        split_hi(c + 2, h + 2, s, width)
                elif kind == "values":
                    for k in range(KD):
                        act.wait_ge(wv_in[k % 2], 16 * (k // 2 + 1))
                        me(act.activation(WVH[:, k, :], G5[k % 2][:, :, :].rearrange("p r n -> p (r n)"), ACT.Copy), wv_hi)
                    for t in range(NC + 1):
                        act.wait_ge(v_mm[t % 2], t // 2 + 1)
                        rows = P if t < NC else NS
                        dst = V[:, t, :] if t < NC else Vs[:, :]
                        me(act.activation(dst, psum[0:rows, 6 + t % 2, :], ACT.Copy), v_ev[t % 2])
                elif kind == "s5_prep":
                    act.wait_ge(prm_in, 16 * (c + 1))
                    if c:
                        act.wait_ge(s5_full, c)
                    me(act.activation(sm[:, 0, :], prm[:, 8:12], ACT.Exp), p_dt)
                    act.wait_ge(p_e, c + 1)
                    me(act.activation(sm[:, 2, :], sm[:, 1, :], ACT.Exp))
                    me(act.activation(sm[:, 3, :], sm[:, 1, :], ACT.Exp, scale=float(L)))
                    act.wait_ge(p_ang, c + 1)
                    me(act.activation(sm[:, 6:8, :], sm[:, 4:6, :], ACT.Sin), p_sin)
                elif kind == "s5_in":
                    for i, x in enumerate(("wre", "wim")):
                        ps, fr = use((kind, c, x))
                        me(act.activation(BT[i][:, :, :], ps.rearrange("p (r n) -> p r n", r=PR), ACT.Copy), fr)
                elif kind == "s5_out":
                    act.wait_ge(s5_full, c + 1)
                    if c:
                        act.wait_ge(ys_out, 16 * c)
                    for q in range(4):
                        ps, fr = use((kind, c, q))
                        gs = Y_GROUPS[q]
                        me(act.activation(Ysb[:, gs[0]:gs[-1] + 1:2, :], ps[:, 0:len(gs) * (NS + NL)].rearrange(
                            "p (g n) -> p g n", n=NS + NL), ACT.Copy), fr)
                elif kind == "h_prep":
                    if c == 0:
                        act.wait_ge(ys_out, 16 * HEADS)
                        act.wait_ge(s5_out, 16 * HEADS)
                    act.wait_ge(fq_in[c % 2], 32 * (c // 2 + 1))
                    act.wait_ge(sg_in, 16 * (c + 1))
                    if c:
                        act.wait_ge(o_full, c)
                    fz = FZ[c % 2]
                    me(act.activation(K[:, :], fz[:, :], ACT.Sigmoid, scale=-1.0))
                    me.sync()
                    me(act.activation(fz[:, :], fz[:, :], ACT.Sigmoid), sig_done)
                    me(act.activation(SG[:, :], SG[:, :], ACT.Sigmoid), sig_g)
                    act.wait_ge(lnarg, c + 1)
                    me(act.activation(tA[:, 0:TP], tA[:, 0:TP], ACT.Ln))
                    me(act.activation(tB[:, 0:TP], tB[:, 0:TP], ACT.Ln), ln_done)
                elif kind == "level_prep":
                    l = step[2]
                    act.wait_ge(ex_arg, 8 * c + l)
                    e = EL[(l - 1) % 3]
                    me(act.activation(e[:, 0:TP], e[:, 0:TP], ACT.Exp), ex_done)
                elif kind == "state":
                    act.wait_ge(ex_arg, 8 * c + 8)
                    e = EL[7 % 3]
                    me(act.activation(e[:, 0:TP], e[:, 0:TP], ACT.Exp), ex_done)
                    act.wait_ge(b_ready, c + 1)
                    me(act.activation(Qs[:, :], B[:, 0:TP], ACT.Exp))
                    me(act.activation(A8[:, :], B[:, CH - 1:TP:CH], ACT.Exp), ex_a8)
                    for b in range(2):
                        ps, fr = use((kind, c, f"t{b}"))
                        me(act.activation(KT[:, 4 * b:4 * b + 4, :], ps.rearrange("p (c n) -> p c n", c=4), ACT.Copy), fr)
                elif kind == "h_out":
                    if c:
                        act.wait_ge(o_out, 16 * c)
                    for b in range(2):
                        ps, fr = use((kind, c, f"o{b}"))
                        me(act.activation(O[:, 512 * b:512 * b + 512], ps, ACT.Copy), fr)
                    ps, fr = use((kind, c, "os"))
                    me(act.activation(O[:, TP:T], ps[:, 0:NS], ACT.Copy), fr)
                    me.sync()
                    me(act.activation(EL[2][:, :], O[:, :], ACT.Square), sq_ready)
                    for b in range(NB):
                        ps, fr = use((kind, c, f"m{b}"))
                        me(act.activation(tB[:, CW * b:CW * b + CW], ps[:, 0:CW], ACT.Ln, bias=eps_rms[:, :]), fr)
                    me.sync()
                    me(act.activation(tB[:, :], tB[:, :], ACT.Exp, scale=-0.5), rms_e)
                elif kind == "gelu":
                    act.wait_ge(y_in, 16 * GC * (c + 1))
                    if c:
                        act.wait_ge(g_lo, c)
                    else:
                        act.wait_ge(mm_done, GLU_N)
                        act.wait_ge(st_out[2], 16 * 5)
                        act.wait_ge(st_out[1], 16 * 5)
                    src = st[0][:, :].rearrange("p (t n) -> p n t", t=L)
                    me(act.activation(st[1][:, 0:TP].rearrange("p (n t) -> p n t", t=L), src[:, NS:NS + NL, :], ACT.Gelu))
                    me(act.activation(st[1][:, TP:T], src[:, 0:NS, 0], ACT.Gelu), g_ready)
                    me.sync()
                    me(act.activation(XH[:, c, :], st[1][:, 0:T], ACT.Copy), g_hi)
                elif kind == "mix":
                    act.wait_ge(oa_in, 16 * (c + 1))
                    act.wait_ge(mm_done, OUT_N)
                    me(act.activation(XH[:, c, :], st[0][:, 0:T], ACT.Copy), m_hi)

            def layer_norm(w):
                for m in range(KD):
                    act.wait_ge(xc_ready, KD * w + m + 1)
                    if KD * w + m >= 2:
                        act.wait_ge(sq_mm, KD * w + m - 1)
                    me(act.activation(sq[m % 2][:, :], R[:, m, :], ACT.Square), sq_done)
                act.wait_ge(sq_mm, KD * (w + 1))
                me(act.activation(b3(rstd[:, :]), banks(0), ACT.Ln, bias=eps_ln[:, :]))
                me.sync()
                me(act.activation(rstd[:, :], rstd[:, :], ACT.Exp, scale=-0.5), var_e)

            layer_norm(0)
            for m in range(KD):
                act.wait_ge(t_ready, m + 1)
                if m == 0:
                    act.wait_ge(mm_done, FFN_N)
                me(act.activation(R[:, m, :], R[:, m, :], ACT.Identity, scale=ln_sb[:, 0, m:m + 1], bias=ln_sb[:, 1, m:m + 1]))
                me.sync()
                me(act.activation(XH[:, m, :], R[:, m, :], ACT.Copy), x1_hi)
                if m < 2:
                    split_hi(FFN_N + m, FFN_N // 2 + 1, m, KD * P)
            n0 = FFN_N
            nhi = None
            for q, (j0, nk) in enumerate(PARTS):
                def pair(i, first=False, last=False):
                    for s in range(2):
                        n = n0 + 2 * i + s
                        jj = 2 * (j0 + i) + s
                        act.wait_ge(mm_done, n + 1)
                        if not first:
                            act.wait_ge(conv_done, jj - 1)
                            act.wait_ge(cache_out[s], 16 * (j0 + i))
                            act.wait_ge(a_lo, j0 + i)
                        elif s == 0:
                            act.wait_ge(halo, 1)
                            act.wait_ge(x1_lo, KD)
                        act.wait_ge(cp_in[s], 16 * (j0 + i + 1))
                        act.activation(b3(ub[s][:, 2:2 + T]), banks(s), ACT.Copy).then_inc(u_full, 1)
                        act.activation(b3(hb[s][:, :]), banks(s), ACT.Identity, scale=cp[s][:, 2:3], bias=cp[s][:, 3:4]).then_inc(evac[s], 1)
                        if not last:
                            act.wait_ge(loaded[s], 16 * (n0 // 2 + i + 2))
                            act.activation(wh[s][:, :], raw[s][:, :], ACT.Copy).then_inc(hi_done, 1)
                        else:
                            act.wait_ge(loaded[s], 16 * (n0 // 2 + i + 2))
                            act.activation(wh[s][:, 0:nk * P], raw[s][:, 0:nk * P], ACT.Copy).then_inc(hi_done, 1)
                    act.wait_ge(conv_done, 2 * (j0 + i) + 2)
                    act.activation(hb[1][:, :], hb[1][:, :], ACT.Silu).then_inc(silu_done, 1)
                    act.wait_ge(a_ready, j0 + i + 1)
                    act.activation(AH[:, bass.ds(i, 1), :].rearrange("p a n -> p (a n)"), hb[0][:, :], ACT.Copy).then_inc(a_hi, 1)
                a = 0
                if j0 == 0:
                    pair(0, first=True)
                    a = 1
                with act.Fori(a, nk - 1) as i:
                    pair(i)
                pair(nk - 1, last=True)
                n0 += 2 * nk
                with act.Fori(0, KD // 2 - 1) as i:
                    for s in range(2):
                        act.wait_ge(loaded[s], 16 * (n0 // 2 + i + 2))
                        act.wait_ge(mm_done, n0 + 2 * i + s + 1)
                        act.activation(wh[s][:, 0:nk * P], raw[s][:, 0:nk * P], ACT.Copy).then_inc(hi_done, 1)
                n0 += KD
                if q + 1 < len(PARTS):
                    for s in range(2):
                        act.wait_ge(loaded[s], 16 * (n0 // 2 + 1))
                        act.wait_ge(mm_done, n0 + s - 1)
                        act.activation(wh[s][:, :], raw[s][:, :], ACT.Copy).then_inc(hi_done, 1)
            layer_norm(1)
            for m in range(KD):
                act.wait_ge(t_ready, KD + m + 1)
                me(act.activation(R[:, m, :], R[:, m, :], ACT.Identity, scale=ln_sb[:, 2, m:m + 1], bias=ln_sb[:, 3, m:m + 1]), x1_hi)

        @block.gpsimd
        def _(pool):
            me = Lane(pool, pool_own)
            pool.memset(ident[:, :], 0.0).then_inc(pool_own, 1)
            me.count[id(pool_own)] = 1
            pool.wait_ge(pool_own, 1)
            me(pool.affine_select(out=ident[:, :], in_=ident[:, :], compare_op=ALU.not_equal, fill=1.0, base=0,
                                  pattern=[[-1, P]], channel_multiplier=1))
            me(pool.memset(masks[:, :, :], 0.0))
            me.sync()
            me(pool.affine_select(out=masks[:, 0, :], in_=masks[:, 0, :], compare_op=ALU.not_equal, fill=1.0, base=0,
                                  pattern=[[-1, P]], channel_multiplier=1))
            for l, hh in enumerate(LEVELS):
                v = masks[:, l + 1, :].rearrange("p (b two x) -> p b two x", two=2, x=hh)[:, :, 1, :]
                me(pool.memset(v, 1.0))
                me.sync()
                me(pool.affine_select(out=v, in_=v, compare_op=ALU.is_ge, fill=0.0, base=0,
                                      pattern=[[-2 * hh, P // (2 * hh)], [0, hh]], channel_multiplier=1))
                me.sync()
                me(pool.affine_select(out=v, in_=v, compare_op=ALU.is_ge, fill=0.0, base=hh - 1,
                                      pattern=[[2 * hh, P // (2 * hh)], [0, hh]], channel_multiplier=-1))
            me(pool.memset(U[:, :, :], 0.0))
            me(pool.memset(TM[:, :, :], 0.0))
            me(pool.memset(H5[0][:, :, :], 0.0))
            me(pool.memset(H5[1][:, :, :], 0.0), consts)

            def split_lo(n, slot, width):
                pool.wait_ge(hi_done, n + 1)
                me(pool.tensor_tensor(wl[slot][:, 0:width], raw[slot][:, 0:width], wh[slot][:, 0:width].bitcast(F32), ALU.subtract), lo_done)

            def split(dst, src, hi):
                return pool.tensor_tensor(dst, src, hi.bitcast(F32), ALU.subtract)

            split_lo(0, 0, KD * P)
            split_lo(1, 1, KD * P)
            for step in ORDER:
                kind, c = step[0], step[1]
                if kind == "unit":
                    if GLU_N <= c < OUT_N:
                        m = c - GLU_N
                        pool.wait_ge(z_hi, m + 1)
                        me(split(XL[:, HEADS + m, :], st[2][:, 0:T], XH[:, HEADS + m, :]), z_lo)
                    if after_unit(c) is not None:
                        _, width = static_source(c + 2)
                        split_lo(c + 2, c % 2, width)
                elif kind == "h_prep" and c == 0:
                    pool.wait_ge(ys_out, 16 * HEADS)
                    pool.wait_ge(s5_out, 16 * HEADS)
                    me(pool.memset(sel[:, :, :], 0.0))
                    me(pool.memset(SC[:, :, :], 0.0))
                    me(pool.memset(S_all[:, 0, :], 0.0))
                    me.sync()
                    me(pool.affine_select(out=sel[:, :, :], in_=sel[:, :, :], compare_op=ALU.not_equal, fill=1.0, base=0,
                                          pattern=[[-1, NS], [0, P]], channel_multiplier=1), consts)
                elif kind == "gelu":
                    pool.wait_ge(g_hi, c + 1)
                    me(split(XL[:, c, :], st[1][:, 0:T], XH[:, c, :]), g_lo)
                elif kind == "mix":
                    pool.wait_ge(m_hi, c + 1)
                    me(split(XL[:, c, :], st[0][:, 0:T], XH[:, c, :]), m_lo)
            for m in range(KD):
                pool.wait_ge(*evacuated(OUT_N + m))
                if m == 1:
                    me(pool.tensor_tensor(racc[:, :], R[:, 0, :], R[:, 1, :], ALU.add))
                elif m > 1:
                    me.sync()
                    me(pool.tensor_tensor(racc[:, :], racc[:, :], R[:, m, :], ALU.add), racc_ready if m == KD - 1 else None)
            for m in range(KD):
                if m < 2:
                    pass
                pool.wait_ge(x1_hi, m + 1)
                me(split(XL[:, m, :], R[:, m, :], XH[:, m, :]), x1_lo)
                if m < 2:
                    split_lo(FFN_N + m, m, KD * P)
            n0 = FFN_N
            for q, (j0, nk) in enumerate(PARTS):
                def pair(i, width):
                    for s in range(2):
                        pool.wait_ge(hi_done, n0 + 2 * i + s + 3)
                        pool.tensor_tensor(wl[s][:, 0:width], raw[s][:, 0:width], wh[s][:, 0:width].bitcast(F32), ALU.subtract).then_inc(lo_done, 1)
                    pool.wait_ge(a_hi, j0 + i + 1)
                    a = bass.ds(i, 1)
                    pool.tensor_tensor(AL[:, a, :].rearrange("p a n -> p (a n)"), hb[0][:, :],
                                       AH[:, a, :].rearrange("p a n -> p (a n)").bitcast(F32), ALU.subtract).then_inc(a_lo, 1)
                with pool.Fori(0, nk - 1) as i:
                    pair(i, KD * P)
                pair(nk - 1, nk * P)
                n0 += 2 * nk
                with pool.Fori(0, KD // 2 - 1) as i:
                    for s in range(2):
                        pool.wait_ge(hi_done, n0 + 2 * i + s + 3)
                        pool.tensor_tensor(wl[s][:, 0:nk * P], raw[s][:, 0:nk * P], wh[s][:, 0:nk * P].bitcast(F32), ALU.subtract).then_inc(lo_done, 1)
                n0 += KD
                if q + 1 < len(PARTS):
                    for s in range(2):
                        pool.wait_ge(hi_done, n0 + s + 1)
                        pool.tensor_tensor(wl[s][:, :], raw[s][:, :], wh[s][:, :].bitcast(F32), ALU.subtract).then_inc(lo_done, 1)
            for s in range(2):
                pool.wait_ge(evac[s], n0 // 2)
            me(pool.tensor_tensor(racc[:, :], R[:, 0, :], R[:, 1, :], ALU.add))
            for m in range(2, KD):
                me.sync()
                me(pool.tensor_tensor(racc[:, :], racc[:, :], R[:, m, :], ALU.add), racc_ready if m == KD - 1 else None)

        @block.tensor
        def _(pe):
            def unit(n, slot, nk, xh, xl, ready=None):
                pe.wait_ge(lo_done, n + 1)
                if not isinstance(n, int) or n >= 2:
                    pe.wait_ge(evac[slot], (n0_half(n)))
                for k in range(nk):
                    if ready:
                        ready(k)
                    w_h, w_l = wh[slot][:, k * P:(k + 1) * P], wl[slot][:, k * P:(k + 1) * P]
                    for p_, (w, x) in enumerate(((w_h, xh), (w_h, xl), (w_l, xh))):
                        for b in range(NB):
                            last = nc.tensor.matmul(psum[:, 3 * slot + b, 0:CW], w, x[:, k, CW * b:CW * b + CW],
                                                    start=(k == 0 and p_ == 0), stop=(k == nk - 1 and p_ == 2))
                last.then_inc(mm_done, 1)

            half = {}

            def n0_half(n):
                return half["v"] if half.get("v") is not None else n // 2

            class Use:
                def __init__(self, name):
                    self.b, k = USES[name]
                    if k:
                        pe.wait_ge(free[self.b], k)
                    elif True:
                        pe.wait_ge(v_ev[self.b], 5 - self.b)
                    self.ps = psum[:, 6 + self.b, :]

                def done(self, ins):
                    ins.then_inc(fill[self.b], 1)

            pe.wait_ge(x_lo, 1)
            for step in ORDER:
                kind, c = step[0], step[1]
                if kind == "unit":
                    s = c % 2
                    if c < GLU_N:
                        unit(c, s, KD, XH, XL, (lambda k: pe.wait_ge(x_lo, k + 1)) if c == 0 else None)
                    elif c < OUT_N:
                        if c == GLU_N:
                            pe.wait_ge(g_lo, HEADS)
                        unit(c, s, HEADS, XH, XL)
                    else:
                        if c == OUT_N:
                            pe.wait_ge(z_lo, HEADS)
                            pe.wait_ge(m_lo, HEADS)
                        unit(c, s, KD, XH, XL)
                elif kind == "values":
                    pe.wait_ge(wv_lo, KD)
                    for t in range(NC + 1):
                        cols = slice(t * P, t * P + P) if t < NC else slice(TP, T)
                        rows = P if t < NC else NS
                        if t >= 2:
                            pe.wait_ge(v_ev[t % 2], t // 2)
                        for k in range(KD):
                            for p_, (x, w) in enumerate(((XH, WVH), (XH, WVL), (XL, WVH))):
                                last = nc.tensor.matmul(psum[0:rows, 6 + t % 2, :], x[:, k, cols], w[:, k, :],
                                                        start=(k == 0 and p_ == 0), stop=(k == KD - 1 and p_ == 2))
                        last.then_inc(v_mm[t % 2], 1)
                elif kind == "s5_in":
                    pe.wait_ge(wb_ready, c + 1)
                    for i, x in enumerate(("wre", "wim")):
                        u = Use((kind, c, x))
                        for r in range(PR):
                            last = nc.tensor.transpose(u.ps[:, r * P:(r + 1) * P], WB[i][:, r, :], ident[:, :])
                        u.done(last)
                    pe.wait_ge(ca_ready, c + 1)
                    for q in range(2):
                        u = Use((kind, c, f"k{q}"))
                        for r in range(PR):
                            lo = SS * q
                            o = u.ps[0:16, r * P:(r + 1) * P]
                            for i in range(2):
                                last = nc.tensor.matmul(o, bb[i][lo:lo + SS, r, :],
                                                        CA[i][lo:lo + SS, r, 0:L, :].rearrange("p t j -> p (t j)"),
                                                        start=(i == 0), stop=(i == 1))
                        u.done(last)
                    pe.wait_ge(*freed((kind, c, "wre")))
                    pe.wait_ge(*freed((kind, c, "wim")))
                    pe.wait_ge(u_in, 160 * (c + 1))
                    for q in range(2):
                        for i, x in enumerate(("dre", "dim")):
                            u = Use((kind, c, f"{x}{q}"))
                            for rr in range(2):
                                for gi in range(2):
                                    r = 2 * q + rr
                                    last = nc.tensor.matmul(u.ps[SS * gi:SS * gi + SS, rr * UC:(rr + 1) * UC],
                                                            BT[i][:, r, SS * gi:SS * gi + SS], U[:, 2 * r + gi, :],
                                                            start=True, stop=True)
                            u.done(last)
                elif kind == "s5_out":
                    pe.wait_ge(h5_ready, c + 1)
                    pe.wait_ge(t_in, 16 * L * (c + 1))
                    for q in range(4):
                        u = Use((kind, c, q))
                        for i, g in enumerate(Y_GROUPS[q]):
                            r, lo = g // 2, SS * (g % 2)
                            o = u.ps[:, i * (NS + NL):(i + 1) * (NS + NL)]
                            nc.tensor.matmul(o, TM[:, g, :], U[:, g, 0:NS + NL], start=True, stop=False)
                            for i in range(2):
                                last = nc.tensor.matmul(o, CA[i][lo:lo + SS, r, 1:L + 1, :].rearrange("p t j -> p (t j)"),
                                                        H5[i][lo:lo + SS, r, 0:NS + NL], start=False, stop=(i == 1))
                        u.done(last)
                elif kind == "level":
                    l = step[2]
                    if l == 0:
                        pe.wait_ge(b_ready, c + 1)
                    else:
                        pe.wait_ge(lv_ready, 7 * c + l)
                    for b in range(2):
                        u = Use((kind, c, l, b))
                        for i in range(4):
                            t = slice((4 * b + i) * CH, (4 * b + i + 1) * CH)
                            w, x = (K[:, t], Q[c % 2][:, t]) if l == 0 else (EL[(l - 1) % 3][:, t],) * 2
                            last = nc.tensor.matmul(u.ps[:, i * CH:(i + 1) * CH], w, x, start=True, stop=True)
                        u.done(last)
                elif kind == "state":
                    pe.wait_ge(qs_ready, c + 1)
                    e = EL[7 % 3]
                    for b in range(2):
                        u = Use((kind, c, f"t{b}"))
                        for i in range(4):
                            t = slice((4 * b + i) * CH, (4 * b + i + 1) * CH)
                            last = nc.tensor.transpose(u.ps[:, i * CH:(i + 1) * CH], e[:, t], ident[:, :])
                        u.done(last)
                    for b in range(2):
                        pe.wait_ge(*freed((kind, c, f"t{b}")))
                        u = Use((kind, c, f"kv{b}"))
                        for i in range(4):
                            last = nc.tensor.matmul(u.ps[:, i * P:(i + 1) * P], KT[:, 4 * b + i, :],
                                                    V[:, 4 * b + i, c * P:(c + 1) * P], start=True, stop=True)
                        u.done(last)
                    pe.wait_ge(consts, 2)
                    for b in range(2):
                        u = Use((kind, c, f"vb{b}"))
                        for i in range(4):
                            last = nc.tensor.matmul(u.ps[:, i * P:(i + 1) * P], sel[:, 4 * b + i, :],
                                                    Vs[:, c * P:(c + 1) * P], start=True, stop=True)
                        u.done(last)
                elif kind == "h_out":
                    for b in range(2):
                        pe.wait_ge(*freed(("level", c, len(LEVELS), b)))
                    for b in range(2):
                        pe.wait_ge(*freed(("state", c, f"kv{b}")))
                        u = Use((kind, c, f"o{b}"))
                        for i in range(4):
                            k = 4 * b + i
                            o = u.ps[:, i * CH:(i + 1) * CH]
                            nc.tensor.matmul(o, V[:, k, c * P:(c + 1) * P], SC[:, k, :], start=True, stop=False)
                            last = nc.tensor.matmul(o, S_all[:, k, :], Qs[:, k * CH:(k + 1) * CH], start=False, stop=True)
                        u.done(last)
                    pe.wait_ge(sn_ready, c + 1)
                    u = Use((kind, c, "os"))
                    for b in range(NS):
                        last = nc.tensor.matmul(u.ps[:, b:b + 1], S0[:, b, :], Q[c % 2][:, TP + b:TP + b + 1], start=True, stop=True)
                    u.done(last)
                    pe.wait_ge(sq_ready, c + 1)
                    for b in range(NB):
                        u = Use((kind, c, f"m{b}"))
                        u.done(nc.tensor.matmul(u.ps[:, 0:CW], ones_rms[:, :], EL[2][:, CW * b:CW * b + CW], start=True, stop=True))

            def layer_norm(w, n_units):
                pe.wait_ge(racc_ready, w + 1)
                for b in range(NB):
                    u = Use(("ln", w, "mean", b))
                    u.done(nc.tensor.matmul(u.ps[:, 0:CW], ones_ln[:, :], racc[:, CW * b:CW * b + CW], start=True, stop=True))
                for m in range(KD):
                    pe.wait_ge(sq_done, KD * w + m + 1)
                    for b in range(NB):
                        if m == 0 and b == 0:
                            pe.wait_ge(evac[0], n_units // 2)
                        last = nc.tensor.matmul(psum[:, b, 0:CW], ones_ln[:, :], sq[m % 2][:, CW * b:CW * b + CW],
                                                start=(m == 0), stop=(m == KD - 1))
                    last.then_inc(sq_mm, 1)

            layer_norm(0, FFN_N)
            n0 = FFN_N
            for q, (j0, nk) in enumerate(PARTS):
                def pair(i, first=False):
                    for s in range(2):
                        half["v"] = n0 // 2 + i
                        if first and s == 0:
                            pe.wait_ge(var_e, 1)
                        unit(n0 + 2 * i + s, s, KD, XH, XL, (lambda k: pe.wait_ge(x1_lo, k + 1)) if first and s == 0 else None)
                a = 0
                if q == 0:
                    pair(0, True)
                    a = 1
                with pe.Fori(a, nk) as i:
                    pair(i)
                n0 += 2 * nk

                def down(i, first=False):
                    for s in range(2):
                        half["v"] = n0 // 2 + i
                        unit(n0 + 2 * i + s, s, nk, AH, AL, (lambda k: pe.wait_ge(a_lo, j0 + k + 1)) if first and s == 0 else None)
                down(0, True)
                with pe.Fori(1, KD // 2) as i:
                    down(i)
                n0 += KD
            half["v"] = None
            layer_norm(1, n0)

        @block.vector
        def _(dve):
            me = Lane(dve, dve_own)
            TT, TS, STT = dve.tensor_tensor, dve.tensor_scalar, dve.scalar_tensor_tensor

            def use(name):
                b, k = USES[name]
                dve.wait_ge(fill[b], k + 1)
                return psum[:, 6 + b, :], (free[b], k + 1)

            me(dve.memset(ones_rms[:, :], 1.0 / P))
            me(dve.memset(ones_ln[:, :], 1.0 / D))
            me(dve.memset(one[:, :], 1.0))
            me(dve.memset(eps_rms[:, :], RMS_EPS))
            me(dve.memset(eps_ln[:, :], LN_EPS), dconsts)
            dve.wait_ge(small_in, 64)
            me(TT(lbt[:, 1, :], lbt[:, 0, :], lbt[:, 0, :], ALU.subtract), lbd)
            dve.wait_ge(lbe, 1)
            me(dve.reciprocal(lbt[:, 2, :], lbt[:, 1, :]))
            me.sync()
            me(TT(lbt[:, 2, :], lbt[:, 2, :], lbt[:, 1, :], ALU.mult))
            me.sync()
            me(TT(lb[:, :], lbt[:, 2, :], lbt[:, 2, :], ALU.subtract))
            me.sync()
            me(TS(oml[:, :], lb[:, :], -1.0, 1.0, ALU.mult, ALU.add))
            for k in range(KD):
                dve.wait_ge(x_hi, k + 1)
                me(TT(XL[:, k, :], st[k % 2][:, 0:T], XH[:, k, :].bitcast(F32), ALU.subtract), x_lo)

            def s5_prep(c):
                lre, lim = prm[:, 0:4], prm[:, 4:8]
                bre, bim, cre, cim = (prm[:, 12 + 64 * i:76 + 64 * i].rearrange("p (r j) -> p r j", j=16) for i in range(4))
                S = lambda i: sm[:, i, :]

                def do(ins, event=None):
                    me(ins, event)
                    me.sync()
                dve.wait_ge(p_dt, c + 1)
                dve.wait_ge(prm_in, 16 * (c + 1))
                do(TS(S(8), lre, -1e-4, None, ALU.min))
                do(TT(S(9), lim, S(0), ALU.mult))
                do(TT(S(1), S(8), S(0), ALU.mult), p_e)
                do(TS(S(10), S(9), INV_TWO_PI, ROUND, ALU.mult, ALU.add))
                do(TS(S(10), S(10), ROUND, None, ALU.subtract))
                do(STT(S(9), S(10), -TWO_PI_1, S(9), ALU.mult, ALU.add))
                do(STT(S(9), S(10), -TWO_PI_2, S(9), ALU.mult, ALU.add))
                do(STT(S(9), S(10), -TWO_PI_3, S(9), ALU.mult, ALU.add))
                do(TS(S(4), S(9), PI_SAFE, -PI_SAFE, ALU.min, ALU.max))
                do(TS(S(11), S(9), 1.5707963267948966, None, ALU.add))
                do(TS(S(12), S(11), 3.141592653589793, -6.283185307179586, ALU.is_gt, ALU.mult))
                do(TT(S(11), S(11), S(12), ALU.add))
                do(TS(S(5), S(11), PI_SAFE, -PI_SAFE, ALU.min, ALU.max), p_ang)
                dve.wait_ge(p_sin, c + 1)
                sin, cos, mag = S(6), S(7), S(2)
                if c:
                    dve.wait_ge(*filled(("s5_out", c - 1, 3)))
                PWv = PW[:, :, :, :]
                do(TT(PWv[:, 0, :, 1], mag, cos, ALU.mult))
                do(TT(PWv[:, 1, :, 1], mag, sin, ALU.mult))
                if c == 0:
                    do(dve.memset(PWv[:, 0, :, 0], 1.0))
                    do(dve.memset(PWv[:, 1, :, 0], 0.0))
                    do(dve.memset(E[:, 0, :, 0], 1.0))
                    do(dve.memset(E[:, 1, :, 0], 0.0))
                ar, ai = PWv[:, 0, :, 1], PWv[:, 1, :, 1]
                do(TS(S(13), ar, -1.0, None, ALU.add))
                do(TT(S(14), S(8), S(8), ALU.mult))
                do(TT(S(15), lim, lim, ALU.mult))
                do(TT(S(14), S(14), S(15), ALU.add))
                do(dve.reciprocal(S(14), S(14)))
                do(TT(S(15), S(13), S(8), ALU.mult))
                do(TT(S(16), ai, lim, ALU.mult))
                do(TT(S(15), S(15), S(16), ALU.add))
                do(TT(S(17), S(15), S(14), ALU.mult))
                do(TT(S(15), ai, S(8), ALU.mult))
                do(TT(S(16), S(13), lim, ALU.mult))
                do(TT(S(15), S(15), S(16), ALU.subtract))
                do(TT(S(18), S(15), S(14), ALU.mult))
                bc = lambda a: a.unsqueeze(2).to_broadcast([P, PR, 16])
                t0, t1 = ta5[:, 0:64].rearrange("p (r j) -> p r j", j=16), tb5[:, 0:64].rearrange("p (r j) -> p r j", j=16)
                for o, (x, y, op) in zip(bb, ((bre, bim, ALU.subtract), (bim, bre, ALU.add))):
                    me(TT(t0, x, bc(S(17)), ALU.mult))
                    do(TT(t1, y, bc(S(18)), ALU.mult))
                    do(TT(o[:, :, :], t0, t1, op))

                def powers(A, n, top):
                    m = 1
                    while m < top:
                        w = min(m, top - m)
                        src = A[:, :, :, 1:1 + w]
                        f = [A[:, i, :, m:m + 1].unsqueeze(1).to_broadcast([P, 2, PR, w]) for i in range(2)]
                        u_ = [x[:, 0:2 * PR * w].rearrange("p (i r n) -> p i r n", i=2, r=PR) for x in (ta5, tb5)]
                        me(TT(u_[0], src, f[0], ALU.mult))
                        do(TT(u_[1], src, f[1], ALU.mult))
                        me(TT(A[:, 0, :, m + 1:m + 1 + w], u_[0][:, 0], u_[1][:, 1], ALU.subtract))
                        do(TT(A[:, 1, :, m + 1:m + 1 + w], u_[0][:, 1], u_[1][:, 0], ALU.add))
                        m *= 2
                powers(PWv, 0, L)
                bt = lambda a: a.unsqueeze(3).to_broadcast([P, PR, L + 1, 16])
                bj = lambda a: a.unsqueeze(2).to_broadcast([P, PR, L + 1, 16])
                u0, u1 = (x[:, 0:PR * (L + 1) * 16].rearrange("p (r t j) -> p r t j", r=PR, t=L + 1) for x in (ta5, tb5))
                me(TT(u0, bj(cre), bt(PWv[:, 0]), ALU.mult))
                do(TT(u1, bj(cim), bt(PWv[:, 1]), ALU.mult))
                do(TT(CA[0][:, :, :, :], u0, u1, ALU.subtract))
                me(TT(u0, bj(cre), bt(PWv[:, 1]), ALU.mult))
                do(TT(u1, bj(cim), bt(PWv[:, 0]), ALU.mult))
                do(STT(CA[1][:, :, :, :].rearrange("p r t j -> p (r t j)"), ta5[:, 0:PR * (L + 1) * 16], -1.0,
                       tb5[:, 0:PR * (L + 1) * 16], ALU.mult, ALU.subtract), ca_ready)
                bt = lambda a: a.unsqueeze(3).to_broadcast([P, PR, L, 16])
                bj = lambda a: a.unsqueeze(2).to_broadcast([P, PR, L, 16])
                u0, u1 = (x[:, 0:PR * L * 16].rearrange("p (r t j) -> p r t j", r=PR, t=L) for x in (ta5, tb5))
                if c == 0:
                    dve.wait_ge(consts, 1)
                for i, op in ((0, ALU.subtract), (1, ALU.add)):
                    me(TT(u0, bj(bb[i][:, :, :]), bt(PWv[:, 0, :, 0:L]), ALU.mult))
                    do(TT(u1, bj(bb[1 - i][:, :, :]), bt(PWv[:, 1, :, 0:L]), ALU.mult))
                    do(TT(WB[i].rearrange("p r (t j) -> p r t j", j=16), u0, u1, op), wb_ready if i else None)
                S2 = [(S(19), S(20)), (S(21), S(22))]
                x, y = cos, sin
                for i in range(3):
                    ox, oy = (E[:, 0, :, 1], E[:, 1, :, 1]) if i == 2 else S2[i]
                    me(TT(S(23), x, x, ALU.mult))
                    me(TT(S(24), y, y, ALU.mult))
                    do(TT(S(25), x, y, ALU.mult))
                    me(TT(ox, S(23), S(24), ALU.subtract))
                    do(TS(oy, S(25), 2.0, None, ALU.mult))
                    x, y = ox, oy
                powers(E[:, :, :, :], 0, NL - 1)

            def s5_in(c):
                for q in range(2):
                    ps, fr = use(("s5_in", c, f"k{q}"))
                    if c:
                        dve.wait_ge(t_in, 16 * L * c)
                    me(dve.tensor_copy(KS[:, q:GC:2, :], ps[0:16, :].rearrange("p (g n) -> p g n", g=4)), fr)
                    me.sync()
                    v = KS[:, q:GC:2, 0:16]
                    tv = ta5[0:16, 0:64].rearrange("p (g n) -> p g n", g=4)
                    me(TT(tv, ident[0:16, 0:16].unsqueeze(1).to_broadcast([16, 4, 16]),
                          dk[:, GC * c + q:GC * c + GC:2].unsqueeze(2).to_broadcast([16, 4, 16]), ALU.mult))
                    me.sync()
                    me(TT(v, v, tv, ALU.add), k_ready)
                    me.sync()
                for q in range(2):
                    (pr, fr), (pi, fi) = use(("s5_in", c, f"dre{q}")), use(("s5_in", c, f"dim{q}"))
                    vr, vi = (x[:, 0:2 * UC].rearrange("p (r n) -> p r n", r=2) for x in (pr, pi))
                    cs, sn = E[:, 0, 2 * q:2 * q + 2, :], E[:, 1, 2 * q:2 * q + 2, :]
                    x0, x1 = (x[:, 0:2 * NL].rearrange("p (r n) -> p r n", r=2) for x in (ta5, tb5))
                    x2, x3 = (x[:, 512:512 + 2 * NL].rearrange("p (r n) -> p r n", r=2) for x in (ta5, tb5))
                    r2 = slice(2 * q, 2 * q + 2)
                    pr_, pi_ = vr[:, :, NS:NS + NL], vi[:, :, NS:NS + NL]
                    me(TT(x0, pr_, cs, ALU.mult))
                    me(TT(x1, pi_, sn, ALU.mult))
                    me(TT(x2, pi_, cs, ALU.mult))
                    me(TT(x3, pr_, sn, ALU.mult))
                    me(dve.tensor_copy(ds_[0][:, r2, :], vr[:, :, NS + NL:UC]), fr)
                    me(dve.tensor_copy(ds_[1][:, r2, :], vi[:, :, NS + NL:UC]), fi)
                    me.sync()
                    me(TT(G5[0][:, r2, :], x0, x1, ALU.add))
                    me(TT(G5[1][:, r2, :], x2, x3, ALU.subtract))
                    me.sync()
                for i in range(2):
                    for r in range(PR):
                        me(dve.tensor_tensor_scan((ta5, tb5)[i][:, r * NL:(r + 1) * NL], sm[:, 3, r:r + 1].to_broadcast([P, NL]),
                                                  G5[i][:, r, :], 0.0, ALU.mult, ALU.add))
                me.sync()
                gr, gi = (x[:, 0:PR * NL].rearrange("p (r n) -> p r n", r=PR) for x in (ta5, tb5))
                y2, y3 = (x[:, 512:1024].rearrange("p (r n) -> p r n", r=PR) for x in (ta5, tb5))
                cs, sn = E[:, 0, :, :], E[:, 1, :, :]
                me(TT(G5[0][:, :, :], gr, cs, ALU.mult))
                me(TT(G5[1][:, :, :], gi, sn, ALU.mult))
                me(TT(y2, gr, sn, ALU.mult))
                me(TT(y3, gi, cs, ALU.mult))
                me.sync()
                dve.wait_ge(*freed(("s5_in", c, "wim")))
                h0 = [prm[:, 268 + 32 * i:300 + 32 * i].rearrange("p (r b) -> p r b", b=NS) for i in range(2)]
                me(dve.tensor_copy(H5[0][:, :, 0:NS], h0[0]))
                me(dve.tensor_copy(H5[1][:, :, 0:NS], h0[1]))
                me(TT(H5[0][:, :, NS + 1:HC], G5[0][:, :, :], G5[1][:, :, :], ALU.subtract))
                me(TT(H5[1][:, :, NS + 1:HC], y2, y3, ALU.add), h5_ready)
                me.sync()
                if c:
                    dve.wait_ge(s5_out, 16 * c)
                for i in range(2):
                    me(dve.tensor_copy(s5o[:, i, :, NS:NS + 1], H5[i][:, :, HC - 1:HC]))
                t4 = [x[:, 32 * i:32 * i + 32].rearrange("p (r b) -> p r b", b=NS) for i, x in enumerate((ta5, ta5, ta5, ta5))]
                ar, ai = (PW[:, i, :, 1:2].to_broadcast([P, PR, NS]) for i in range(2))
                me(TT(t4[0], h0[0], ar, ALU.mult))
                me(TT(t4[1], h0[1], ai, ALU.mult))
                me(TT(t4[2], h0[0], ai, ALU.mult))
                me(TT(t4[3], h0[1], ar, ALU.mult))
                me.sync()
                me(TT(t4[0], t4[0], t4[1], ALU.subtract))
                me(TT(t4[2], t4[2], t4[3], ALU.add))
                me.sync()
                me(TT(s5o[:, 0, :, 0:NS], t4[0], ds_[0][:, :, :], ALU.add))
                me(TT(s5o[:, 1, :, 0:NS], t4[2], ds_[1][:, :, :], ALU.add), s5_full)
                me.sync()

            def h_prep(h):
                if h == 0:
                    dve.wait_ge(ys_out, 16 * HEADS)
                    dve.wait_ge(s5_out, 16 * HEADS)
                fz = FZ[h % 2]
                dve.wait_ge(sig_done, h + 1)
                me(TS(fz[:, :], fz[:, :], oml[:, h:h + 1], lb[:, h:h + 1], ALU.mult, ALU.add))
                me(TS(K[:, :], K[:, :], oml[:, h:h + 1], None, ALU.mult))
                me.sync()
                me(TS(tA[:, 0:TP], fz[:, 0:TP], 1.0 / TWO60, None, ALU.max))
                me(TS(tB[:, 0:TP], fz[:, 0:TP], TWO60, F_FLOOR * TWO60, ALU.mult, ALU.max))
                me(TS(fz[:, TP:T], fz[:, TP:T], F_FLOOR, None, ALU.max))
                me.sync()
                me(TS(tB[:, 0:TP], tB[:, 0:TP], 1.0, None, ALU.min), lnarg)
                dve.wait_ge(ln_done, h + 1)
                me(TT(tA[:, 0:TP], tA[:, 0:TP], tB[:, 0:TP], ALU.add))
                me.sync()
                for k in range(NC):
                    t = slice(k * CH, (k + 1) * CH)
                    me(dve.tensor_tensor_scan(B[:, t], one[:, 0:1].to_broadcast([P, CH]), tA[:, t], 0.0, ALU.mult, ALU.add),
                       b_ready if k == NC - 1 else None)
                me.sync()

            def halves(ap, hh):
                v = ap[:, 0:TP].rearrange("p (b two x) -> p b two x", two=2, x=hh)
                return v[:, :, 0, :], v[:, :, 1, :], v[:, :, 0, hh - 1:hh].to_broadcast([P, TP // (2 * hh), hh])

            def level_prep(h, l):
                hh = LEVELS[l - 1]
                e0, e1, _ = halves(EL[(l - 1) % 3], hh)
                b0, b1, mid = halves(B, hh)
                if l > 3:
                    dve.wait_ge(*filled(("level", h, l - 3, 1)))
                me(TT(e0, mid, b0, ALU.subtract))
                me(TT(e1, b1, mid, ALU.subtract), ex_arg)
                dve.wait_ge(ex_done, 8 * h + l)
                me(TT(e0, e0, halves(K, hh)[0], ALU.mult))
                me(TT(e1, e1, halves(Q[h % 2], hh)[1], ALU.mult), lv_ready)

            def level(h, l):
                for b in range(2):
                    ps, fr = use(("level", h, l, b))
                    me(dve.copy_predicated(SC[:, 4 * b:4 * b + 4, :], masks[:, l:l + 1, :].to_broadcast([P, 4, CH]),
                                           ps.rearrange("p (c n) -> p c n", c=4)), fr)
                me.sync()

            def state(h):
                e = EL[7 % 3]
                ev = e[:, 0:TP].rearrange("p (c n) -> p c n", c=NC)
                bv = B[:, 0:TP].rearrange("p (c n) -> p c n", c=NC)
                dve.wait_ge(*filled(("level", h, 5, 1)))
                me(TT(ev, bv[:, :, CH - 1:CH].to_broadcast([P, NC, CH]), bv, ALU.subtract), ex_arg)
                dve.wait_ge(ex_done, 8 * h + 8)
                me(TT(e[:, 0:TP], e[:, 0:TP], K[:, 0:TP], ALU.mult))
                dve.wait_ge(ex_a8, h + 1)
                me(TT(Qs[:, :], Qs[:, :], Q[h % 2][:, 0:TP], ALU.mult), qs_ready)
                fz = FZ[h % 2]
                dve.wait_ge(s0_in, 16 * (h + 1))
                me(TT(S0[:, :, :], S0[:, :, :], fz[:, TP:T].unsqueeze(2).to_broadcast([P, NS, P]), ALU.mult))
                for b in range(2):
                    ps, fr = use(("state", h, f"kv{b}"))
                    for i in range(4):
                        k = 4 * b + i
                        me.sync()
                        me(STT(S_all[:, k + 1, :], S_all[:, k, :], A8[:, k:k + 1], ps[:, i * P:(i + 1) * P], ALU.mult, ALU.add),
                           fr if i == 3 else None)
                tv = tA[:, 0:TP].rearrange("p (b n) -> p b n", b=NS)
                for b in range(2):
                    ps, fr = use(("state", h, f"vb{b}"))
                    me(TT(tv[:, 4 * b:4 * b + 4, :], ps.rearrange("p (b n) -> p b n", b=4),
                          K[:, TP + 4 * b:TP + 4 * b + 4].unsqueeze(2).to_broadcast([P, 4, P]), ALU.mult), fr)
                me.sync()
                me(TT(S0[:, :, :], S0[:, :, :], tv, ALU.add), sn_ready)

            def h_out(h):
                dve.wait_ge(rms_e, h + 1)
                me(TT(O[:, :], O[:, :], tB[:, :], ALU.mult))
                me.sync()
                dve.wait_ge(sig_g, h + 1)
                me(STT(O[:, :], O[:, :], ng[:, :], SG[:, :], ALU.mult, ALU.mult), o_full)

            for step in ORDER:
                kind, c = step[0], step[1]
                if kind == "values":
                    for k in range(KD):
                        dve.wait_ge(wv_hi, k + 1)
                        me(TT(WVL[:, k, :], G5[k % 2][:, :, :].rearrange("p r n -> p (r n)"), WVH[:, k, :].bitcast(F32), ALU.subtract), wv_lo)
                elif kind == "s5_prep":
                    s5_prep(c)
                elif kind == "s5_in":
                    s5_in(c)
                elif kind == "h_prep":
                    h_prep(c)
                elif kind == "level_prep":
                    level_prep(c, step[2])
                elif kind == "level":
                    if c == 0 and step[2] == 0:
                        dve.wait_ge(consts, 2)
                    level(c, step[2])
                elif kind == "state":
                    state(c)
                elif kind == "h_out":
                    h_out(c)
                elif kind == "unit" and GLU_N <= c < OUT_N:
                    m = c - GLU_N
                    dve.wait_ge(evac[c % 2], c // 2 + 1)
                    if m:
                        dve.wait_ge(z_lo, m)
                    me(TT(st[2][:, 0:T], XH[:, m, :].bitcast(F32), XL[:, m, :].bitcast(F32), ALU.add))
                    me.sync()
                    me(TT(st[2][:, 0:T], st[2][:, 0:T], st[1][:, 0:T], ALU.mult), z_ready)
                elif kind == "unit" and c >= OUT_N:
                    m = c - OUT_N
                    dve.wait_ge(mm_done, c + 1)
                    dve.wait_ge(xt_in[m % 2], 16 * (m // 2 + 1))
                    if m == 0:
                        dve.wait_ge(o_out, 16 * HEADS)
                        dve.wait_ge(st_saved, 32 * HEADS)
                        dve.wait_ge(m_lo, HEADS)
                    me(STT(b3(R[:, m, :]), b3(xt[m % 2][:, :]), ALPHA, banks(c % 2), ALU.mult, ALU.add), evacuated(c))

            def layer_norm(w):
                for b in range(NB):
                    ps, fr = use(("ln", w, "mean", b))
                    me(dve.tensor_copy(rstd[:, CW * b:CW * b + CW], ps[:, 0:CW]), fr)
                me.sync()
                for m in range(KD):
                    me(TT(R[:, m, :], R[:, m, :], rstd[:, :], ALU.subtract), xc_ready)
                dve.wait_ge(var_e, w + 1)
                for m in range(KD):
                    me(TT(R[:, m, :], R[:, m, :], rstd[:, :], ALU.mult), t_ready)

            layer_norm(0)
            dve.wait_ge(x1_lo, KD)
            me(dve.memset(ub[0][:, 0:2], 0.0))
            me(dve.memset(ub[1][:, 0:2], 0.0), halo)
            n0 = FFN_N
            tick = 0
            for q, (j0, nk) in enumerate(PARTS):
                def pair(i):
                    for s in range(2):
                        jj = 2 * (j0 + i) + s
                        dve.wait_ge(evac[s], (n0 // 2) + i + 1)
                        dve.wait_ge(u_full, jj + 1)
                        dve.wait_ge(cp_in[s], 16 * (j0 + i + 1))
                        h_, u_, w = hb[s], ub[s], cp[s]
                        STT(h_[:, 0:TP], u_[:, 1:1 + TP], w[:, 1:2], h_[:, 0:TP], ALU.mult, ALU.add)
                        STT(h_[:, TP:T], w[:, 12:20], w[:, 1:2], h_[:, TP:T], ALU.mult, ALU.add).then_inc(h0_ready, 1)
                        dve.wait_ge(h0_ready, jj + 1)
                        STT(h_[:, 0:TP], u_[:, 0:TP], w[:, 0:1], h_[:, 0:TP], ALU.mult, ALU.add)
                        STT(h_[:, TP:T], w[:, 4:12], w[:, 0:1], h_[:, TP:T], ALU.mult, ALU.add).then_inc(conv_done, 1)
                    dve.wait_ge(silu_done, j0 + i + 1)
                    TT(hb[0][:, :], hb[0][:, :], hb[1][:, :], ALU.mult).then_inc(a_ready, 1)
                with dve.Fori(0, nk) as i:
                    pair(i)
                n0 += 2 * nk

                def down(i):
                    for s in range(2):
                        m = bass.ds(2 * i + s, 1)
                        n = n0 + 2 * i + s
                        dve.wait_ge(mm_done, n + 1)
                        r = R[:, m, :].rearrange("p a n -> p (a n)")
                        if q == 0:
                            STT(b3(r), b3(r), ALPHA, banks(s), ALU.mult, ALU.add).then_inc(evac[s], 1)
                        else:
                            TT(b3(r), b3(r), banks(s), ALU.add).then_inc(evac[s], 1)
                with dve.Fori(0, KD // 2) as i:
                    down(i)
                n0 += KD
            dve.wait_ge(evac[0], n0 // 2)
            dve.wait_ge(evac[1], n0 // 2)
            layer_norm(1)


_OUTS = [((KD, P, T), "yT"), ((HEADS, P, P), "hp"), ((HEADS, P, 2, PR, NS + 1), "s5st"),
         ((2 * JT, P, 2 + NS), "cache_new"), ((NS, HEADS, P, P), "hs"), ((NS, 2 * FF), "cache_row0")]


def _layout(x_prompt, x_sample, state_hgrn, state_s5_re, state_s5_im, cache_ffn_conv, w_in, hgrn_lb_logits, hgrn_norm_g,
            s5_lambda_re, s5_lambda_im, s5_log_dt, s5_b_re, s5_b_im, s5_c_re, s5_c_im, s5_d, w_glu, w_out, ln1_g, ln1_b,
            w_ffn_up, ffn_conv_w, ffn_conv_b, w_ffn_down, ln2_g, ln2_b):
    import numpy as np

    def tiles(w, kt, nt):
        return w.reshape(kt, P, nt, P).transpose(2, 1, 0, 3).reshape(nt, P, kt * P)

    x = np.concatenate([x_prompt[0], x_sample[:, 0]], axis=0)
    win = tiles(w_in[0], KD, 20)
    order_in = [16 + c for c in range(4)] + [b + h for h in range(4) for b in (4, 0, 12)]
    up = [t + JT * s for t in range(JT) for s in range(2)]

    def per_group(a):
        a = a.reshape((HEADS, PR, 2, SS) + a.shape[2:])
        return np.moveaxis(a, 1, 3).reshape((HEADS, P, -1))

    ldt = np.broadcast_to(s5_log_dt[0][:, None], (G, SS))
    s5p = np.concatenate([per_group(a) for a in (
        s5_lambda_re[0], s5_lambda_im[0], ldt, s5_b_re[0], s5_b_im[0],
        s5_c_re[0].transpose(0, 2, 1), s5_c_im[0].transpose(0, 2, 1),
        state_s5_re[0].transpose(1, 2, 0), state_s5_im[0].transpose(1, 2, 0))], axis=2)
    cache = cache_ffn_conv[0]
    by_tile = lambda a: a.reshape(-1, 2 * JT, P).transpose(1, 2, 0)[up]
    convp = np.concatenate([by_tile(ffn_conv_w[0]), by_tile(ffn_conv_b), by_tile(cache[:, 0]), by_tile(cache[:, 1])], axis=2)
    d = dict(
        xT=x.T.reshape(KD, P, T), w_units=win[order_in], w_v=w_in[0][:, 1024:1536].reshape(KD, P, 512),
        w_glu=tiles(w_glu[0], HEADS, HEADS), w_out=tiles(w_out[0], KD, KD), w_up=tiles(w_ffn_up[0], KD, 2 * JT)[up],
        w_dn=tiles(w_ffn_down[0], JT, KD), s5p=s5p, dskip=s5_d[0].reshape(G, 16).T,
        lbl=hgrn_lb_logits[0].reshape(HEADS, P).T, normg=hgrn_norm_g.T,
        lnp=np.stack([a.reshape(KD, P).T for a in (ln1_g[0], ln1_b[0], ln2_g[0], ln2_b[0])], axis=1),
        convp=convp, s0=state_hgrn[0], cache_old=cache)
    return {k: np.ascontiguousarray(v) for k, v in d.items()}


def kernel(**inputs):
    import numpy as np
    import concourse.bacc as bacc
    from concourse.bass_utils import run_bass_kernel_spmd

    nc = bacc.Bacc("TRN2", target_bir_lowering=False, num_devices=1)
    arrays = _layout(**{k: np.asarray(v) for k, v in inputs.items()})
    args = [nc.dram_tensor(f"in_{k}", a.shape, F32, kind="ExternalInput").ap() for k, a in arrays.items()]
    args += [nc.dram_tensor(f"out_{k}", shape, F32, kind="ExternalOutput").ap() for shape, k in _OUTS]
    layer(nc, *args)
    r = run_bass_kernel_spmd(nc, [{f"in_{k}": a for k, a in arrays.items()}], core_ids=[0]).results[0]
    yT, hp, s5st, cn, hs, row0 = (r[f"out_{k}"] for _, k in _OUTS)
    y = yT.reshape(D, T).T
    s5 = s5st.reshape(HEADS, 2, SS, 2, PR, NS + 1).transpose(3, 5, 0, 4, 1, 2).reshape(2, NS + 1, G, SS)
    down = [2 * t + s for s in range(2) for t in range(JT)]
    rows = cn[down].reshape(2 * FF, 2 + NS).T
    return (np.ascontiguousarray(y[:TP])[None], np.ascontiguousarray(y[TP:])[:, None], hp[None, None],
            np.ascontiguousarray(s5[0, NS:])[None], np.ascontiguousarray(s5[1, NS:])[None],
            np.ascontiguousarray(rows[:2])[None, None], hs[None],
            np.ascontiguousarray(s5[0, :NS])[None], np.ascontiguousarray(s5[1, :NS])[None],
            np.stack([row0, rows[2:]], axis=1)[None])
```

```python
import concourse.bass as bass
from concourse import mybir
from contextlib import ExitStack

F32 = mybir.dt.float32
F32R = mybir.dt.float32r
ALU = mybir.AluOpType
ACT = mybir.ActivationFunctionType

P = 128
D = 1024
KD = D // P
TP = 1024
NS = 8
T = TP + NS
NB = 3
CW = T // NB
HEADS = 4
CH = 128
NC = TP // CH
FF = 2816
JT = FF // P
G = 32
GC = G // HEADS
PR = GC // 2
SS = 64
L = 8
NL = TP // L
UC = NS + NL + NS
HC = NS + 1 + NL
ALPHA = 2.0 ** 0.25
LN_EPS = 1e-5
RMS_EPS = 1e-6
F_FLOOR = 1e-20
TWO60 = 2.0 ** 60
PARTS = [(0, 8), (8, 7), (15, 7)]
TWO_PI_1 = 6.28125
TWO_PI_2 = 0.0019350051879882812
TWO_PI_3 = 3.019916050e-07
INV_TWO_PI = 0.15915494309189535
ROUND = 12582912.0
PI_SAFE = 3.1415925
U_N, F_N, GLU_N, OUT_N, FFN_N = 0, 4, 16, 20, 28
Y_GROUPS = [(0, 2, 4), (6,), (1, 3, 5), (7,)]
LEVELS = [1, 2, 4, 8, 16, 32, 64]


def unit_of(kind, h):
    return F_N + 3 * h + kind


DIRECT = (14, 15)


def rows_of(n):
    if n < GLU_N:
        return list(range(KD))
    if n < OUT_N:
        return list(range(HEADS))
    return list(range(HEADS, KD)) + list(range(HEADS))


def order():
    o, queue = [], []

    def unit(n, parts=None):
        last = len(rows_of(n)) - 1
        return [(1.32, [("part", n, i)] + ([("unit", n)] if i == last else []))
                for i in (range(last + 1) if parts is None else parts)]

    def put(us):
        while us > 0 and queue:
            if queue[0][1][-1] == ("unit", DIRECT[0]) and ("fin", 1) not in o:
                return
            t, steps = queue.pop(0)
            o.extend(steps)
            us -= t

    def before(*step):
        while queue and step not in o:
            put(0.1)

    queue += unit(0) + unit(1)
    put(100)
    o.append(("s5_param", 0))
    queue += unit(2) + unit(3) + [(5.2, [("values", t)]) for t in range(NC + 1)]
    for n in range(F_N, 14):
        queue += unit(n)
    queue += unit(14, range(4)) + unit(15, range(4)) + unit(14, range(4, KD)) + unit(15, range(4, KD))
    for c in range(HEADS):
        o.append(("s5_prep", c))
        put(8)
        o += [("s5_k", c), ("s5_w", c)]
        put(9)
        o.append(("s5_d", c))
        put(10)
        o.append(("s5_y", c))
    before("unit", unit_of(2, 0))
    o += [("hp_load", 0), ("hp_sig", 0), ("hp_a", 0)]
    put(10)
    o += [("hp_b", 0), ("sub", 0, 1)]
    last = len(LEVELS)
    for h in range(HEADS):
        for l in range(last + 1):
            if l + 2 <= last + 1:
                o.append(("sub", h, l + 2))
            if l + 1 <= last + 1:
                o.append(("mul", h, l + 1))
            o.append(("level", h, l))
            more = {0: [("s0_load", h)] + ([("ms", h - 1)] if h else []),
                    1: [("fin", h - 1)] if h else [],
                    2: [("vb", h)],
                    3: [("hp_load", h + 1)],
                    4: [("qs", h)],
                    5: [("hp_sig", h + 1), ("hp_a", h + 1)],
                    6: [("hp_b", h + 1)]}.get(l, [])
            if l == 3 and h + 1 < HEADS:
                before("unit", unit_of(2, h + 1) if h + 1 < HEADS - 1 else unit_of(0, h + 1))
            if h == 2 and l == 5:
                before("unit", DIRECT[1])
            o += [s for s in more if s[1] < HEADS]
            if h == 2:
                if l == 0:
                    o += [("y_load", 0), ("y_load", 1)]
                if l < HEADS:
                    o.append(("gelu", l))
                    if l + 2 < HEADS:
                        o.append(("y_load", l + 2))
                if l == HEADS:
                    for n in range(GLU_N, OUT_N):
                        queue += unit(n)
            if h == 3 and l == 4:
                put(100)
                o += [("mix", m) for m in range(HEADS - 1)]
                queue += unit(OUT_N, range(KD - 1)) + unit(OUT_N + 1, range(KD - 1))
            put(2.5 if h < 2 else 1.3)
        o.append(("kt", h))
        put(1.3)
        if h + 1 < HEADS:
            o.append(("sub", h + 1, 1))
        o.append(("kv", h))
        put(3.9 if h < 2 else 2.6)
        o += [("o", h), ("save", h)]
        if h == 1:
            before("part", DIRECT[1], HEADS - 1)
    put(3.9)
    o.append(("ms", HEADS - 1))
    put(3.9)
    o.append(("fin", HEADS - 1))
    o.append(("mix", HEADS - 1))
    put(100)
    queue += unit(OUT_N, [KD - 1]) + unit(OUT_N + 1, [KD - 1])
    for n in range(OUT_N + 2, FFN_N):
        queue += unit(n)
    put(1000)
    return o


ORDER = order()


def bank_uses():
    names = []
    parts = {"values": ("",), "s5_k": (0, 1), "s5_w": (0, 1), "s5_d": ("re0", "im0", "re1", "im1"), "s5_y": range(4),
             "kt": (0, 1), "kv": (0, 1), "vb": (0, 1), "o": (0, 1, "s"), "ms": range(NB)}
    for s in ORDER:
        if s[0] == "level":
            names += [s + (b,) for b in range(2)]
        elif s[0] in parts:
            names += [s + (x,) for x in parts[s[0]]]
    names += [("ln", w, i) for w in range(2) for i in range(NB)]
    return {name: (i % 2, i // 2) for i, name in enumerate(names)}


USES = bank_uses()


class Lane:

    def __init__(self, eng, own):
        self.eng, self.own, self.count, self.last = eng, own, {}, None

    def __call__(self, ins, event=None, by=1):
        if isinstance(event, tuple):
            ins.then_inc(event[0], by)
            self.last = event
            return event
        sem = self.own if event is None else event
        ins.then_inc(sem, by)
        key = id(sem)
        self.count[key] = self.count.get(key, 0) + by
        self.last = (sem, self.count[key])
        return self.last

    def sync(self, token=None):
        token = token or self.last
        if token:
            self.eng.wait_ge(*token)


def layer(nc, xT, w_units, w_v, w_glu, w_out, w_up, w_dn, s5q, s5p, dskip, lbl, normg, lnp, convp, s0, cache_old,
          yT, hp, s5st, cache_new, hs, cache_row0):
    ctx = ExitStack()
    with ctx:
        def sb(name, shape, dt=F32, c=ctx):
            return c.enter_context(nc.sbuf_tensor(name, shape, dt))

        def sem(name):
            return ctx.enter_context(nc.semaphore(name))

        XH, XL = sb("XH", [P, KD, T], F32R), sb("XL", [P, KD, T], F32R)
        raw = [sb(f"raw{i}", [P, KD * P]) for i in range(2)]
        wh = [sb(f"wh{i}", [P, KD * P], F32R) for i in range(2)]
        wl = [sb(f"wl{i}", [P, KD * P], F32R) for i in range(2)]
        ident = sb("ident", [P, P])
        ones_rms = sb("ones_rms", [P, P])
        ones_ln = sb("ones_ln", [P, P])
        one = sb("one", [P, 1])
        eps_rms, eps_ln = sb("eps_rms", [P, 1]), sb("eps_ln", [P, 1])
        lb, oml, lbt = sb("lb", [P, HEADS]), sb("oml", [P, HEADS]), sb("lbt", [P, 3, HEADS])
        ng, ln_sb = sb("ng", [P, 1]), sb("ln_sb", [P, 4, KD])
        psum = ctx.enter_context(nc.psum_tensor("psum", [P, 8, 512], F32))

        ph1 = ExitStack()
        masks = sb("masks", [P, len(LEVELS) + 1, P], mybir.dt.int8, ph1)
        V, Vs = sb("V", [P, NC, 512], F32, ph1), sb("Vs", [NS, 512], F32, ph1)
        st = [sb(f"st{i}", [P, GC * (NS + NL)], F32, ph1) for i in range(3)]
        pa = ExitStack()
        WVH, WVL = sb("WVH", [P, KD, 512], F32R, pa), sb("WVL", [P, KD, 512], F32R, pa)
        U = sb("U", [P, GC, UC], F32, pa)
        TM = sb("TM", [P, GC, P], F32, pa)
        BT = [sb(f"BT{i}", [P, PR, P], F32, pa) for i in range(2)]
        prm = [sb(f"prm{i}", [P, 320], F32, pa) for i in range(2)]
        lam = sb("lam", [P, 3, G // 2], F32, pa)
        CA = [sb(f"CA{i}", [P, PR, L + 1, 16], F32, pa) for i in range(2)]
        E = sb("E", [P, 2, PR, NL], F32, pa)
        PW = sb("PW", [P, 2, G // 2, L + 1], F32, pa)
        G5 = [sb(f"G5{i}", [P, PR, NL], F32, pa) for i in range(2)]
        H5 = [sb(f"H5{i}", [P, PR, HC], F32, pa) for i in range(2)]
        ds_ = [sb(f"ds{i}", [P, PR, NS], F32, pa) for i in range(2)]
        KS = sb("KS", [16, GC, P], F32, pa)
        Ysb = sb("Ysb", [P, GC, NS + NL], F32, pa)
        dk = sb("dk", [16, G], F32, pa)
        sm = sb("sm", [P, 28, G // 2], F32, pa)
        bb = [sb(f"bb{i}", [P, PR, 16], F32, pa) for i in range(2)]
        s5o = sb("s5o", [P, 2, PR, NS + 1], F32, pa)
        ta5, tb5 = sb("ta5", [P, 1024], F32, pa), sb("tb5", [P, 1024], F32, pa)
        WB = [H5[i][:, :, NS + 1:NS + 1 + NL] for i in range(2)]
        pa.close()
        pb = ExitStack()
        FZ, Q = [sb(f"FZ{i}", [P, T], F32, pb) for i in range(2)], [sb(f"Q{i}", [P, T], F32, pb) for i in range(2)]
        SG, K = [sb(f"SG{i}", [P, T], F32, pb) for i in range(2)], [sb(f"K{i}", [P, T], F32, pb) for i in range(2)]
        B = FZ
        tA, tB = sb("tA", [P, T], F32, pb), sb("tB", [P, T], F32, pb)
        EL = [sb(f"EL{i}", [P, T], F32, pb) for i in range(3)]
        Qs = sb("Qs", [P, TP], F32, pb)
        SC = sb("SC", [P, NC, CH], F32, pb)
        KTQ = sb("KTQ", [P, T], F32, pb)
        KT = KTQ[:, 0:TP].rearrange("p (c n) -> p c n", c=NC)
        S_all = sb("S_all", [P, NC + 1, P], F32, pb)
        S0 = sb("S0", [P, NS, P], F32, pb)
        O = sb("O", [P, T], F32, pb)
        A8 = sb("A8", [P, NC], F32, pb)
        sel = sb("sel", [NS, NS, P], F32, pb)
        pb.close()
        ph1.close()
        R = sb("R", [P, KD, T])
        p2 = ExitStack()
        xt = [sb(f"xt{i}", [P, T], F32, p2) for i in range(2)]
        racc = sb("racc", [P, T], F32, p2)
        sq = [sb(f"sq{i}", [P, T], F32, p2) for i in range(2)]
        rstd = sb("rstd", [P, T], F32, p2)
        p2.close()
        AH, AL = sb("AH", [P, PARTS[0][1], T], F32R), sb("AL", [P, PARTS[0][1], T], F32R)
        ub = [sb(f"ub{i}", [P, 2 + T]) for i in range(2)]
        hb = [sb(f"hb{i}", [P, T]) for i in range(2)]
        cp = [sb(f"cp{i}", [P, 20]) for i in range(2)]

        uscr = nc.dram_tensor("uscr", [HEADS, P, T], F32).ap()
        fscr = nc.dram_tensor("fscr", [3 * HEADS, P, T], F32).ap()
        yscr = nc.dram_tensor("yscr", [HEADS, P, GC * (NS + NL)], F32).ap()
        oscr = nc.dram_tensor("oscr", [HEADS, P, T], F32).ap()

        def sems(names):
            return (sem(x) for x in names.split())

        def two(name):
            return [sem(f"{name}{i}") for i in range(2)]

        loaded = two("loaded")
        hi_done, lo_done = sems("hi_done lo_done")
        mm_done = sem("mm_done")
        evac = two("evac")
        fill, free = two("fill"), two("free")
        act_own, dve_own, pool_own = sems("act_own dve_own pool_own")
        small_in, consts, dconsts, lbd, lbe = sems("small_in consts dconsts lbd lbe")
        x_in = [sem(f"x_in{i}") for i in range(3)]
        x_hi, x_lo = sems("x_hi x_lo")
        wv_in = [sem(f"wv_in{i}") for i in range(4)]
        wv_hi, wv_lo, x_used = sems("wv_hi wv_lo x_used")
        st_out = [sem(f"st_out{i}") for i in range(3)]
        prm_in, (lam_in, u_in, t_in) = two("prm_in"), sems("lam_in u_in t_in")
        p_dt, p_e, p_ang, p_sin, wb_ready, ca_ready, k_ready = sems("p_dt p_e p_ang p_sin wb_ready ca_ready k_ready")
        h5_ready, ys_out, s5_full, s5_out = sems("h5_ready ys_out s5_full s5_out")
        fq_in, (s0_in, s0_free, hp_saved, hs_saved) = two("fq_in"), sems("s0_in s0_free hp_saved hs_saved")
        sig_done, lnarg, ln_done, b_ready = sems("sig_done lnarg ln_done b_ready")
        ex_arg, ex_done, ex_a8, lv_ready, qs_ready = sems("ex_arg ex_done ex_a8 lv_ready qs_ready")
        sn_ready, sq_ready, rms_e, o_full, o_out = sems("sn_ready sq_ready rms_e o_full o_out")
        y_in, (g_ready, g_hi, g_lo) = two("y_in"), sems("g_ready g_hi g_lo")
        z_ready, z_hi, z_lo, oa_in, m_hi, m_lo = sems("z_ready z_hi z_lo oa_in m_hi m_lo")
        xt_in, (racc_ready, xc_ready, sq_done, sq_mm) = two("xt_in"), sems("racc_ready xc_ready sq_done sq_mm")
        var_e, t_ready, x1_hi, x1_lo, y_out = sems("var_e t_ready x1_hi x1_lo y_out")
        cp_in, cache_out = two("cp_in"), two("cache_out")
        halo, u_full, h0_ready, conv_done, silu_done = sems("halo u_full h0_ready conv_done silu_done")
        a_ready, a_hi, a_lo, row0_out = sems("a_ready a_hi a_lo row0_out")
        block = ctx.enter_context(nc.Block())

        def banks(slot):
            return psum[:, 3 * slot:3 * slot + 3, 0:CW]

        wv_st = [G5[0][:, :, :].rearrange("p r n -> p (r n)"), G5[1][:, :, :].rearrange("p r n -> p (r n)"),
                 Ysb[:, 0:4, :].rearrange("p g n -> p (g n)")[:, 0:512], Ysb[:, 4:8, :].rearrange(
                     "p g n -> p (g n)")[:, 0:512]]

        def b3(ap):
            return ap.rearrange("p (b n) -> p b n", b=NB)

        def evacuated(n):
            return evac[n % 2], n // 2 + 1

        def filled(name):
            b, k = USES[name]
            return fill[b], k + 1

        def freed(name):
            b, k = USES[name]
            return free[b], k + 1

        def static_source(n):
            if n < GLU_N:
                return w_units[n], KD * P
            if n < OUT_N:
                return w_glu[n - GLU_N], HEADS * P
            return w_out[n - OUT_N], KD * P

        def stored(i, n):
            return st_out[i], 16 * len([m for m in range(min(n, DIRECT[0])) if m % 3 == i])

        def after_unit(n):
            return n + 2 if n + 2 < FFN_N else None

        @block.sync
        def _(sp):
            def load_weights(n, half, slot, src, width):
                if not isinstance(n, int) or n >= 2:
                    sp.wait_ge(lo_done, n - 1)
                sp.dma_start(raw[slot][:, 0:width], src).then_inc(loaded[slot], 16)

            def load_x(k):
                if k >= 3:
                    sp.wait_ge(x_lo, k - 2)
                sp.dma_start(st[k % 3][:, 0:T], xT[k]).then_inc(x_in[k % 3], 16)

            def load_wv(k):
                s = k % 4
                if k >= 4:
                    sp.wait_ge(wv_lo, k - 3)
                sp.dma_start(wv_st[s], w_v[k]).then_inc(wv_in[s], 16)

            def store_unit(n):
                sp.wait_ge(*evacuated(n))
                dst = uscr[n] if n < F_N else fscr[n - F_N]
                sp.dma_start(dst, st[n % 3][:, 0:T]).then_inc(st_out[n % 3], 16)

            def load_u(c):
                sp.wait_ge(st_out[c % 3], 16 * (c // 3 + 1))
                if c == 0:
                    sp.wait_ge(consts, 1)
                else:
                    sp.wait_ge(*filled(("s5_y", c - 1, 3)))
                v = uscr[c].rearrange("(g j) n -> j g n", j=16)
                for s in range(L):
                    sp.dma_start(U[16 * s:16 * s + 16, :, NS:NS + NL], v[:, :, NL * (7 - s):NL * (8 - s)]).then_inc(u_in, 16)
                sp.dma_start(U[16 * 7:16 * 8, :, 0:NS], v[:, :, TP:T]).then_inc(u_in, 16)
                sp.dma_start(U[0:16, :, NS + NL:UC], v[:, :, TP:T]).then_inc(u_in, 16)

            sp.dma_start(lam[:, :, :].rearrange("p f n -> p (f n)"), s5q).then_inc(lam_in, 16)
            load_x(0)
            load_weights(0, 0, 0, w_units[0], KD * P)
            load_x(1)
            load_x(2)
            for src, dst in ((lbl, lbt[:, 0, :]), (normg, ng[:, :]), (lnp, ln_sb[:, :, :]), (dskip, dk[:, :])):
                sp.dma_start(dst, src).then_inc(small_in, 16)
            for c in range(2):
                sp.dma_start(prm[c][:, :], s5p[c]).then_inc(prm_in[c], 16)
            for k in range(3, KD):
                load_x(k)
            load_weights(1, 0, 1, w_units[1], KD * P)
            for k in range(KD):
                load_wv(k)
            load_weights(2, 0, 0, w_units[2], KD * P)
            sp.dma_start(cache_row0, cache_old[:, 1, :]).then_inc(row0_out, 16)
            for step in ORDER:
                kind, c = step[0], step[1]
                if kind == "unit":
                    if c < DIRECT[0]:
                        store_unit(c)
                    if c + 3 < FFN_N:
                        src, width = static_source(c + 3)
                        load_weights(c + 3, 0, (c + 3) % 2, src, width)
                    if c >= OUT_N and c - OUT_N + 2 < KD:
                        m = c - OUT_N + 2
                        sp.wait_ge(*evacuated(c))
                        sp.dma_start(xt[m % 2][:, :], xT[m]).then_inc(xt_in[m % 2], 16)
                elif kind == "s5_prep" and 0 < c < HEADS - 1:
                    sp.wait_ge(s5_full, c)
                    sp.dma_start(prm[(c + 1) % 2][:, :], s5p[c + 1]).then_inc(prm_in[(c + 1) % 2], 16)
                elif kind == "s5_k":
                    load_u(c)
                elif kind == "s5_d":
                    sp.wait_ge(k_ready, 2 * (c + 1))
                    if c:
                        sp.wait_ge(*filled(("s5_y", c - 1, 3)))
                    for s in range(L):
                        sp.dma_start(TM[16 * (7 - s):16 * (8 - s), :, 16 * s:P], KS[:, :, 0:P - 16 * s]).then_inc(t_in, 16)
                elif kind == "s5_y":
                    sp.wait_ge(s5_full, c + 1)
                    sp.dma_start(s5st[c], s5o[:, :, :, :]).then_inc(s5_out, 16)
                    sp.wait_ge(*freed(("s5_y", c, 3)))
                    sp.wait_ge(*freed(("s5_y", c, 2)))
                    sp.dma_start(yscr[c], Ysb[:, :, :].rearrange("p g n -> p (g n)")).then_inc(ys_out, 16)
                elif kind == "hp_load":
                    if c == 0:
                        sp.wait_ge(ys_out, 16 * HEADS)
                        sp.wait_ge(s5_out, 16 * HEADS)
                    elif c >= 2:
                        sp.wait_ge(o_full, c - 1)
                    for i, dst in enumerate((FZ, Q, SG)):
                        n = unit_of(i, c)
                        if n not in DIRECT:
                            sp.wait_ge(*stored(n % 3, n + 1))
                            sp.dma_start(dst[c % 2][:, :], fscr[n - F_N]).then_inc(fq_in[c % 2], 16)
                elif kind == "s0_load":
                    if c:
                        sp.wait_ge(hs_saved, 16 * c)
                        sp.wait_ge(*filled(("o", c - 1, "s")))
                    sp.dma_start(S0[:, :, :], s0[:, c].rearrange("b d e -> d b e")).then_inc(s0_in, 16)
                elif kind == "save":
                    sp.wait_ge(sn_ready, c + 1)
                    sp.dma_start(hs[:, c].rearrange("b d e -> d b e"), S0[:, :, :]).then_inc(hs_saved, 16)
                    sp.wait_ge(*freed(("kv", c, 1)))
                    sp.dma_start(hp[c], S_all[:, NC, :]).then_inc(hp_saved, 16)
                elif kind == "fin" and c < HEADS - 1:
                    sp.wait_ge(o_full, c + 1)
                    sp.dma_start(oscr[c], O[:, :]).then_inc(o_out, 16)
                elif kind == "y_load":
                    if c < 2:
                        sp.wait_ge(*stored((0, 2)[c], DIRECT[0]))
                    else:
                        sp.wait_ge(g_ready, c - 1)
                    v = yscr[c].rearrange("(t j) (g n) -> j g t n", j=16, g=GC)
                    for g in range(GC):
                        sp.dma_start(st[2 * (c % 2)][16 * g:16 * g + 16, :].rearrange("p (t n) -> p t n", t=L),
                                     v[:, g]).then_inc(y_in[c % 2], 16)
                elif kind == "mix" and c < HEADS - 1:
                    sp.wait_ge(g_lo, HEADS)
                    sp.wait_ge(o_out, 16 * (c + 1))
                    if c >= 1:
                        sp.wait_ge(m_lo, c)
                    sp.dma_start(st[0][:, 0:T], oscr[c]).then_inc(oa_in, 16)
                elif kind == "mix":
                    sp.wait_ge(m_lo, HEADS)
                    sp.wait_ge(hp_saved, 16 * HEADS)
                    sp.wait_ge(hs_saved, 16 * HEADS)
                    for m in range(2):
                        sp.dma_start(xt[m][:, :], xT[m]).then_inc(xt_in[m], 16)
            def conv_params(j0, i, s, first):
                if not first:
                    sp.wait_ge(conv_done, 2 * (j0 + i) + s - 1)
                sp.dma_start(cp[s][:, :], convp[bass.ds(2 * (j0 + i) + s, 1)].rearrange("a p n -> p (a n)")).then_inc(cp_in[s], 16)

            def store_cache(j):
                for s in range(2):
                    sp.wait_ge(u_full, 2 * j + s + 1)
                    sp.dma_start(cache_new[bass.ds(2 * j + s, 1)].rearrange("a p n -> p (a n)"), ub[s][:, TP:2 + T]).then_inc(cache_out[s], 16)

            n0 = FFN_N
            for j0, nk in PARTS:
                def pair(i, first=False):
                    for s in range(2):
                        load_weights(n0 + 2 * i + s, 0, s, w_up[bass.ds(2 * (j0 + i) + s, 1)].rearrange("a p n -> p (a n)"), KD * P)
                        conv_params(j0, i, s, first)
                    if not first:
                        store_cache(j0 + i - 1)
                if j0 == 0:
                    pair(0, True)
                    with sp.Fori(1, nk) as i:
                        pair(i)
                else:
                    with sp.Fori(0, nk) as i:
                        pair(i)
                n0 += 2 * nk
                with sp.Fori(0, KD // 2) as i:
                    for s in range(2):
                        load_weights(n0 + 2 * i + s, 0, s,
                                     w_dn[bass.ds(2 * i + s, 1), :, j0 * P:(j0 + nk) * P].rearrange("a p n -> p (a n)"), nk * P)
                n0 += KD
            store_cache(JT - 1)
            for m in range(KD):
                sp.wait_ge(x1_hi, KD + m + 1)
                sp.dma_start(yT[m], R[:, m, :]).then_inc(y_out, 16)
            sp.wait_ge(y_out, 16 * KD)
            sp.wait_ge(row0_out, 16)
            sp.wait_ge(s5_out, 16 * HEADS)
            sp.wait_ge(hp_saved, 16 * HEADS)
            sp.wait_ge(hs_saved, 16 * HEADS)
            for s in range(2):
                sp.wait_ge(cache_out[s], 16 * JT)

        @block.scalar
        def _(act):
            me = Lane(act, act_own)

            def split_hi(n, count, slot, width):
                act.wait_ge(loaded[slot], 16 * count)
                if not isinstance(n, int) or n >= 2:
                    act.wait_ge(mm_done, n - 1)
                me(act.activation(wh[slot][:, 0:width], raw[slot][:, 0:width], ACT.Copy), hi_done)

            act.wait_ge(small_in, 64)
            act.wait_ge(lbd, 1)
            me(act.activation(lbt[:, 1, :], lbt[:, 1, :], ACT.Exp), lbe)
            for k in range(KD):
                act.wait_ge(x_in[k % 3], 16 * (k // 3 + 1))
                me(act.activation(XH[:, k, :], st[k % 3][:, 0:T], ACT.Copy), x_hi)
                if k == 0:
                    split_hi(0, 1, 0, KD * P)
            split_hi(1, 1, 1, KD * P)
            for k in range(KD):
                act.wait_ge(wv_in[k % 4], 16 * (k // 4 + 1))
                me(act.activation(WVH[:, k, :], wv_st[k % 4], ACT.Copy), wv_hi)


            def use(name):
                b, k = USES[name]
                act.wait_ge(fill[b], k + 1)
                return psum[:, 6 + b, :], (free[b], k + 1)

            for step in ORDER:
                kind, c = step[0], step[1]
                if kind == "unit":
                    s, h = c % 2, c // 2
                    act_unit = c < OUT_N
                    if act_unit:
                        act.wait_ge(mm_done, c + 1)
                    if c < GLU_N:
                        if c in DIRECT:
                            act.wait_ge(o_full, 2)
                            act.wait_ge(sig_done, 4)
                            dst = (Q, SG)[c - DIRECT[0]][1][:, :]
                        else:
                            if c >= 3:
                                act.wait_ge(st_out[c % 3], 16 * (c // 3))
                            else:
                                act.wait_ge(x_lo, KD)
                            dst = st[c % 3][:, 0:T]
                        if c < F_N:
                            for b in range(NB):
                                nn = min(CW, TP - b * CW) // L
                                me(act.activation(dst[:, 0:TP].rearrange("p (t n) -> p n t", t=L)[:, 43 * b:43 * b + nn, :],
                                                  psum[:, 3 * s + b, 0:nn * L].rearrange("p (n t) -> p n t", t=L), ACT.Copy))
                            me(act.activation(dst[:, TP:T], psum[:, 3 * s + 2, CW - NS:CW], ACT.Copy), evacuated(c))
                        else:
                            me(act.activation(b3(dst), banks(s), ACT.Copy), evacuated(c))
                    elif c < OUT_N:
                        m = c - GLU_N
                        if m:
                            act.wait_ge(z_lo, m)
                        else:
                            act.wait_ge(g_lo, HEADS)
                        me(act.activation(b3(st[1][:, 0:T]), banks(s), ACT.Sigmoid), evacuated(c))
                        act.wait_ge(z_ready, m + 1)
                        me(act.activation(XH[:, HEADS + m, :], st[2][:, 0:T], ACT.Copy), z_hi)
                    if after_unit(c) is not None:
                        _, width = static_source(c + 2)
                        split_hi(c + 2, h + 2, s, width)
                elif kind == "values":
                    ps, fr = use((kind, c, ""))
                    me(act.activation(V[:, c, :] if c < NC else Vs[:, :], ps[0:P if c < NC else NS, :], ACT.Copy), fr)
                elif kind == "s5_w":
                    for i in range(2):
                        ps, fr = use((kind, c, i))
                        me(act.activation(BT[i][:, :, :], ps.rearrange("p (r n) -> p r n", r=PR), ACT.Copy), fr)
                elif kind == "s5_y":
                    if c:
                        act.wait_ge(ys_out, 16 * c)
                    for q in range(4):
                        ps, fr = use((kind, c, q))
                        gs = Y_GROUPS[q]
                        me(act.activation(Ysb[:, gs[0]:gs[-1] + 1:2, :], ps[:, 0:len(gs) * (NS + NL)].rearrange(
                            "p (g n) -> p g n", n=NS + NL), ACT.Copy), fr)
                elif kind == "hp_sig":
                    act.wait_ge(fq_in[c % 2], (48, 48, 96, 64)[c])
                    if c == HEADS - 1:
                        act.wait_ge(*evacuated(DIRECT[1]))
                    fz = FZ[c % 2]
                    me(act.activation(K[c % 2][:, :], fz[:, :], ACT.Sigmoid, scale=-1.0))
                    me.sync()
                    me(act.activation(fz[:, :], fz[:, :], ACT.Sigmoid), sig_done)
                    me(act.activation(SG[c % 2][:, :], SG[c % 2][:, :], ACT.Sigmoid), sig_done)
                elif kind == "hp_a":
                    act.wait_ge(lnarg, c + 1)
                    me(act.activation(tA[:, 0:TP], tA[:, 0:TP], ACT.Ln))
                    me(act.activation(tB[:, 0:TP], tB[:, 0:TP], ACT.Ln), ln_done)
                elif kind == "sub":
                    l = step[2]
                    act.wait_ge(ex_arg, 8 * c + l)
                    e = EL[(l - 1) % 3]
                    me(act.activation(e[:, 0:TP], e[:, 0:TP], ACT.Exp), ex_done)
                elif kind == "qs":
                    act.wait_ge(b_ready, c + 1)
                    me(act.activation(Qs[:, :], B[c % 2][:, 0:TP], ACT.Exp))
                    me(act.activation(A8[:, :], B[c % 2][:, CH - 1:TP:CH], ACT.Exp), ex_a8)
                elif kind == "kt":
                    if c:
                        act.wait_ge(*filled(("ms", c - 1, 2)))
                    for b in range(2):
                        ps, fr = use((kind, c, b))
                        me(act.activation(KT[:, 4 * b:4 * b + 4, :], ps.rearrange("p (c n) -> p c n", c=4), ACT.Copy), fr)
                elif kind == "o":
                    if c:
                        act.wait_ge(o_out, 16 * c)
                    for b in range(2):
                        ps, fr = use((kind, c, b))
                        me(act.activation(O[:, 512 * b:512 * b + 512], ps, ACT.Copy), fr)
                    ps, fr = use((kind, c, "s"))
                    me(act.activation(O[:, TP:T], ps[:, 0:NS], ACT.Copy), fr)
                    me.sync()
                    me(act.activation(KTQ[:, :], O[:, :], ACT.Square), sq_ready)
                elif kind == "ms":
                    if c + 1 < HEADS:
                        act.wait_ge(b_ready, c + 2)
                    for b in range(NB):
                        ps, fr = use((kind, c, b))
                        me(act.activation(tB[:, CW * b:CW * b + CW], ps[:, 0:CW], ACT.Ln, bias=eps_rms[:, :]), fr)
                    me.sync()
                    me(act.activation(tB[:, :], tB[:, :], ACT.Exp, scale=-0.5), rms_e)
                elif kind == "gelu":
                    act.wait_ge(y_in[c % 2], 16 * GC * (c // 2 + 1))
                    if c:
                        act.wait_ge(g_lo, c)
                    else:
                        act.wait_ge(x_used, 1)
                        act.wait_ge(*stored(1, DIRECT[0]))
                    src = st[2 * (c % 2)][:, :].rearrange("p (t n) -> p n t", t=L)
                    me(act.activation(st[1][:, 0:TP].rearrange("p (n t) -> p n t", t=L), src[:, NS:NS + NL, :], ACT.Gelu))
                    me(act.activation(st[1][:, TP:T], src[:, 0:NS, 0], ACT.Gelu), g_ready)
                    me.sync()
                    me(act.activation(XH[:, c, :], st[1][:, 0:T], ACT.Copy), g_hi)
                elif kind == "mix":
                    if c < HEADS - 1:
                        act.wait_ge(oa_in, 16 * (c + 1))
                    else:
                        act.wait_ge(o_full, HEADS)
                    act.wait_ge(mm_done, OUT_N)
                    me(act.activation(XH[:, c, :], st[0][:, 0:T] if c < HEADS - 1 else O[:, :], ACT.Copy), m_hi)
                elif kind == "s5_param":
                    act.wait_ge(lam_in, 16)
                    me(act.activation(sm[:, 0, :], lam[:, 2, :], ACT.Exp), p_dt)
                    act.wait_ge(p_e, 1)
                    me(act.activation(sm[:, 2, :], sm[:, 1, :], ACT.Exp))
                    me(act.activation(sm[:, 3, :], sm[:, 1, :], ACT.Exp, scale=float(L)))
                    act.wait_ge(p_ang, 1)
                    me(act.activation(sm[:, 6:8, :], sm[:, 4:6, :], ACT.Sin), p_sin)

            def layer_norm(w):
                for m in range(KD):
                    act.wait_ge(xc_ready, KD * w + m + 1)
                    if KD * w + m >= 2:
                        act.wait_ge(sq_mm, KD * w + m - 1)
                    me(act.activation(sq[m % 2][:, :], R[:, m, :], ACT.Square), sq_done)
                act.wait_ge(sq_mm, KD * (w + 1))
                me(act.activation(b3(rstd[:, :]), banks(0), ACT.Ln, bias=eps_ln[:, :]))
                me.sync()
                me(act.activation(rstd[:, :], rstd[:, :], ACT.Exp, scale=-0.5), var_e)

            layer_norm(0)
            for m in range(KD):
                act.wait_ge(t_ready, m + 1)
                if m == 0:
                    act.wait_ge(mm_done, FFN_N)
                me(act.activation(R[:, m, :], R[:, m, :], ACT.Identity, scale=ln_sb[:, 0, m:m + 1], bias=ln_sb[:, 1, m:m + 1]))
                me.sync()
                me(act.activation(XH[:, m, :], R[:, m, :], ACT.Copy), x1_hi)
                if m < 2:
                    split_hi(FFN_N + m, FFN_N // 2 + 1, m, KD * P)
            n0 = FFN_N
            nhi = None
            for q, (j0, nk) in enumerate(PARTS):
                def pair(i, first=False, last=False):
                    for s in range(2):
                        n = n0 + 2 * i + s
                        jj = 2 * (j0 + i) + s
                        act.wait_ge(mm_done, n + 1)
                        if not first:
                            act.wait_ge(conv_done, jj - 1)
                            act.wait_ge(cache_out[s], 16 * (j0 + i))
                            act.wait_ge(a_lo, j0 + i)
                        elif s == 0:
                            act.wait_ge(halo, 1)
                            act.wait_ge(x1_lo, KD)
                        act.wait_ge(cp_in[s], 16 * (j0 + i + 1))
                        act.activation(b3(ub[s][:, 2:2 + T]), banks(s), ACT.Copy).then_inc(u_full, 1)
                        act.activation(b3(hb[s][:, :]), banks(s), ACT.Identity, scale=cp[s][:, 2:3], bias=cp[s][:, 3:4]).then_inc(evac[s], 1)
                        if not last:
                            act.wait_ge(loaded[s], 16 * (n0 // 2 + i + 2))
                            act.activation(wh[s][:, :], raw[s][:, :], ACT.Copy).then_inc(hi_done, 1)
                        else:
                            act.wait_ge(loaded[s], 16 * (n0 // 2 + i + 2))
                            act.activation(wh[s][:, 0:nk * P], raw[s][:, 0:nk * P], ACT.Copy).then_inc(hi_done, 1)
                    act.wait_ge(conv_done, 2 * (j0 + i) + 2)
                    act.activation(hb[1][:, :], hb[1][:, :], ACT.Silu).then_inc(silu_done, 1)
                    act.wait_ge(a_ready, j0 + i + 1)
                    act.activation(AH[:, bass.ds(i, 1), :].rearrange("p a n -> p (a n)"), hb[0][:, :], ACT.Copy).then_inc(a_hi, 1)
                a = 0
                if j0 == 0:
                    pair(0, first=True)
                    a = 1
                with act.Fori(a, nk - 1) as i:
                    pair(i)
                pair(nk - 1, last=True)
                n0 += 2 * nk
                with act.Fori(0, KD // 2 - 1) as i:
                    for s in range(2):
                        act.wait_ge(loaded[s], 16 * (n0 // 2 + i + 2))
                        act.wait_ge(mm_done, n0 + 2 * i + s + 1)
                        act.activation(wh[s][:, 0:nk * P], raw[s][:, 0:nk * P], ACT.Copy).then_inc(hi_done, 1)
                n0 += KD
                if q + 1 < len(PARTS):
                    for s in range(2):
                        act.wait_ge(loaded[s], 16 * (n0 // 2 + 1))
                        act.wait_ge(mm_done, n0 + s - 1)
                        act.activation(wh[s][:, :], raw[s][:, :], ACT.Copy).then_inc(hi_done, 1)
            layer_norm(1)
            for m in range(KD):
                act.wait_ge(t_ready, KD + m + 1)
                me(act.activation(R[:, m, :], R[:, m, :], ACT.Identity, scale=ln_sb[:, 2, m:m + 1], bias=ln_sb[:, 3, m:m + 1]), x1_hi)

        @block.gpsimd
        def _(pool):
            me = Lane(pool, pool_own)
            pool.memset(ident[:, :], 0.0).then_inc(pool_own, 1)
            me.count[id(pool_own)] = 1
            pool.wait_ge(pool_own, 1)
            me(pool.affine_select(out=ident[:, :], in_=ident[:, :], compare_op=ALU.not_equal, fill=1.0, base=0,
                                  pattern=[[-1, P]], channel_multiplier=1))
            me(pool.memset(U[:, :, :], 0.0))
            me(pool.memset(TM[:, :, :], 0.0))
            me(pool.memset(H5[0][:, :, :], 0.0))
            me(pool.memset(H5[1][:, :, :], 0.0), consts)

            def split_lo(n, slot, width):
                pool.wait_ge(hi_done, n + 1)
                me(pool.tensor_tensor(wl[slot][:, 0:width], raw[slot][:, 0:width], wh[slot][:, 0:width].bitcast(F32), ALU.subtract), lo_done)

            def split(dst, src, hi):
                return pool.tensor_tensor(dst, src, hi.bitcast(F32), ALU.subtract)

            split_lo(0, 0, KD * P)
            split_lo(1, 1, KD * P)
            for k in range(KD):
                pool.wait_ge(wv_hi, k + 1)
                me(split(WVL[:, k, :], wv_st[k % 4], WVH[:, k, :]), wv_lo)
            me(pool.memset(masks[:, :, :], 0.0))
            me.sync()
            me(pool.affine_select(out=masks[:, 0, :], in_=masks[:, 0, :], compare_op=ALU.not_equal, fill=1.0, base=0,
                                  pattern=[[-1, P]], channel_multiplier=1))
            for l, hh in enumerate(LEVELS):
                v = masks[:, l + 1, :].rearrange("p (b two x) -> p b two x", two=2, x=hh)[:, :, 1, :]
                me(pool.memset(v, 1.0))
                me.sync()
                me(pool.affine_select(out=v, in_=v, compare_op=ALU.is_ge, fill=0.0, base=0,
                                      pattern=[[-2 * hh, P // (2 * hh)], [0, hh]], channel_multiplier=1))
                me.sync()
                me(pool.affine_select(out=v, in_=v, compare_op=ALU.is_ge, fill=0.0, base=hh - 1,
                                      pattern=[[2 * hh, P // (2 * hh)], [0, hh]], channel_multiplier=-1))
            for step in ORDER:
                kind, c = step[0], step[1]
                if kind == "unit":
                    if GLU_N <= c < OUT_N:
                        m = c - GLU_N
                        pool.wait_ge(z_hi, m + 1)
                        me(split(XL[:, HEADS + m, :], st[2][:, 0:T], XH[:, HEADS + m, :]), z_lo)
                    if after_unit(c) is not None:
                        _, width = static_source(c + 2)
                        split_lo(c + 2, c % 2, width)
                elif kind == "hp_load" and c == 0:
                    pool.wait_ge(ys_out, 16 * HEADS)
                    pool.wait_ge(s5_out, 16 * HEADS)
                    me(pool.memset(sel[:, :, :], 0.0))
                    me(pool.memset(SC[:, :, :], 0.0))
                    me(pool.memset(S_all[:, 0, :], 0.0))
                    me.sync()
                    me(pool.affine_select(out=sel[:, :, :], in_=sel[:, :, :], compare_op=ALU.not_equal, fill=1.0, base=0,
                                          pattern=[[-1, NS], [0, P]], channel_multiplier=1), consts)
                elif kind == "vb":
                    pool.wait_ge(s0_in, 16 * (c + 1))
                    pool.wait_ge(b_ready, c + 1)
                    me(pool.tensor_tensor(S0[:, :, :], S0[:, :, :], FZ[c % 2][:, TP:T].unsqueeze(2).to_broadcast([P, NS, P]), ALU.mult))
                    pool.wait_ge(*freed((kind, c, 0)))
                    pool.wait_ge(*freed((kind, c, 1)))
                    me.sync()
                    me(pool.tensor_tensor(S0[:, :, :], S0[:, :, :], tA[:, 0:TP].rearrange("p (b n) -> p b n", b=NS), ALU.add), sn_ready)
                elif kind == "qs":
                    pool.wait_ge(ex_a8, c + 1)
                    me(pool.tensor_tensor(Qs[:, :], Qs[:, :], Q[c % 2][:, 0:TP], ALU.mult), qs_ready)
                elif kind == "gelu":
                    pool.wait_ge(g_hi, c + 1)
                    me(split(XL[:, c, :], st[1][:, 0:T], XH[:, c, :]), g_lo)
                elif kind == "mix":
                    pool.wait_ge(m_hi, c + 1)
                    me(split(XL[:, c, :], st[0][:, 0:T] if c < HEADS - 1 else O[:, :], XH[:, c, :]), m_lo)
            for m in range(KD):
                pool.wait_ge(*evacuated(OUT_N + m))
                if m == 1:
                    me(pool.tensor_tensor(racc[:, :], R[:, 0, :], R[:, 1, :], ALU.add))
                elif m > 1:
                    me.sync()
                    me(pool.tensor_tensor(racc[:, :], racc[:, :], R[:, m, :], ALU.add), racc_ready if m == KD - 1 else None)
            for m in range(KD):
                if m < 2:
                    pass
                pool.wait_ge(x1_hi, m + 1)
                me(split(XL[:, m, :], R[:, m, :], XH[:, m, :]), x1_lo)
                if m < 2:
                    split_lo(FFN_N + m, m, KD * P)
            n0 = FFN_N
            for q, (j0, nk) in enumerate(PARTS):
                def pair(i, width):
                    for s in range(2):
                        pool.wait_ge(hi_done, n0 + 2 * i + s + 3)
                        pool.tensor_tensor(wl[s][:, 0:width], raw[s][:, 0:width], wh[s][:, 0:width].bitcast(F32), ALU.subtract).then_inc(lo_done, 1)
                    pool.wait_ge(a_hi, j0 + i + 1)
                    a = bass.ds(i, 1)
                    pool.tensor_tensor(AL[:, a, :].rearrange("p a n -> p (a n)"), hb[0][:, :],
                                       AH[:, a, :].rearrange("p a n -> p (a n)").bitcast(F32), ALU.subtract).then_inc(a_lo, 1)
                with pool.Fori(0, nk - 1) as i:
                    pair(i, KD * P)
                pair(nk - 1, nk * P)
                n0 += 2 * nk
                with pool.Fori(0, KD // 2 - 1) as i:
                    for s in range(2):
                        pool.wait_ge(hi_done, n0 + 2 * i + s + 3)
                        pool.tensor_tensor(wl[s][:, 0:nk * P], raw[s][:, 0:nk * P], wh[s][:, 0:nk * P].bitcast(F32), ALU.subtract).then_inc(lo_done, 1)
                n0 += KD
                if q + 1 < len(PARTS):
                    for s in range(2):
                        pool.wait_ge(hi_done, n0 + s + 1)
                        pool.tensor_tensor(wl[s][:, :], raw[s][:, :], wh[s][:, :].bitcast(F32), ALU.subtract).then_inc(lo_done, 1)
            for s in range(2):
                pool.wait_ge(evac[s], n0 // 2)
            me(pool.tensor_tensor(racc[:, :], R[:, 0, :], R[:, 1, :], ALU.add))
            for m in range(2, KD):
                me.sync()
                me(pool.tensor_tensor(racc[:, :], racc[:, :], R[:, m, :], ALU.add), racc_ready if m == KD - 1 else None)

        @block.tensor
        def _(pe):
            def products(slot, k, xh, xl, first, last):
                w_h, w_l = wh[slot][:, k * P:(k + 1) * P], wl[slot][:, k * P:(k + 1) * P]
                for p_, (w, x) in enumerate(((w_h, xh), (w_h, xl), (w_l, xh))):
                    for b in range(NB):
                        ins = nc.tensor.matmul(psum[:, 3 * slot + b, 0:CW], w, x[:, k, CW * b:CW * b + CW],
                                               start=(first and p_ == 0), stop=(last and p_ == 2))
                return ins

            def unit(n, slot, nk, xh, xl, ready=None):
                pe.wait_ge(lo_done, n + 1)
                if not isinstance(n, int) or n >= 2:
                    pe.wait_ge(evac[slot], (n0_half(n)))
                for k in range(nk):
                    if ready:
                        ready(k)
                    last = products(slot, k, xh, xl, k == 0, k == nk - 1)
                last.then_inc(mm_done, 1)

            half = {}

            def n0_half(n):
                return half["v"] if half.get("v") is not None else n // 2

            class Use:
                def __init__(self, name):
                    self.b, k = USES[name]
                    if k:
                        pe.wait_ge(free[self.b], k)
                    self.ps = psum[:, 6 + self.b, :]

                def done(self, ins):
                    ins.then_inc(fill[self.b], 1)

            pe.wait_ge(x_lo, 1)
            for step in ORDER:
                kind, c = step[0], step[1]
                if kind == "part":
                    i, s, rows = step[2], c % 2, rows_of(c)
                    k = rows[i]
                    if i == 0:
                        pe.wait_ge(lo_done, c + 1)
                        if c >= 2:
                            pe.wait_ge(evac[s], c // 2)
                    if c == 0:
                        pe.wait_ge(x_lo, k + 1)
                    elif c == GLU_N:
                        pe.wait_ge(g_lo, HEADS)
                    elif c >= OUT_N and k >= HEADS:
                        pe.wait_ge(z_lo, HEADS)
                    elif c >= OUT_N:
                        pe.wait_ge(m_lo, k + 1)
                    last = products(s, k, XH, XL, i == 0, i == len(rows) - 1)
                    if i == len(rows) - 1:
                        last.then_inc(mm_done, 1)
                    elif (c, i) == (GLU_N - 1, HEADS - 1):
                        last.then_inc(x_used, 1)
                elif kind == "values":
                    cols = slice(c * P, c * P + P) if c < NC else slice(TP, T)
                    u = Use((kind, c, ""))
                    for k in range(KD):
                        pe.wait_ge(wv_lo, k + 1)
                        for p_, (x, w) in enumerate(((XH, WVH), (XH, WVL), (XL, WVH))):
                            last = nc.tensor.matmul(u.ps[0:P if c < NC else NS, :], x[:, k, cols], w[:, k, :],
                                                    start=(k == 0 and p_ == 0), stop=(k == KD - 1 and p_ == 2))
                    u.done(last)
                elif kind == "s5_k":
                    pe.wait_ge(ca_ready, c + 1)
                    for q in range(2):
                        u = Use((kind, c, q))
                        for r in range(PR):
                            lo = SS * q
                            o = u.ps[0:16, r * P:(r + 1) * P]
                            for i in range(2):
                                last = nc.tensor.matmul(o, bb[i][lo:lo + SS, r, :],
                                                        CA[i][lo:lo + SS, r, 0:L, :].rearrange("p t j -> p (t j)"),
                                                        start=(i == 0), stop=(i == 1))
                        u.done(last)
                elif kind == "s5_w":
                    pe.wait_ge(wb_ready, c + 1)
                    for i in range(2):
                        u = Use((kind, c, i))
                        for r in range(PR):
                            last = nc.tensor.transpose(u.ps[:, r * P:(r + 1) * P], WB[i][:, r, :], ident[:, :])
                        u.done(last)
                elif kind == "s5_d":
                    pe.wait_ge(*freed(("s5_w", c, 0)))
                    pe.wait_ge(*freed(("s5_w", c, 1)))
                    pe.wait_ge(u_in, 160 * (c + 1))
                    for q in range(2):
                        for i, x in enumerate(("re", "im")):
                            u = Use((kind, c, f"{x}{q}"))
                            for rr in range(2):
                                for gi in range(2):
                                    r = 2 * q + rr
                                    last = nc.tensor.matmul(u.ps[SS * gi:SS * gi + SS, rr * UC:(rr + 1) * UC],
                                                            BT[i][:, r, SS * gi:SS * gi + SS], U[:, 2 * r + gi, :],
                                                            start=True, stop=True)
                            u.done(last)
                elif kind == "s5_y":
                    pe.wait_ge(h5_ready, c + 1)
                    pe.wait_ge(t_in, 16 * L * (c + 1))
                    for q in range(4):
                        u = Use((kind, c, q))
                        for i, g in enumerate(Y_GROUPS[q]):
                            r, lo = g // 2, SS * (g % 2)
                            o = u.ps[:, i * (NS + NL):(i + 1) * (NS + NL)]
                            nc.tensor.matmul(o, TM[:, g, :], U[:, g, 0:NS + NL], start=True, stop=False)
                            for i in range(2):
                                last = nc.tensor.matmul(o, CA[i][lo:lo + SS, r, 1:L + 1, :].rearrange("p t j -> p (t j)"),
                                                        H5[i][lo:lo + SS, r, 0:NS + NL], start=False, stop=(i == 1))
                        u.done(last)
                elif kind == "level":
                    l = step[2]
                    if l == 0:
                        pe.wait_ge(b_ready, c + 1)
                    else:
                        pe.wait_ge(lv_ready, 8 * c + l)
                    for b in range(2):
                        u = Use((kind, c, l, b))
                        for i in range(4):
                            t = slice((4 * b + i) * CH, (4 * b + i + 1) * CH)
                            w, x = (K[c % 2][:, t], Q[c % 2][:, t]) if l == 0 else (EL[(l - 1) % 3][:, t],) * 2
                            last = nc.tensor.matmul(u.ps[:, i * CH:(i + 1) * CH], w, x, start=True, stop=True)
                        u.done(last)
                elif kind == "kt":
                    pe.wait_ge(lv_ready, 8 * c + 8)
                    e = EL[7 % 3]
                    for b in range(2):
                        u = Use((kind, c, b))
                        for i in range(4):
                            t = slice((4 * b + i) * CH, (4 * b + i + 1) * CH)
                            last = nc.tensor.transpose(u.ps[:, i * CH:(i + 1) * CH], e[:, t], ident[:, :])
                        u.done(last)
                elif kind == "kv":
                    for b in range(2):
                        pe.wait_ge(*freed(("kt", c, b)))
                        u = Use((kind, c, b))
                        for i in range(4):
                            last = nc.tensor.matmul(u.ps[:, i * P:(i + 1) * P], KT[:, 4 * b + i, :],
                                                    V[:, 4 * b + i, c * P:(c + 1) * P], start=True, stop=True)
                        u.done(last)
                elif kind == "vb":
                    pe.wait_ge(consts, 2)
                    for b in range(2):
                        u = Use((kind, c, b))
                        for i in range(4):
                            last = nc.tensor.matmul(u.ps[:, i * P:(i + 1) * P], sel[:, 4 * b + i, :],
                                                    Vs[:, c * P:(c + 1) * P], start=True, stop=True)
                        u.done(last)
                elif kind == "o":
                    for b in range(2):
                        pe.wait_ge(*freed(("level", c, len(LEVELS), b)))
                    pe.wait_ge(qs_ready, c + 1)
                    for b in range(2):
                        pe.wait_ge(*freed(("kv", c, b)))
                        u = Use((kind, c, b))
                        for i in range(4):
                            k = 4 * b + i
                            o = u.ps[:, i * CH:(i + 1) * CH]
                            nc.tensor.matmul(o, V[:, k, c * P:(c + 1) * P], SC[:, k, :], start=True, stop=False)
                            last = nc.tensor.matmul(o, S_all[:, k, :], Qs[:, k * CH:(k + 1) * CH], start=False, stop=True)
                        u.done(last)
                    pe.wait_ge(sn_ready, c + 1)
                    u = Use((kind, c, "s"))
                    for b in range(NS):
                        last = nc.tensor.matmul(u.ps[:, b:b + 1], S0[:, b, :], Q[c % 2][:, TP + b:TP + b + 1], start=True, stop=True)
                    u.done(last)
                elif kind == "ms":
                    pe.wait_ge(sq_ready, c + 1)
                    for b in range(NB):
                        u = Use((kind, c, b))
                        u.done(nc.tensor.matmul(u.ps[:, 0:CW], ones_rms[:, :], KTQ[:, CW * b:CW * b + CW], start=True, stop=True))

            def layer_norm(w, n_units):
                pe.wait_ge(racc_ready, w + 1)
                for b in range(NB):
                    u = Use(("ln", w, b))
                    u.done(nc.tensor.matmul(u.ps[:, 0:CW], ones_ln[:, :], racc[:, CW * b:CW * b + CW], start=True, stop=True))
                for m in range(KD):
                    pe.wait_ge(sq_done, KD * w + m + 1)
                    for b in range(NB):
                        if m == 0 and b == 0:
                            pe.wait_ge(evac[0], n_units // 2)
                        last = nc.tensor.matmul(psum[:, b, 0:CW], ones_ln[:, :], sq[m % 2][:, CW * b:CW * b + CW],
                                                start=(m == 0), stop=(m == KD - 1))
                    last.then_inc(sq_mm, 1)

            layer_norm(0, FFN_N)
            n0 = FFN_N
            for q, (j0, nk) in enumerate(PARTS):
                def pair(i, first=False):
                    for s in range(2):
                        half["v"] = n0 // 2 + i
                        if first and s == 0:
                            pe.wait_ge(var_e, 1)
                        unit(n0 + 2 * i + s, s, KD, XH, XL, (lambda k: pe.wait_ge(x1_lo, k + 1)) if first and s == 0 else None)
                a = 0
                if q == 0:
                    pair(0, True)
                    a = 1
                with pe.Fori(a, nk) as i:
                    pair(i)
                n0 += 2 * nk

                def down(i, first=False):
                    for s in range(2):
                        half["v"] = n0 // 2 + i
                        unit(n0 + 2 * i + s, s, nk, AH, AL, (lambda k: pe.wait_ge(a_lo, j0 + k + 1)) if first and s == 0 else None)
                down(0, True)
                with pe.Fori(1, KD // 2) as i:
                    down(i)
                n0 += KD
            half["v"] = None
            layer_norm(1, n0)

        @block.vector
        def _(dve):
            me = Lane(dve, dve_own)
            TT, TS, STT = dve.tensor_tensor, dve.tensor_scalar, dve.scalar_tensor_tensor

            def use(name):
                b, k = USES[name]
                dve.wait_ge(fill[b], k + 1)
                return psum[:, 6 + b, :], (free[b], k + 1)

            me(dve.memset(ones_rms[:, :], 1.0 / P))
            me(dve.memset(ones_ln[:, :], 1.0 / D))
            me(dve.memset(one[:, :], 1.0))
            me(dve.memset(eps_rms[:, :], RMS_EPS))
            me(dve.memset(eps_ln[:, :], LN_EPS), dconsts)
            dve.wait_ge(small_in, 64)
            me(TT(lbt[:, 1, :], lbt[:, 0, :], lbt[:, 0, :], ALU.subtract), lbd)
            dve.wait_ge(lbe, 1)
            me(dve.reciprocal(lbt[:, 2, :], lbt[:, 1, :]))
            me.sync()
            me(TT(lbt[:, 2, :], lbt[:, 2, :], lbt[:, 1, :], ALU.mult))
            me.sync()
            me(TT(lb[:, :], lbt[:, 2, :], lbt[:, 2, :], ALU.subtract))
            me.sync()
            me(TS(oml[:, :], lb[:, :], -1.0, 1.0, ALU.mult, ALU.add))
            def do(ins, event=None):
                me(ins, event)
                me.sync()

            def S(i):
                return sm[:, i, :]

            def powers(A, top):
                m, n = 1, A.shape[2]
                while m < top:
                    w = min(m, top - m)
                    src = A[:, :, :, 1:1 + w]
                    f = [A[:, i, :, m:m + 1].unsqueeze(1).to_broadcast([P, 2, n, w]) for i in range(2)]
                    u_ = [x[:, 0:2 * n * w].rearrange("p (i r n) -> p i r n", i=2, r=n) for x in (ta5, tb5)]
                    me(TT(u_[0], src, f[0], ALU.mult))
                    do(TT(u_[1], src, f[1], ALU.mult))
                    me(TT(A[:, 0, :, m + 1:m + 1 + w], u_[0][:, 0], u_[1][:, 1], ALU.subtract))
                    do(TT(A[:, 1, :, m + 1:m + 1 + w], u_[0][:, 1], u_[1][:, 0], ALU.add))
                    m *= 2

            def s5_angle():
                dve.wait_ge(p_dt, 1)
                dve.wait_ge(lam_in, 16)
                do(TS(S(8), lam[:, 0, :], -1e-4, None, ALU.min))
                me(TT(S(9), lam[:, 1, :], S(0), ALU.mult))
                do(TT(S(1), S(8), S(0), ALU.mult), p_e)
                do(TS(S(10), S(9), INV_TWO_PI, ROUND, ALU.mult, ALU.add))
                do(TS(S(10), S(10), ROUND, None, ALU.subtract))
                do(STT(S(9), S(10), -TWO_PI_1, S(9), ALU.mult, ALU.add))
                do(STT(S(9), S(10), -TWO_PI_2, S(9), ALU.mult, ALU.add))
                do(STT(S(9), S(10), -TWO_PI_3, S(9), ALU.mult, ALU.add))
                me(TS(S(4), S(9), PI_SAFE, -PI_SAFE, ALU.min, ALU.max))
                do(TS(S(11), S(9), 1.5707963267948966, None, ALU.add))
                do(TS(S(12), S(11), 3.141592653589793, -6.283185307179586, ALU.is_gt, ALU.mult))
                do(TT(S(11), S(11), S(12), ALU.add))
                do(TS(S(5), S(11), PI_SAFE, -PI_SAFE, ALU.min, ALU.max), p_ang)

            def s5_param():
                dve.wait_ge(p_sin, 1)
                lim, sin, cos, mag = lam[:, 1, :], S(6), S(7), S(2)
                me(TT(PW[:, 0, :, 1], mag, cos, ALU.mult))
                me(TT(PW[:, 1, :, 1], mag, sin, ALU.mult))
                me(dve.memset(PW[:, 0, :, 0], 1.0))
                me(dve.memset(PW[:, 1, :, 0], 0.0))
                me(dve.memset(E[:, 0, :, 0], 1.0))
                me(dve.memset(E[:, 1, :, 0], 0.0))
                me(TT(S(14), S(8), S(8), ALU.mult))
                do(TT(S(15), lim, lim, ALU.mult))
                ar, ai = PW[:, 0, :, 1], PW[:, 1, :, 1]
                me(TS(S(13), ar, -1.0, None, ALU.add))
                do(TT(S(14), S(14), S(15), ALU.add))
                me(dve.reciprocal(S(14), S(14)))
                me(TT(S(15), S(13), S(8), ALU.mult))
                me(TT(S(16), ai, lim, ALU.mult))
                me(TT(S(17), ai, S(8), ALU.mult))
                do(TT(S(18), S(13), lim, ALU.mult))
                me(TT(S(15), S(15), S(16), ALU.add))
                do(TT(S(17), S(17), S(18), ALU.subtract))
                me(TT(S(5), S(17), S(14), ALU.mult))
                do(TT(S(4), S(15), S(14), ALU.mult))
                x, y = cos, sin
                for i in range(3):
                    ox, oy = S(19 + 2 * i), S(20 + 2 * i)
                    me(TT(S(25), x, x, ALU.mult))
                    me(TT(S(26), y, y, ALU.mult))
                    do(TT(S(27), x, y, ALU.mult))
                    me(TT(ox, S(25), S(26), ALU.subtract))
                    do(TS(oy, S(27), 2.0, None, ALU.mult))
                    x, y = ox, oy
                powers(PW[:, :, :, :], L)

            for k in range(KD):
                dve.wait_ge(x_hi, k + 1)
                me(TT(XL[:, k, :], st[k % 3][:, 0:T], XH[:, k, :].bitcast(F32), ALU.subtract), x_lo)

            def s5_prep(c):
                p5, r4 = prm[c % 2], slice(PR * c, PR * c + PR)
                bre, bim, cre, cim = (p5[:, 64 * i:64 * i + 64].rearrange("p (r j) -> p r j", j=16) for i in range(4))
                PWv = PW[:, :, r4, :]
                dve.wait_ge(prm_in[c % 2], 16 * (c // 2 + 1))
                bc = lambda a: a[:, r4].unsqueeze(2).to_broadcast([P, PR, 16])
                t0, t1 = ([x[:, 64 * i:64 * i + 64].rearrange("p (r j) -> p r j", j=16) for i in range(2)] for x in (ta5, tb5))
                for i, (x, y) in enumerate(((bre, bim), (bim, bre))):
                    me(TT(t0[i], x, bc(S(4)), ALU.mult))
                    me(TT(t1[i], y, bc(S(5)), ALU.mult))
                me.sync()
                if c:
                    dve.wait_ge(*filled(("s5_y", c - 1, 3)))
                me(TT(bb[0][:, :, :], t0[0], t1[0], ALU.subtract))
                do(TT(bb[1][:, :, :], t0[1], t1[1], ALU.add))
                bt = lambda a: a.unsqueeze(3).to_broadcast([P, PR, L + 1, 16])
                bj = lambda a: a.unsqueeze(2).to_broadcast([P, PR, L + 1, 16])
                u0, u1 = (x[:, 0:PR * (L + 1) * 16].rearrange("p (r t j) -> p r t j", r=PR, t=L + 1) for x in (ta5, tb5))
                me(TT(u0, bj(cre), bt(PWv[:, 0]), ALU.mult))
                do(TT(u1, bj(cim), bt(PWv[:, 1]), ALU.mult))
                do(TT(CA[0][:, :, :, :], u0, u1, ALU.subtract))
                me(TT(u0, bj(cre), bt(PWv[:, 1]), ALU.mult))
                do(TT(u1, bj(cim), bt(PWv[:, 0]), ALU.mult))
                do(STT(CA[1][:, :, :, :].rearrange("p r t j -> p (r t j)"), ta5[:, 0:PR * (L + 1) * 16], -1.0,
                       tb5[:, 0:PR * (L + 1) * 16], ALU.mult, ALU.subtract), ca_ready)
                bt = lambda a: a.unsqueeze(3).to_broadcast([P, PR, L, 16])
                bj = lambda a: a.unsqueeze(2).to_broadcast([P, PR, L, 16])
                u0, u1 = (x[:, 0:PR * L * 16].rearrange("p (r t j) -> p r t j", r=PR, t=L) for x in (ta5, tb5))
                if c == 0:
                    dve.wait_ge(consts, 1)
                for i, op in ((0, ALU.subtract), (1, ALU.add)):
                    me(TT(u0, bj(bb[i][:, :, :]), bt(PWv[:, 0, :, 0:L]), ALU.mult))
                    do(TT(u1, bj(bb[1 - i][:, :, :]), bt(PWv[:, 1, :, 0:L]), ALU.mult))
                    do(TT(WB[i].rearrange("p r (t j) -> p r t j", j=16), u0, u1, op), wb_ready if i else None)

            def s5_k(c):
                for q in range(2):
                    ps, fr = use(("s5_k", c, q))
                    if c:
                        dve.wait_ge(t_in, 16 * L * c)
                    me(dve.tensor_copy(KS[:, q:GC:2, :], ps[0:16, :].rearrange("p (g n) -> p g n", g=4)), fr)
                    v = KS[:, q:GC:2, 0:16]
                    tv = ta5[0:16, 0:64].rearrange("p (g n) -> p g n", g=4)
                    do(TT(tv, ident[0:16, 0:16].unsqueeze(1).to_broadcast([16, 4, 16]),
                          dk[:, GC * c + q:GC * c + GC:2].unsqueeze(2).to_broadcast([16, 4, 16]), ALU.mult))
                    do(TT(v, v, tv, ALU.add), k_ready)
                r4 = slice(PR * c, PR * c + PR)
                me(dve.tensor_copy(E[:, 0, :, 1], S(23)[:, r4]))
                do(dve.tensor_copy(E[:, 1, :, 1], S(24)[:, r4]))
                powers(E[:, :, :, :], NL - 1)

            def s5_d(c):
                r4 = slice(PR * c, PR * c + PR)
                if c == 0:
                    dve.wait_ge(wv_lo, KD)
                for q in range(2):
                    (pr, fr), (pi, fi) = use(("s5_d", c, f"re{q}")), use(("s5_d", c, f"im{q}"))
                    vr, vi = (x[:, 0:2 * UC].rearrange("p (r n) -> p r n", r=2) for x in (pr, pi))
                    cs, sn = E[:, 0, 2 * q:2 * q + 2, :], E[:, 1, 2 * q:2 * q + 2, :]
                    x0, x1 = (x[:, 0:2 * NL].rearrange("p (r n) -> p r n", r=2) for x in (ta5, tb5))
                    x2, x3 = (x[:, 512:512 + 2 * NL].rearrange("p (r n) -> p r n", r=2) for x in (ta5, tb5))
                    r2 = slice(2 * q, 2 * q + 2)
                    pr_, pi_ = vr[:, :, NS:NS + NL], vi[:, :, NS:NS + NL]
                    me(TT(x0, pr_, cs, ALU.mult))
                    me(TT(x1, pi_, sn, ALU.mult))
                    me(TT(x2, pi_, cs, ALU.mult))
                    me(TT(x3, pr_, sn, ALU.mult))
                    me(dve.tensor_copy(ds_[0][:, r2, :], vr[:, :, NS + NL:UC]), fr)
                    me(dve.tensor_copy(ds_[1][:, r2, :], vi[:, :, NS + NL:UC]), fi)
                    me.sync()
                    me(TT(G5[0][:, r2, :], x0, x1, ALU.add))
                    me(TT(G5[1][:, r2, :], x2, x3, ALU.subtract))
                    me.sync()
                for i in range(2):
                    for r in range(PR):
                        me(dve.tensor_tensor_scan((ta5, tb5)[i][:, r * NL:(r + 1) * NL], sm[:, 3, PR * c + r:PR * c + r + 1].to_broadcast([P, NL]),
                                                  G5[i][:, r, :], 0.0, ALU.mult, ALU.add))
                me.sync()
                gr, gi = (x[:, 0:PR * NL].rearrange("p (r n) -> p r n", r=PR) for x in (ta5, tb5))
                y2, y3 = (x[:, 512:1024].rearrange("p (r n) -> p r n", r=PR) for x in (ta5, tb5))
                cs, sn = E[:, 0, :, :], E[:, 1, :, :]
                me(TT(G5[0][:, :, :], gr, cs, ALU.mult))
                me(TT(G5[1][:, :, :], gi, sn, ALU.mult))
                me(TT(y2, gr, sn, ALU.mult))
                me(TT(y3, gi, cs, ALU.mult))
                me.sync()
                dve.wait_ge(*freed(("s5_w", c, 1)))
                h0 = [prm[c % 2][:, 256 + 32 * i:288 + 32 * i].rearrange("p (r b) -> p r b", b=NS) for i in range(2)]
                me(dve.tensor_copy(H5[0][:, :, 0:NS], h0[0]))
                me(dve.tensor_copy(H5[1][:, :, 0:NS], h0[1]))
                me(TT(H5[0][:, :, NS + 1:HC], G5[0][:, :, :], G5[1][:, :, :], ALU.subtract))
                me(TT(H5[1][:, :, NS + 1:HC], y2, y3, ALU.add), h5_ready)
                me.sync()
                if c:
                    dve.wait_ge(s5_out, 16 * c)
                for i in range(2):
                    me(dve.tensor_copy(s5o[:, i, :, NS:NS + 1], H5[i][:, :, HC - 1:HC]))
                t4 = [x[:, 32 * i:32 * i + 32].rearrange("p (r b) -> p r b", b=NS) for i, x in enumerate((ta5, ta5, ta5, ta5))]
                ar, ai = (PW[:, i, r4, 1:2].to_broadcast([P, PR, NS]) for i in range(2))
                me(TT(t4[0], h0[0], ar, ALU.mult))
                me(TT(t4[1], h0[1], ai, ALU.mult))
                me(TT(t4[2], h0[0], ai, ALU.mult))
                me(TT(t4[3], h0[1], ar, ALU.mult))
                me.sync()
                me(TT(t4[0], t4[0], t4[1], ALU.subtract))
                me(TT(t4[2], t4[2], t4[3], ALU.add))
                me.sync()
                me(TT(s5o[:, 0, :, 0:NS], t4[0], ds_[0][:, :, :], ALU.add))
                me(TT(s5o[:, 1, :, 0:NS], t4[2], ds_[1][:, :, :], ALU.add), s5_full)
                me.sync()

            def hp_a(h):
                fz = FZ[h % 2]
                dve.wait_ge(sig_done, 2 * h + 1)
                if h:
                    dve.wait_ge(sn_ready, h)
                me(TS(fz[:, :], fz[:, :], oml[:, h:h + 1], lb[:, h:h + 1], ALU.mult, ALU.add))
                me(TS(K[h % 2][:, :], K[h % 2][:, :], oml[:, h:h + 1], None, ALU.mult))
                me.sync()
                me(TS(tB[:, 0:TP], fz[:, 0:TP], TWO60, F_FLOOR * TWO60, ALU.mult, ALU.max))
                me(TS(tA[:, 0:TP], fz[:, 0:TP], 1.0 / TWO60, None, ALU.max))
                me(TS(fz[:, TP:T], fz[:, TP:T], F_FLOOR, None, ALU.max))
                me.sync()
                me(TS(tB[:, 0:TP], tB[:, 0:TP], 1.0, None, ALU.min), lnarg)

            def hp_b(h):
                dve.wait_ge(ln_done, h + 1)
                me(TT(tA[:, 0:TP], tA[:, 0:TP], tB[:, 0:TP], ALU.add))
                me.sync()
                for k in range(NC):
                    t = slice(k * CH, (k + 1) * CH)
                    me(dve.tensor_tensor_scan(B[h % 2][:, t], one[:, 0:1].to_broadcast([P, CH]), tA[:, t], 0.0, ALU.mult, ALU.add),
                       b_ready if k == NC - 1 else None)
                me.sync()

            def halves(ap, hh):
                v = ap[:, 0:TP].rearrange("p (b two x) -> p b two x", two=2, x=hh)
                return v[:, :, 0, :], v[:, :, 1, :], v[:, :, 0, hh - 1:hh].to_broadcast([P, TP // (2 * hh), hh])

            def sub(h, l):
                if l > 3:
                    dve.wait_ge(*filled(("level", h, l - 3, 1)))
                elif h:
                    dve.wait_ge(*filled({1: ("level", h - 1, 7, 1), 2: ("kt", h - 1, 1), 3: ("level", h - 1, 6, 1)}[l]))
                if l == 8:
                    ev = EL[7 % 3][:, 0:TP].rearrange("p (c n) -> p c n", c=NC)
                    bv = B[h % 2][:, 0:TP].rearrange("p (c n) -> p c n", c=NC)
                    me(TT(ev, bv[:, :, CH - 1:CH].to_broadcast([P, NC, CH]), bv, ALU.subtract), ex_arg)
                    return
                hh = LEVELS[l - 1]
                e0, e1, _ = halves(EL[(l - 1) % 3], hh)
                b0, b1, mid = halves(B[h % 2], hh)
                me(TT(e0, mid, b0, ALU.subtract))
                me(TT(e1, b1, mid, ALU.subtract), ex_arg)

            def mul(h, l):
                dve.wait_ge(ex_done, 8 * h + l)
                e = EL[(l - 1) % 3]
                if l == 8:
                    me(TT(e[:, 0:TP], e[:, 0:TP], K[h % 2][:, 0:TP], ALU.mult), lv_ready)
                    return
                hh = LEVELS[l - 1]
                e0, e1, _ = halves(e, hh)
                me(TT(e0, e0, halves(K[h % 2], hh)[0], ALU.mult))
                me(TT(e1, e1, halves(Q[h % 2], hh)[1], ALU.mult), lv_ready)

            def level(h, l):
                for b in range(2):
                    ps, fr = use(("level", h, l, b))
                    me(dve.copy_predicated(SC[:, 4 * b:4 * b + 4, :], masks[:, l:l + 1, :].to_broadcast([P, 4, CH]),
                                           ps.rearrange("p (c n) -> p c n", c=4)), fr)
                me.sync()

            def kv(h):
                dve.wait_ge(ex_a8, h + 1)
                if h:
                    dve.wait_ge(hp_saved, 16 * h)
                for b in range(2):
                    ps, fr = use(("kv", h, b))
                    for i in range(4):
                        k = 4 * b + i
                        me.sync()
                        me(STT(S_all[:, k + 1, :], S_all[:, k, :], A8[:, k:k + 1], ps[:, i * P:(i + 1) * P], ALU.mult, ALU.add),
                           fr if i == 3 else None)
                me.sync()

            def vb(h):
                tv = tA[:, 0:TP].rearrange("p (b n) -> p b n", b=NS)
                for b in range(2):
                    ps, fr = use(("vb", h, b))
                    me(TT(tv[:, 4 * b:4 * b + 4, :], ps.rearrange("p (b n) -> p b n", b=4),
                          K[h % 2][:, TP + 4 * b:TP + 4 * b + 4].unsqueeze(2).to_broadcast([P, 4, P]), ALU.mult), fr)

            def fin(h):
                dve.wait_ge(rms_e, h + 1)
                me(TT(O[:, :], O[:, :], tB[:, :], ALU.mult))
                me.sync()
                dve.wait_ge(sig_done, 2 * h + 2)
                me(STT(O[:, :], O[:, :], ng[:, :], SG[h % 2][:, :], ALU.mult, ALU.mult), o_full)

            first_level = True
            for step in ORDER:
                kind, c = step[0], step[1]
                if kind == "s5_param":
                    s5_angle()
                    s5_param()
                elif kind == "s5_prep":
                    s5_prep(c)
                elif kind == "s5_k":
                    s5_k(c)
                elif kind == "s5_d":
                    s5_d(c)
                elif kind == "hp_load" and c == 0:
                    dve.wait_ge(ys_out, 16 * HEADS)
                    dve.wait_ge(s5_out, 16 * HEADS)
                elif kind == "hp_a":
                    hp_a(c)
                elif kind == "hp_b":
                    hp_b(c)
                elif kind == "sub":
                    sub(c, step[2])
                elif kind == "mul":
                    mul(c, step[2])
                elif kind == "level":
                    if first_level:
                        dve.wait_ge(consts, 2)
                        first_level = False
                    level(c, step[2])
                elif kind == "kv":
                    kv(c)
                elif kind == "vb":
                    vb(c)
                elif kind == "fin":
                    fin(c)
                elif kind == "unit" and GLU_N <= c < OUT_N:
                    m = c - GLU_N
                    dve.wait_ge(evac[c % 2], c // 2 + 1)
                    if m:
                        dve.wait_ge(z_lo, m)
                    me(TT(st[2][:, 0:T], XH[:, m, :].bitcast(F32), XL[:, m, :].bitcast(F32), ALU.add))
                    me.sync()
                    me(TT(st[2][:, 0:T], st[2][:, 0:T], st[1][:, 0:T], ALU.mult), z_ready)
                elif kind == "unit" and c >= OUT_N:
                    m = c - OUT_N
                    dve.wait_ge(mm_done, c + 1)
                    dve.wait_ge(xt_in[m % 2], 16 * (m // 2 + 1))
                    if m == 0:
                        dve.wait_ge(o_out, 16 * (HEADS - 1))
                        dve.wait_ge(hp_saved, 16 * HEADS)
                        dve.wait_ge(hs_saved, 16 * HEADS)
                        dve.wait_ge(m_lo, HEADS)
                    me(STT(b3(R[:, m, :]), b3(xt[m % 2][:, :]), ALPHA, banks(c % 2), ALU.mult, ALU.add), evacuated(c))

            def layer_norm(w):
                for b in range(NB):
                    ps, fr = use(("ln", w, b))
                    me(dve.tensor_copy(rstd[:, CW * b:CW * b + CW], ps[:, 0:CW]), fr)
                me.sync()
                for m in range(KD):
                    me(TT(R[:, m, :], R[:, m, :], rstd[:, :], ALU.subtract), xc_ready)
                dve.wait_ge(var_e, w + 1)
                for m in range(KD):
                    me(TT(R[:, m, :], R[:, m, :], rstd[:, :], ALU.mult), t_ready)

            layer_norm(0)
            dve.wait_ge(x1_lo, KD)
            me(dve.memset(ub[0][:, 0:2], 0.0))
            me(dve.memset(ub[1][:, 0:2], 0.0), halo)
            n0 = FFN_N
            tick = 0
            for q, (j0, nk) in enumerate(PARTS):
                def pair(i):
                    for s in range(2):
                        jj = 2 * (j0 + i) + s
                        dve.wait_ge(evac[s], (n0 // 2) + i + 1)
                        dve.wait_ge(u_full, jj + 1)
                        dve.wait_ge(cp_in[s], 16 * (j0 + i + 1))
                        h_, u_, w = hb[s], ub[s], cp[s]
                        STT(h_[:, 0:TP], u_[:, 1:1 + TP], w[:, 1:2], h_[:, 0:TP], ALU.mult, ALU.add)
                        STT(h_[:, TP:T], w[:, 12:20], w[:, 1:2], h_[:, TP:T], ALU.mult, ALU.add).then_inc(h0_ready, 1)
                        dve.wait_ge(h0_ready, jj + 1)
                        STT(h_[:, 0:TP], u_[:, 0:TP], w[:, 0:1], h_[:, 0:TP], ALU.mult, ALU.add)
                        STT(h_[:, TP:T], w[:, 4:12], w[:, 0:1], h_[:, TP:T], ALU.mult, ALU.add).then_inc(conv_done, 1)
                    dve.wait_ge(silu_done, j0 + i + 1)
                    TT(hb[0][:, :], hb[0][:, :], hb[1][:, :], ALU.mult).then_inc(a_ready, 1)
                with dve.Fori(0, nk) as i:
                    pair(i)
                n0 += 2 * nk

                def down(i):
                    for s in range(2):
                        m = bass.ds(2 * i + s, 1)
                        n = n0 + 2 * i + s
                        dve.wait_ge(mm_done, n + 1)
                        r = R[:, m, :].rearrange("p a n -> p (a n)")
                        if q == 0:
                            STT(b3(r), b3(r), ALPHA, banks(s), ALU.mult, ALU.add).then_inc(evac[s], 1)
                        else:
                            TT(b3(r), b3(r), banks(s), ALU.add).then_inc(evac[s], 1)
                with dve.Fori(0, KD // 2) as i:
                    down(i)
                n0 += KD
            dve.wait_ge(evac[0], n0 // 2)
            dve.wait_ge(evac[1], n0 // 2)
            layer_norm(1)


_OUTS = [((KD, P, T), "yT"), ((HEADS, P, P), "hp"), ((HEADS, P, 2, PR, NS + 1), "s5st"),
         ((2 * JT, P, 2 + NS), "cache_new"), ((NS, HEADS, P, P), "hs"), ((NS, 2 * FF), "cache_row0")]


def _layout(x_prompt, x_sample, state_hgrn, state_s5_re, state_s5_im, cache_ffn_conv, w_in, hgrn_lb_logits, hgrn_norm_g,
            s5_lambda_re, s5_lambda_im, s5_log_dt, s5_b_re, s5_b_im, s5_c_re, s5_c_im, s5_d, w_glu, w_out, ln1_g, ln1_b,
            w_ffn_up, ffn_conv_w, ffn_conv_b, w_ffn_down, ln2_g, ln2_b):
    import numpy as np

    def tiles(w, kt, nt):
        return w.reshape(kt, P, nt, P).transpose(2, 1, 0, 3).reshape(nt, P, kt * P)

    x = np.concatenate([x_prompt[0], x_sample[:, 0]], axis=0)
    win = tiles(w_in[0], KD, 20)
    order_in = [16 + c for c in range(4)] + [b + h for h in range(4) for b in (4, 0, 12)]
    up = [t + JT * s for t in range(JT) for s in range(2)]

    def per_group(a):
        a = a.reshape((HEADS, PR, 2, SS) + a.shape[2:])
        return np.moveaxis(a, 1, 3).reshape((HEADS, P, -1))

    ldt = np.broadcast_to(s5_log_dt[0][:, None], (G, SS))
    s5q = np.stack([per_group(a) for a in (s5_lambda_re[0], s5_lambda_im[0], ldt)]).transpose(2, 0, 1, 3).reshape(P, -1)
    s5p = np.concatenate([per_group(a) for a in (
        s5_b_re[0], s5_b_im[0],
        s5_c_re[0].transpose(0, 2, 1), s5_c_im[0].transpose(0, 2, 1),
        state_s5_re[0].transpose(1, 2, 0), state_s5_im[0].transpose(1, 2, 0))], axis=2)
    cache = cache_ffn_conv[0]
    by_tile = lambda a: a.reshape(-1, 2 * JT, P).transpose(1, 2, 0)[up]
    convp = np.concatenate([by_tile(ffn_conv_w[0]), by_tile(ffn_conv_b), by_tile(cache[:, 0]), by_tile(cache[:, 1])], axis=2)
    d = dict(
        xT=x.T.reshape(KD, P, T), w_units=win[order_in], w_v=w_in[0][:, 1024:1536].reshape(KD, P, 512),
        w_glu=tiles(w_glu[0], HEADS, HEADS), w_out=tiles(w_out[0], KD, KD), w_up=tiles(w_ffn_up[0], KD, 2 * JT)[up],
        w_dn=tiles(w_ffn_down[0], JT, KD), s5q=s5q, s5p=s5p, dskip=s5_d[0].reshape(G, 16).T,
        lbl=hgrn_lb_logits[0].reshape(HEADS, P).T, normg=hgrn_norm_g.T,
        lnp=np.stack([a.reshape(KD, P).T for a in (ln1_g[0], ln1_b[0], ln2_g[0], ln2_b[0])], axis=1),
        convp=convp, s0=state_hgrn[0], cache_old=cache)
    return {k: np.ascontiguousarray(v) for k, v in d.items()}


def kernel(**inputs):
    import numpy as np
    import concourse.bacc as bacc
    from concourse.bass_utils import run_bass_kernel_spmd

    nc = bacc.Bacc("TRN2", target_bir_lowering=False, num_devices=1)
    arrays = _layout(**{k: np.asarray(v) for k, v in inputs.items()})
    args = [nc.dram_tensor(f"in_{k}", a.shape, F32, kind="ExternalInput").ap() for k, a in arrays.items()]
    args += [nc.dram_tensor(f"out_{k}", shape, F32, kind="ExternalOutput").ap() for shape, k in _OUTS]
    layer(nc, *args)
    r = run_bass_kernel_spmd(nc, [{f"in_{k}": a for k, a in arrays.items()}], core_ids=[0]).results[0]
    yT, hp, s5st, cn, hs, row0 = (r[f"out_{k}"] for _, k in _OUTS)
    y = yT.reshape(D, T).T
    s5 = s5st.reshape(HEADS, 2, SS, 2, PR, NS + 1).transpose(3, 5, 0, 4, 1, 2).reshape(2, NS + 1, G, SS)
    down = [2 * t + s for s in range(2) for t in range(JT)]
    rows = cn[down].reshape(2 * FF, 2 + NS).T
    return (np.ascontiguousarray(y[:TP])[None], np.ascontiguousarray(y[TP:])[:, None], hp[None, None],
            np.ascontiguousarray(s5[0, NS:])[None], np.ascontiguousarray(s5[1, NS:])[None],
            np.ascontiguousarray(rows[:2])[None, None], hs[None],
            np.ascontiguousarray(s5[0, :NS])[None], np.ascontiguousarray(s5[1, :NS])[None],
            np.stack([row0, rows[2:]], axis=1)[None])
```

```python
import concourse.bass as bass
from concourse import mybir
from contextlib import ExitStack

F32 = mybir.dt.float32
F32R = mybir.dt.float32r
ALU = mybir.AluOpType
ACT = mybir.ActivationFunctionType

P = 128
D = 1024
KD = D // P
TP = 1024
NS = 8
T = TP + NS
NB = 3
CW = T // NB
HEADS = 4
CH = 128
NC = TP // CH
FF = 2816
JT = FF // P
G = 32
GC = G // HEADS
PR = GC // 2
SS = 64
L = 8
NL = TP // L
UC = NS + NL + NS
HC = NS + 1 + NL
ALPHA = 2.0 ** 0.25
LN_EPS = 1e-5
RMS_EPS = 1e-6
F_FLOOR = 1e-20
TWO60 = 2.0 ** 60
PARTS = [(0, 8), (8, 7), (15, 7)]
TWO_PI_1 = 6.28125
TWO_PI_2 = 0.0019350051879882812
TWO_PI_3 = 3.019916050e-07
INV_TWO_PI = 0.15915494309189535
ROUND = 12582912.0
PI_SAFE = 3.1415925
U_N, F_N, GLU_N, OUT_N, FFN_N = 0, 4, 16, 20, 28
Y_GROUPS = [(0, 2, 4), (6,), (1, 3, 5), (7,)]
LEVELS = [1, 2, 4, 8, 16, 32, 64]


def unit_of(kind, h):
    return F_N + 3 * h + kind


DIRECT = (14, 15)


def rows_of(n):
    if n < GLU_N:
        return list(range(KD))
    if n < OUT_N:
        return list(range(HEADS))
    return list(range(HEADS, KD)) + list(range(HEADS))


def order():
    o, queue = [], []

    def unit(n, parts=None):
        last = len(rows_of(n)) - 1
        return [(1.32, [("part", n, i)] + ([("unit", n)] if i == last else []) +
                 ([("z", n - 1 - GLU_N)] if GLU_N < n < OUT_N and i == 1 else []))
                for i in (range(last + 1) if parts is None else parts)]

    def put(us):
        while us > 0 and queue:
            if (queue[0][1][-1] == ("unit", DIRECT[0]) and ("o", 1) not in o or
                    queue[0][1][-1] == ("unit", DIRECT[1]) and ("fin", 1) not in o):
                return
            t, steps = queue.pop(0)
            o.extend(steps)
            us -= t

    def before(*step):
        while queue and step not in o:
            put(0.1)

    queue += unit(0) + unit(1)
    o.append(("s5_param", 0))
    put(100)
    o.append(("wv", 0))
    queue += unit(2) + unit(3)
    later = [p for n in range(F_N, DIRECT[0]) for p in unit(n)]
    for t in range(NC + 1):
        queue += [(5.2, [("values", t)])] + later[:3]
        del later[:3]
    queue += later
    queue += unit(14, range(4)) + unit(15, range(4)) + unit(14, range(4, KD)) + unit(15, range(4, KD))
    for c in range(HEADS):
        o.append(("s5_prep", c))
        put(8)
        o += [("s5_k", c), ("s5_w", c)]
        put(9)
        if c == HEADS - 1:
            before("unit", unit_of(2, 0))
            o += [("hp_load", 0), ("hp_sig", 0)]
        o.append(("s5_d", c, 0))
        put(2)
        o.append(("s5_d", c, 1))
        put(9)
        o.append(("s5_y", c))
    o += [("hp_a", 0)]
    put(7)
    o += [("hp_b", 0), ("sub", 0, 1)]
    last = len(LEVELS)
    for h in range(HEADS):
        for l in range(last + 1):
            if l + 2 <= last + 1:
                o.append(("sub", h, l + 2))
            if l + 1 <= last + 1:
                o.append(("mul", h, l + 1))
            o.append(("level", h, l))
            more = {0: [("s0_load", h)] + ([("ms", h - 1)] if h else []),
                    1: [("fin", h - 1)] if h else [],
                    2: [("vb", h)],
                    3: [("hp_load", h + 1), ("qs", h)],
                    4: [("hp_sig", h + 1)],
                    5: [("hp_a", h + 1)],
                    6: [("hp_b", h + 1)]}.get(l, [])
            if l == 3 and h + 1 < HEADS:
                before("unit", unit_of(2, h + 1) if h + 1 < HEADS - 1 else unit_of(0, h + 1))
            if h == 2 and l == 4:
                before("unit", DIRECT[1])
            if l == 0 or l == 2 and h != 2:
                put(1.3)
            o += [s for s in more if s[1] < HEADS]
            if h == 2:
                if l < 3:
                    o.append(("gelu", l + 1))
                if l == 0:
                    o.append(("y_load", 3))
            if h == 3:
                if l == 2:
                    before("unit", OUT_N - 1)
                if l == 3:
                    o += [("z", HEADS - 1), ("mix_load", 0)]
                if 4 <= l <= 6:
                    o.append(("mix", l - 4))
                    if l < 6:
                        o.append(("mix_load", l - 3))
                if l == 5:
                    queue += unit(OUT_N, range(KD - 1)) + unit(OUT_N + 1, range(KD - 1))
            put({0: 2.5, 1: 2.6, 2: 1.3 if l < 4 else 2.6, 3: 2.6 if l < 3 else 1.3}[h]
                - (1.3 if l in (0, 2) and h < 2 else 0))
            if (h, l) == (2, 3):
                for n in range(GLU_N, OUT_N):
                    queue += unit(n)
        if h == 1:
            before("part", DIRECT[1], HEADS - 1)
            o += [("y_load", 0), ("y_load", 1)]
        o.append(("kt", h))
        put(1.3)
        if h + 1 < HEADS:
            o.append(("sub", h + 1, 1))
        o.append(("kv", h))
        if h == 1:
            o += [("gelu", 0), ("y_load", 2)]
        put((3.9, 2.6, 2.6, 2.6)[h])
        o += [("o", h), ("save", h)]
    put(3.9)
    o.append(("ms", HEADS - 1))
    put(3.9)
    o.append(("fin", HEADS - 1))
    o.append(("mix", HEADS - 1))
    put(100)
    queue += unit(OUT_N, [KD - 1]) + unit(OUT_N + 1, [KD - 1])
    for n in range(OUT_N + 2, FFN_N):
        queue += unit(n)
    put(1000)
    return o


ORDER = order()


def bank_uses():
    names = []
    parts = {"values": ("",), "s5_k": (0, 1), "s5_w": (0, 1), "s5_y": range(4),
             "kt": (0, 1), "kv": (0, 1), "vb": (0, 1), "o": (0, 1, "s"), "ms": range(NB)}
    for s in ORDER:
        if s[0] == "level":
            names += [s + (b,) for b in range(1 if s[2] else 2)]
        elif s[0] == "s5_d":
            names += [s[:2] + (f"{x}{s[2]}",) for x in ("re", "im")]
        elif s[0] in parts:
            names += [s + (x,) for x in parts[s[0]]]
    return {name: (i % 2, i // 2) for i, name in enumerate(names)}


USES = bank_uses()


class Lane:

    def __init__(self, eng, own):
        self.eng, self.own, self.count, self.last = eng, own, {}, None

    def __call__(self, ins, event=None, by=1):
        if isinstance(event, tuple):
            ins.then_inc(event[0], by)
            self.last = event
            return event
        sem = self.own if event is None else event
        ins.then_inc(sem, by)
        key = id(sem)
        self.count[key] = self.count.get(key, 0) + by
        self.last = (sem, self.count[key])
        return self.last

    def sync(self, token=None):
        token = token or self.last
        if token:
            self.eng.wait_ge(*token)


def layer(nc, xT, w_units, w_v, w_glu, w_out, w_up, w_dn, s5q, s5p, dskip, lbl, normg, lnp, convp, s0, cache_old,
          yT, hp, s5st, cache_new, hs, cache_row0):
    ctx = ExitStack()
    with ctx:
        def sb(name, shape, dt=F32, c=ctx):
            return c.enter_context(nc.sbuf_tensor(name, shape, dt))

        def sem(name):
            return ctx.enter_context(nc.semaphore(name))

        XH, XL = sb("XH", [P, KD, T], F32R), sb("XL", [P, KD, T], F32R)
        raw = [sb(f"raw{i}", [P, KD * P]) for i in range(2)]
        wh = [sb(f"wh{i}", [P, KD * P], F32R) for i in range(2)]
        wl = [sb(f"wl{i}", [P, KD * P], F32R) for i in range(2)]
        ident = sb("ident", [P, P])
        ones_rms = sb("ones_rms", [P, P])
        ones_ln = sb("ones_ln", [P, P])
        one = sb("one", [P, 1])
        eps_rms, eps_ln = sb("eps_rms", [P, 1]), sb("eps_ln", [P, 1])
        lb, oml, lbt = sb("lb", [P, HEADS]), sb("oml", [P, HEADS]), sb("lbt", [P, 3, HEADS])
        ng, ln_sb = sb("ng", [P, 1]), sb("ln_sb", [P, 4, KD])
        psum = ctx.enter_context(nc.psum_tensor("psum", [P, 8, 512], F32))

        ph1 = ExitStack()
        masks = sb("masks", [P, len(LEVELS) + 1, P], mybir.dt.int8, ph1)
        V, Vs = sb("V", [P, NC, 512], F32, ph1), sb("Vs", [NS, 512], F32, ph1)
        st = [sb(f"st{i}", [P, GC * (NS + NL)], F32, ph1) for i in range(3)]
        pa = ExitStack()
        WVH, WVL = sb("WVH", [P, KD, 512], F32R, pa), sb("WVL", [P, KD, 512], F32R, pa)
        U = sb("U", [P, GC, UC], F32, pa)
        TM = sb("TM", [P, GC, P], F32, pa)
        BT = [sb(f"BT{i}", [P, PR, P], F32, pa) for i in range(2)]
        prm = [sb(f"prm{i}", [P, 320], F32, pa) for i in range(2)]
        lam = sb("lam", [P, 3, G // 2], F32, pa)
        CA = [sb(f"CA{i}", [P, PR, L + 1, 16], F32, pa) for i in range(2)]
        E = sb("E", [P, 2, PR, NL], F32, pa)
        PW = sb("PW", [P, 2, G // 2, L + 1], F32, pa)
        G5 = [sb(f"G5{i}", [P, PR, NL], F32, pa) for i in range(2)]
        H5 = [sb(f"H5{i}", [P, PR, HC], F32, pa) for i in range(2)]
        ds_ = [sb(f"ds{i}", [P, PR, NS], F32, pa) for i in range(2)]
        KS = sb("KS", [16, GC, P], F32, pa)
        Ysb = sb("Ysb", [P, GC, NS + NL], F32, pa)
        dk = sb("dk", [16, G], F32, pa)
        sm = sb("sm", [P, 28, G // 2], F32, pa)
        bb = [sb(f"bb{i}", [P, PR, 16], F32, pa) for i in range(2)]
        s5o = sb("s5o", [P, 2, PR, NS + 1], F32, pa)
        ta5, tb5 = sb("ta5", [P, 1024], F32, pa), sb("tb5", [P, 1024], F32, pa)
        WB = [H5[i][:, :, NS + 1:NS + 1 + NL] for i in range(2)]
        pa.close()
        pb = ExitStack()
        FZ, Q = [sb(f"FZ{i}", [P, T], F32, pb) for i in range(2)], [sb(f"Q{i}", [P, T], F32, pb) for i in range(2)]
        SG, K = [sb(f"SG{i}", [P, T], F32, pb) for i in range(2)], [sb(f"K{i}", [P, T], F32, pb) for i in range(2)]
        B = FZ
        tA, tB = sb("tA", [P, T], F32, pb), sb("tB", [P, T], F32, pb)
        EL = [sb(f"EL{i}", [P, T], F32, pb) for i in range(3)]
        Qs = sb("Qs", [P, TP], F32, pb)
        SC = sb("SC", [P, NC, CH], F32, pb)
        KTQ = sb("KTQ", [P, T], F32, pb)
        KT = KTQ[:, 0:TP].rearrange("p (c n) -> p c n", c=NC)
        S_all = sb("S_all", [P, NC + 1, P], F32, pb)
        S0 = sb("S0", [P, NS, P], F32, pb)
        O = sb("O", [P, T], F32, pb)
        A8 = sb("A8", [P, NC], F32, pb)
        sel = sb("sel", [NS, NS, P], F32, pb)
        gbuf = sb("gbuf", [P, T], F32, pb)
        gel = [st[1][:, 0:T], gbuf[:, :]]
        pb.close()
        ph1.close()
        R = sb("R", [P, KD, T])
        p2 = ExitStack()
        xt = [sb(f"xt{i}", [P, T], F32, p2) for i in range(2)]
        racc = sb("racc", [P, T], F32, p2)
        sq = [sb(f"sq{i}", [P, T], F32, p2) for i in range(2)]
        rstd = sb("rstd", [P, T], F32, p2)
        p2.close()
        AH, AL = sb("AH", [P, PARTS[0][1], T], F32R), sb("AL", [P, PARTS[0][1], T], F32R)
        ub = [sb(f"ub{i}", [P, 2 + T]) for i in range(2)]
        hb = [sb(f"hb{i}", [P, T]) for i in range(2)]
        raccs = [racc[:, :], hb[1][:, :]]
        cp = [sb(f"cp{i}", [P, 20]) for i in range(2)]

        uscr = nc.dram_tensor("uscr", [HEADS, P, T], F32).ap()
        fscr = nc.dram_tensor("fscr", [3 * HEADS, P, T], F32).ap()
        yscr = nc.dram_tensor("yscr", [HEADS, P, GC * (NS + NL)], F32).ap()
        oscr = nc.dram_tensor("oscr", [HEADS, P, T], F32).ap()

        def sems(names):
            return (sem(x) for x in names.split())

        def two(name):
            return [sem(f"{name}{i}") for i in range(2)]

        loaded = two("loaded")
        hi_done, lo_done = sems("hi_done lo_done")
        mm_done = sem("mm_done")
        evac = two("evac")
        fill, free = two("fill"), two("free")
        act_own, dve_own, pool_own = sems("act_own dve_own pool_own")
        small_in, consts, dconsts, lbd, lbe = sems("small_in consts dconsts lbd lbe")
        x_in = [sem(f"x_in{i}") for i in range(3)]
        x_hi, x_lo = sems("x_hi x_lo")
        wv_in = [sem(f"wv_in{i}") for i in range(4)]
        wv_hi, wv_lo, x_used = sems("wv_hi wv_lo x_used")
        st_out = [sem(f"st_out{i}") for i in range(3)]
        prm_in, (lam_in, u_in, t_in) = two("prm_in"), sems("lam_in u_in t_in")
        p_dt, p_e, p_ang, p_sin, wb_ready, ca_ready, k_ready = sems("p_dt p_e p_ang p_sin wb_ready ca_ready k_ready")
        h5_ready, ys_out, s5_full, s5_out = sems("h5_ready ys_out s5_full s5_out")
        fq_in, (s0_in, hp_saved, hs_saved) = two("fq_in"), sems("s0_in hp_saved hs_saved")
        sig_done, lnarg, ln_done, b_ready = sems("sig_done lnarg ln_done b_ready")
        ex_arg, ex_done, ex_a8, lv_ready, qs_ready = sems("ex_arg ex_done ex_a8 lv_ready qs_ready")
        sn_ready, sq_ready, rms_e, o_full, o_out = sems("sn_ready sq_ready rms_e o_full o_out")
        y_in, (g_ready, g_hi, g_lo) = two("y_in"), sems("g_ready g_hi g_lo")
        z_ready, z_hi, z_lo, oa_in, m_hi, m_lo = sems("z_ready z_hi z_lo oa_in m_hi m_lo")
        xt_in, (racc_ready, xc_ready, sq_done, sq_mm) = two("xt_in"), sems("racc_ready xc_ready sq_done sq_mm")
        mean_mm = sem("mean_mm")
        var_e, t_ready, x1_hi, y_out = sems("var_e t_ready x1_hi y_out")
        x1_lo = two("x1_lo")
        cp_in, cache_out = two("cp_in"), two("cache_out")
        halo, u_full, h0_ready, conv_done, silu_done = sems("halo u_full h0_ready conv_done silu_done")
        a_ready, a_hi, a_lo, row0_out = sems("a_ready a_hi a_lo row0_out")
        block = ctx.enter_context(nc.Block())

        def banks(slot):
            return psum[:, 3 * slot:3 * slot + 3, 0:CW]

        wv_st = [G5[0][:, :, :].rearrange("p r n -> p (r n)"), G5[1][:, :, :].rearrange("p r n -> p (r n)"),
                 Ysb[:, 0:4, :].rearrange("p g n -> p (g n)")[:, 0:512], Ysb[:, 4:8, :].rearrange(
                     "p g n -> p (g n)")[:, 0:512]]

        def b3(ap):
            return ap.rearrange("p (b n) -> p b n", b=NB)

        def evacuated(n):
            return evac[n % 2], n // 2 + 1

        def filled(name):
            b, k = USES[name]
            return fill[b], k + 1

        def freed(name):
            b, k = USES[name]
            return free[b], k + 1

        def static_source(n):
            if n < GLU_N:
                return w_units[n], KD * P
            if n < OUT_N:
                return w_glu[n - GLU_N], HEADS * P
            return w_out[n - OUT_N], KD * P

        def stored(i, n):
            return st_out[i], 16 * len([m for m in range(min(n, DIRECT[0])) if m % 3 == i])

        @block.sync
        def _(sp):
            def load_weights(n, slot, src, width):
                if not isinstance(n, int) or n >= 2:
                    sp.wait_ge(lo_done, n - 1)
                sp.dma_start(raw[slot][:, 0:width], src).then_inc(loaded[slot], 16)

            def load_x(k):
                if k >= 3:
                    sp.wait_ge(x_lo, k - 2)
                sp.dma_start(st[k % 3][:, 0:T], xT[k]).then_inc(x_in[k % 3], 16)

            def load_wv(k):
                s = k % 4
                if k >= 4:
                    sp.wait_ge(wv_lo, k - 3)
                sp.dma_start(wv_st[s], w_v[k]).then_inc(wv_in[s], 16)

            def store_unit(n):
                sp.wait_ge(*evacuated(n))
                dst = uscr[n] if n < F_N else fscr[n - F_N]
                sp.dma_start(dst, st[n % 3][:, 0:T]).then_inc(st_out[n % 3], 16)

            def load_u(c):
                sp.wait_ge(st_out[c % 3], 16 * (c // 3 + 1))
                if c == 0:
                    sp.wait_ge(consts, 1)
                else:
                    sp.wait_ge(*filled(("s5_y", c - 1, 3)))
                v = uscr[c].rearrange("(g j) n -> j g n", j=16)
                for s in range(L):
                    sp.dma_start(U[16 * s:16 * s + 16, :, NS:NS + NL], v[:, :, NL * (7 - s):NL * (8 - s)]).then_inc(u_in, 16)
                sp.dma_start(U[16 * 7:16 * 8, :, 0:NS], v[:, :, TP:T]).then_inc(u_in, 16)
                sp.dma_start(U[0:16, :, NS + NL:UC], v[:, :, TP:T]).then_inc(u_in, 16)

            sp.dma_start(lam[:, :, :].rearrange("p f n -> p (f n)"), s5q).then_inc(lam_in, 16)
            load_x(0)
            load_weights(0, 0, w_units[0], KD * P)
            load_x(1)
            load_x(2)
            load_x(3)
            load_weights(1, 1, w_units[1], KD * P)
            load_x(4)
            for src, dst in ((lbl, lbt[:, 0, :]), (normg, ng[:, :]), (lnp, ln_sb[:, :, :]), (dskip, dk[:, :])):
                sp.dma_start(dst, src).then_inc(small_in, 16)
            for c in range(2):
                sp.dma_start(prm[c][:, :], s5p[c]).then_inc(prm_in[c], 16)
            for k in range(5, KD):
                load_x(k)
            load_weights(2, 0, w_units[2], KD * P)
            for k in range(4):
                load_wv(k)
            sp.dma_start(cache_row0, cache_old[:, 1, :]).then_inc(row0_out, 16)
            for step in ORDER:
                kind, c = step[0], step[1]
                if kind == "unit":
                    if c < DIRECT[0]:
                        store_unit(c)
                    if c + 3 < FFN_N:
                        src, width = static_source(c + 3)
                        load_weights(c + 3, (c + 3) % 2, src, width)
                    if c >= OUT_N and c - OUT_N + 2 < KD:
                        m = c - OUT_N + 2
                        sp.wait_ge(*evacuated(c))
                        sp.dma_start(xt[m % 2][:, :], xT[m]).then_inc(xt_in[m % 2], 16)
                elif kind == "s5_prep" and 0 < c < HEADS - 1:
                    sp.wait_ge(s5_full, c)
                    sp.dma_start(prm[(c + 1) % 2][:, :], s5p[c + 1]).then_inc(prm_in[(c + 1) % 2], 16)
                elif kind == "wv":
                    for k in range(4, KD):
                        load_wv(k)
                elif kind == "s5_k":
                    load_u(c)
                elif kind == "s5_d" and step[2] == 0:
                    sp.wait_ge(k_ready, 2 * (c + 1))
                    if c:
                        sp.wait_ge(*filled(("s5_y", c - 1, 3)))
                    for s in range(L):
                        sp.dma_start(TM[16 * (7 - s):16 * (8 - s), :, 16 * s:P], KS[:, :, 0:P - 16 * s]).then_inc(t_in, 16)
                elif kind == "s5_y":
                    sp.wait_ge(s5_full, c + 1)
                    sp.dma_start(s5st[c], s5o[:, :, :, :]).then_inc(s5_out, 16)
                    sp.wait_ge(*freed(("s5_y", c, 3)))
                    sp.wait_ge(*freed(("s5_y", c, 2)))
                    sp.dma_start(yscr[c], Ysb[:, :, :].rearrange("p g n -> p (g n)")).then_inc(ys_out, 16)
                elif kind == "hp_load":
                    if c == 0:
                        sp.wait_ge(*filled(("values", NC, "")))
                    elif c >= 2:
                        sp.wait_ge(o_full, c - 1)
                    for i, dst in enumerate((FZ, Q, SG)):
                        n = unit_of(i, c)
                        if n not in DIRECT:
                            sp.wait_ge(*stored(n % 3, n + 1))
                            sp.dma_start(dst[c % 2][:, :], fscr[n - F_N]).then_inc(fq_in[c % 2], 16)
                elif kind == "s0_load":
                    if c == 0:
                        sp.wait_ge(ys_out, 16 * HEADS)
                        sp.wait_ge(s5_out, 16 * HEADS)
                    else:
                        sp.wait_ge(hs_saved, 16 * c)
                        sp.wait_ge(*filled(("o", c - 1, "s")))
                    sp.dma_start(S0[:, :, :], s0[:, c].rearrange("b d e -> d b e")).then_inc(s0_in, 16)
                elif kind == "save":
                    sp.wait_ge(sn_ready, c + 1)
                    sp.dma_start(hs[:, c].rearrange("b d e -> d b e"), S0[:, :, :]).then_inc(hs_saved, 16)
                    sp.wait_ge(*freed(("kv", c, 1)))
                    sp.dma_start(hp[c], S_all[:, NC, :]).then_inc(hp_saved, 16)
                elif kind == "fin" and c < HEADS - 1:
                    sp.wait_ge(o_full, c + 1)
                    sp.dma_start(oscr[c], O[:, :]).then_inc(o_out, 16)
                elif kind == "y_load":
                    if c < 2:
                        sp.wait_ge(*stored((0, 2)[c], DIRECT[0]))
                    else:
                        sp.wait_ge(g_ready, c - 1)
                    v = yscr[c].rearrange("(t j) (g n) -> j g t n", j=16, g=GC)
                    for g in range(GC):
                        sp.dma_start(st[2 * (c % 2)][16 * g:16 * g + 16, :].rearrange("p (t n) -> p t n", t=L),
                                     v[:, g]).then_inc(y_in[c % 2], 16)
                elif kind == "mix_load":
                    sp.wait_ge(g_lo, HEADS)
                    sp.wait_ge(o_out, 16 * (c + 1))
                    if c >= 1:
                        sp.wait_ge(m_lo, c)
                    sp.dma_start(st[0][:, 0:T], oscr[c]).then_inc(oa_in, 16)
                elif kind == "mix" and c == HEADS - 1:
                    sp.wait_ge(m_lo, HEADS)
                    sp.wait_ge(hp_saved, 16 * HEADS)
                    sp.wait_ge(hs_saved, 16 * HEADS)
                    for m in range(2):
                        sp.dma_start(xt[m][:, :], xT[m]).then_inc(xt_in[m], 16)
            def conv_params(j0, i, s, first):
                if not first:
                    sp.wait_ge(conv_done, 2 * (j0 + i) + s - 1)
                sp.dma_start(cp[s][:, :], convp[bass.ds(2 * (j0 + i) + s, 1)].rearrange("a p n -> p (a n)")).then_inc(cp_in[s], 16)

            def store_cache(j):
                for s in range(2):
                    sp.wait_ge(u_full, 2 * j + s + 1)
                    sp.dma_start(cache_new[bass.ds(2 * j + s, 1)].rearrange("a p n -> p (a n)"), ub[s][:, TP:2 + T]).then_inc(cache_out[s], 16)

            n0 = FFN_N
            for j0, nk in PARTS:
                def pair(i, first=False):
                    for s in range(2):
                        load_weights(n0 + 2 * i + s, s, w_up[bass.ds(2 * (j0 + i) + s, 1)].rearrange("a p n -> p (a n)"), KD * P)
                        conv_params(j0, i, s, first)
                    if not first:
                        store_cache(j0 + i - 1)
                if j0 == 0:
                    pair(0, True)
                    with sp.Fori(1, nk) as i:
                        pair(i)
                else:
                    with sp.Fori(0, nk) as i:
                        pair(i)
                n0 += 2 * nk
                with sp.Fori(0, KD // 2) as i:
                    for s in range(2):
                        load_weights(n0 + 2 * i + s, s,
                                     w_dn[bass.ds(2 * i + s, 1), :, j0 * P:(j0 + nk) * P].rearrange("a p n -> p (a n)"), nk * P)
                n0 += KD
            store_cache(JT - 1)
            for m in range(KD):
                sp.wait_ge(x1_hi, KD + m + 1)
                sp.dma_start(yT[m], R[:, m, :]).then_inc(y_out, 16)
            sp.wait_ge(y_out, 16 * KD)
            sp.wait_ge(row0_out, 16)
            sp.wait_ge(s5_out, 16 * HEADS)
            sp.wait_ge(hp_saved, 16 * HEADS)
            sp.wait_ge(hs_saved, 16 * HEADS)
            for s in range(2):
                sp.wait_ge(cache_out[s], 16 * JT)

        @block.scalar
        def _(act):
            me = Lane(act, act_own)

            def exp_and_ln():
                act.preload_act_table_set("natural_log_exp_and_others")

            def split_hi(n, count, slot, width):
                act.wait_ge(loaded[slot], 16 * count)
                if not isinstance(n, int) or n >= 2:
                    act.wait_ge(mm_done, n - 1)
                me(act.activation(wh[slot][:, 0:width], raw[slot][:, 0:width], ACT.Copy), hi_done)

            for k in range(KD):
                act.wait_ge(x_in[k % 3], 16 * (k // 3 + 1))
                me(act.activation(XH[:, k, :], st[k % 3][:, 0:T], ACT.Copy), x_hi)
                if k == 0:
                    split_hi(0, 1, 0, KD * P)
                if k == 3:
                    split_hi(1, 1, 1, KD * P)
            act.wait_ge(lbd, 1)
            me(act.activation(lbt[:, 1, :], lbt[:, 1, :], ACT.Exp), lbe)


            def use(name):
                b, k = USES[name]
                act.wait_ge(fill[b], k + 1)
                return psum[:, 6 + b, :], (free[b], k + 1)

            for step in ORDER:
                kind, c = step[0], step[1]
                if kind == "unit":
                    s, h = c % 2, c // 2
                    act_unit = c < OUT_N
                    if act_unit:
                        act.wait_ge(mm_done, c + 1)
                    if c < GLU_N:
                        if c in DIRECT:
                            if c == DIRECT[0]:
                                act.wait_ge(*filled(("o", 1, "s")))
                            else:
                                act.wait_ge(o_full, 2)
                            act.wait_ge(sig_done, 4)
                            dst = (Q, SG)[c - DIRECT[0]][1][:, :]
                        else:
                            if c >= 3:
                                act.wait_ge(st_out[c % 3], 16 * (c // 3))
                            else:
                                act.wait_ge(x_lo, KD)
                            dst = st[c % 3][:, 0:T]
                        if c < F_N:
                            for b in range(NB):
                                nn = min(CW, TP - b * CW) // L
                                me(act.activation(dst[:, 0:TP].rearrange("p (t n) -> p n t", t=L)[:, 43 * b:43 * b + nn, :],
                                                  psum[:, 3 * s + b, 0:nn * L].rearrange("p (n t) -> p n t", t=L), ACT.Copy))
                            me(act.activation(dst[:, TP:T], psum[:, 3 * s + 2, CW - NS:CW], ACT.Copy), evacuated(c))
                        else:
                            me(act.activation(b3(dst), banks(s), ACT.Copy), evacuated(c))
                    elif c < OUT_N:
                        m = c - GLU_N
                        if m:
                            act.wait_ge(z_ready, m)
                        else:
                            act.wait_ge(g_lo, HEADS)
                        me(act.activation(b3(st[1][:, 0:T]), banks(s), ACT.Sigmoid), evacuated(c))
                        exp_and_ln()
                    split_hi(c + 2, h + 2, s, static_source(c + 2)[1] if c + 2 < FFN_N else KD * P)
                elif kind == "z":
                    act.wait_ge(z_ready, c + 1)
                    me(act.activation(XH[:, HEADS + c, :], st[2][:, 0:T], ACT.Copy), z_hi)
                elif kind == "values":
                    ps, fr = use((kind, c, ""))
                    me(act.activation(V[:, c, :] if c < NC else Vs[:, :], ps[0:P if c < NC else NS, :], ACT.Copy), fr)
                elif kind == "s5_w":
                    for i in range(2):
                        ps, fr = use((kind, c, i))
                        me(act.activation(BT[i][:, :, :], ps.rearrange("p (r n) -> p r n", r=PR), ACT.Copy), fr)
                elif kind == "s5_y":
                    if c:
                        act.wait_ge(ys_out, 16 * c)
                    for q in range(4):
                        ps, fr = use((kind, c, q))
                        gs = Y_GROUPS[q]
                        me(act.activation(Ysb[:, gs[0]:gs[-1] + 1:2, :], ps[:, 0:len(gs) * (NS + NL)].rearrange(
                            "p (g n) -> p g n", n=NS + NL), ACT.Copy), fr)
                elif kind == "hp_sig":
                    act.wait_ge(fq_in[c % 2], (48, 48, 96, 64)[c])
                    if c == HEADS - 1:
                        act.wait_ge(*evacuated(DIRECT[1]))
                    fz = FZ[c % 2]
                    me(act.activation(K[c % 2][:, :], fz[:, :], ACT.Sigmoid, scale=-1.0))
                    me.sync()
                    me(act.activation(fz[:, :], fz[:, :], ACT.Sigmoid), sig_done)
                    me(act.activation(SG[c % 2][:, :], SG[c % 2][:, :], ACT.Sigmoid), sig_done)
                    exp_and_ln()
                elif kind == "hp_a":
                    act.wait_ge(lnarg, c + 1)
                    me(act.activation(tA[:, 0:TP], tA[:, 0:TP], ACT.Ln))
                    me(act.activation(tB[:, 0:TP], tB[:, 0:TP], ACT.Ln), ln_done)
                elif kind == "sub":
                    l = step[2]
                    act.wait_ge(ex_arg, 8 * c + l)
                    e = EL[(l - 1) % 3]
                    me(act.activation(e[:, 0:TP], e[:, 0:TP], ACT.Exp), ex_done)
                elif kind == "qs":
                    act.wait_ge(b_ready, c + 1)
                    me(act.activation(Qs[:, :], B[c % 2][:, 0:TP], ACT.Exp))
                    me(act.activation(A8[:, :], B[c % 2][:, CH - 1:TP:CH], ACT.Exp), ex_a8)
                elif kind == "kt":
                    if c:
                        act.wait_ge(*filled(("ms", c - 1, 2)))
                    for b in range(2):
                        ps, fr = use((kind, c, b))
                        me(act.activation(KT[:, 4 * b:4 * b + 4, :], ps.rearrange("p (c n) -> p c n", c=4), ACT.Copy), fr)
                elif kind == "o":
                    if c:
                        act.wait_ge(o_out, 16 * c)
                    for b in range(2):
                        ps, fr = use((kind, c, b))
                        me(act.activation(O[:, 512 * b:512 * b + 512], ps, ACT.Copy), fr)
                    ps, fr = use((kind, c, "s"))
                    me(act.activation(O[:, TP:T], ps[:, 0:NS], ACT.Copy), fr)
                    me.sync()
                    me(act.activation(KTQ[:, :], O[:, :], ACT.Square), sq_ready)
                elif kind == "ms":
                    if c + 1 < HEADS:
                        act.wait_ge(b_ready, c + 2)
                    for b in range(NB):
                        ps, fr = use((kind, c, b))
                        me(act.activation(tB[:, CW * b:CW * b + CW], ps[:, 0:CW], ACT.Ln, bias=eps_rms[:, :]), fr)
                    me.sync()
                    me(act.activation(tB[:, :], tB[:, :], ACT.Exp, scale=-0.5), rms_e)
                elif kind == "gelu":
                    act.wait_ge(y_in[c % 2], 16 * GC * (c // 2 + 1))
                    if c >= 2:
                        act.wait_ge(g_lo, c - 1)
                    elif c == 0:
                        act.wait_ge(x_used, 1)
                        act.wait_ge(*stored(1, DIRECT[0]))
                    src = st[2 * (c % 2)][:, :].rearrange("p (t n) -> p n t", t=L)
                    out = gel[c % 2]
                    me(act.activation(out[:, 0:TP].rearrange("p (n t) -> p n t", t=L), src[:, NS:NS + NL, :], ACT.Gelu))
                    me(act.activation(out[:, TP:T], src[:, 0:NS, 0], ACT.Gelu), g_ready)
                    exp_and_ln()
                    me.sync()
                    me(act.activation(XH[:, c, :], out, ACT.Copy), g_hi)
                elif kind == "mix":
                    if c < HEADS - 1:
                        act.wait_ge(oa_in, 16 * (c + 1))
                    else:
                        act.wait_ge(o_full, HEADS)
                    act.wait_ge(mm_done, OUT_N)
                    me(act.activation(XH[:, c, :], st[0][:, 0:T] if c < HEADS - 1 else O[:, :], ACT.Copy), m_hi)
                elif kind == "wv":
                    for k in range(KD):
                        act.wait_ge(wv_in[k % 4], 16 * (k // 4 + 1))
                        me(act.activation(WVH[:, k, :], wv_st[k % 4], ACT.Copy), wv_hi)
                elif kind == "s5_param":
                    act.wait_ge(lam_in, 16)
                    me(act.activation(sm[:, 0, :], lam[:, 2, :], ACT.Exp), p_dt)
                    act.wait_ge(p_e, 1)
                    me(act.activation(sm[:, 2, :], sm[:, 1, :], ACT.Exp))
                    me(act.activation(sm[:, 3, :], sm[:, 1, :], ACT.Exp, scale=float(L)))
                    act.wait_ge(p_ang, 1)
                    me(act.activation(sm[:, 6:8, :], sm[:, 4:6, :], ACT.Sin), p_sin)

            def layer_norm(w):
                exp_and_ln()
                for m in range(KD):
                    act.wait_ge(xc_ready, KD * w + m + 1)
                    if KD * w + m >= 2:
                        act.wait_ge(sq_mm, KD * w + m - 1)
                    me(act.activation(sq[m % 2][:, :], R[:, m, :], ACT.Square), sq_done)
                act.wait_ge(sq_mm, KD * (w + 1))
                me(act.activation(b3(rstd[:, :]), banks(1), ACT.Ln, bias=eps_ln[:, :]))
                me.sync()
                me(act.activation(rstd[:, :], rstd[:, :], ACT.Exp, scale=-0.5), var_e)

            layer_norm(0)
            for m in range(KD):
                act.wait_ge(t_ready, m + 1)
                if m == 0:
                    act.wait_ge(mm_done, FFN_N)
                me(act.activation(R[:, m, :], R[:, m, :], ACT.Identity, scale=ln_sb[:, 0, m:m + 1], bias=ln_sb[:, 1, m:m + 1]))
                me.sync()
                me(act.activation(XH[:, m, :], R[:, m, :], ACT.Copy), x1_hi)
            n0 = FFN_N
            nhi = None
            for q, (j0, nk) in enumerate(PARTS):
                def pair(i, first=False, last=False):
                    for s in range(2):
                        n = n0 + 2 * i + s
                        jj = 2 * (j0 + i) + s
                        act.wait_ge(mm_done, n + 1)
                        if not first:
                            act.wait_ge(conv_done, jj - 1)
                            act.wait_ge(cache_out[s], 16 * (j0 + i))
                            act.wait_ge(a_lo, j0 + i)
                        elif s == 0:
                            act.wait_ge(halo, 1)
                            act.wait_ge(x1_lo[0], KD // 2)
                            act.wait_ge(x1_lo[1], KD // 2)
                        act.wait_ge(cp_in[s], 16 * (j0 + i + 1))
                        act.activation(b3(ub[s][:, 2:2 + T]), banks(s), ACT.Copy).then_inc(u_full, 1)
                        act.activation(b3(hb[s][:, :]), banks(s), ACT.Identity, scale=cp[s][:, 2:3], bias=cp[s][:, 3:4]).then_inc(evac[s], 1)
                        if not last:
                            act.wait_ge(loaded[s], 16 * (n0 // 2 + i + 2))
                            act.activation(wh[s][:, :], raw[s][:, :], ACT.Copy).then_inc(hi_done, 1)
                        else:
                            act.wait_ge(loaded[s], 16 * (n0 // 2 + i + 2))
                            act.activation(wh[s][:, 0:nk * P], raw[s][:, 0:nk * P], ACT.Copy).then_inc(hi_done, 1)
                    act.wait_ge(conv_done, 2 * (j0 + i) + 2)
                    act.activation(hb[1][:, :], hb[1][:, :], ACT.Silu).then_inc(silu_done, 1)
                    act.wait_ge(a_ready, j0 + i + 1)
                    act.activation(AH[:, bass.ds(i, 1), :].rearrange("p a n -> p (a n)"), hb[0][:, :], ACT.Copy).then_inc(a_hi, 1)
                a = 0
                if j0 == 0:
                    pair(0, first=True)
                    a = 1
                with act.Fori(a, nk - 1) as i:
                    pair(i)
                pair(nk - 1, last=True)
                n0 += 2 * nk
                with act.Fori(0, KD // 2 - 1) as i:
                    for s in range(2):
                        act.wait_ge(loaded[s], 16 * (n0 // 2 + i + 2))
                        act.wait_ge(mm_done, n0 + 2 * i + s + 1)
                        act.activation(wh[s][:, 0:nk * P], raw[s][:, 0:nk * P], ACT.Copy).then_inc(hi_done, 1)
                n0 += KD
                if q + 1 < len(PARTS):
                    for s in range(2):
                        act.wait_ge(loaded[s], 16 * (n0 // 2 + 1))
                        act.wait_ge(mm_done, n0 + s - 1)
                        act.activation(wh[s][:, :], raw[s][:, :], ACT.Copy).then_inc(hi_done, 1)
            layer_norm(1)
            for m in range(KD):
                act.wait_ge(t_ready, KD + m + 1)
                me(act.activation(R[:, m, :], R[:, m, :], ACT.Identity, scale=ln_sb[:, 2, m:m + 1], bias=ln_sb[:, 3, m:m + 1]), x1_hi)

        @block.gpsimd
        def _(pool):
            me = Lane(pool, pool_own)
            def split_lo(n, slot, width):
                pool.wait_ge(hi_done, n + 1)
                me(pool.tensor_tensor(wl[slot][:, 0:width], raw[slot][:, 0:width], wh[slot][:, 0:width].bitcast(F32), ALU.subtract), lo_done)

            def split(dst, src, hi):
                return pool.tensor_tensor(dst, src, hi.bitcast(F32), ALU.subtract)

            split_lo(0, 0, KD * P)
            me(pool.memset(ident[:, :], 0.0))
            me.sync()
            me(pool.affine_select(out=ident[:, :], in_=ident[:, :], compare_op=ALU.not_equal, fill=1.0, base=0,
                                  pattern=[[-1, P]], channel_multiplier=1))
            me(pool.memset(U[:, :, :], 0.0))
            me(pool.memset(TM[:, :, :], 0.0))
            me(pool.memset(H5[0][:, :, :], 0.0))
            me(pool.memset(H5[1][:, :, :], 0.0), consts)
            split_lo(1, 1, KD * P)
            me(pool.memset(masks[:, :, :], 0.0))
            me.sync()
            me(pool.affine_select(out=masks[:, 0, :], in_=masks[:, 0, :], compare_op=ALU.not_equal, fill=1.0, base=0,
                                  pattern=[[-1, P]], channel_multiplier=1))
            for l, hh in enumerate(LEVELS):
                v = masks[:, l + 1, :].rearrange("p (b two x) -> p b two x", two=2, x=hh)[:, :, 1, :]
                me(pool.memset(v, 1.0))
                me.sync()
                me(pool.affine_select(out=v, in_=v, compare_op=ALU.is_ge, fill=0.0, base=0,
                                      pattern=[[-2 * hh, P // (2 * hh)], [0, hh]], channel_multiplier=1))
                me.sync()
                me(pool.affine_select(out=v, in_=v, compare_op=ALU.is_ge, fill=0.0, base=hh - 1,
                                      pattern=[[2 * hh, P // (2 * hh)], [0, hh]], channel_multiplier=-1))
            for step in ORDER:
                kind, c = step[0], step[1]
                if kind == "z":
                    pool.wait_ge(z_hi, c + 1)
                    me(split(XL[:, HEADS + c, :], st[2][:, 0:T], XH[:, HEADS + c, :]), z_lo)
                elif kind == "unit":
                    m = c - OUT_N
                    if 1 <= m < KD - 1:
                        pool.wait_ge(*evacuated(OUT_N))
                        pool.wait_ge(*evacuated(c))
                        if m > 1:
                            me.sync(summed)
                        summed = me(pool.tensor_tensor(racc[:, :], R[:, 0, :] if m == 1 else racc[:, :], R[:, m, :], ALU.add),
                                    racc_ready if m == KD - 2 else None)
                    split_lo(c + 2, c % 2, static_source(c + 2)[1] if c + 2 < FFN_N else KD * P)
                elif kind == "wv":
                    for k in range(KD):
                        pool.wait_ge(wv_hi, k + 1)
                        me(split(WVL[:, k, :], wv_st[k % 4], WVH[:, k, :]), wv_lo)
                elif kind == "hp_a" and c == 0:
                    pool.wait_ge(ys_out, 16 * HEADS)
                    pool.wait_ge(s5_out, 16 * HEADS)
                    me(pool.memset(sel[:, :, :], 0.0))
                    me(pool.memset(SC[:, :, :], 0.0))
                    me(pool.memset(S_all[:, 0, :], 0.0))
                    me.sync()
                    me(pool.affine_select(out=sel[:, :, :], in_=sel[:, :, :], compare_op=ALU.not_equal, fill=1.0, base=0,
                                          pattern=[[-1, NS], [0, P]], channel_multiplier=1), consts)
                elif kind == "vb":
                    pool.wait_ge(s0_in, 16 * (c + 1))
                    pool.wait_ge(b_ready, c + 1)
                    me(pool.tensor_tensor(S0[:, :, :], S0[:, :, :], FZ[c % 2][:, TP:T].unsqueeze(2).to_broadcast([P, NS, P]), ALU.mult))
                    pool.wait_ge(*freed((kind, c, 0)))
                    pool.wait_ge(*freed((kind, c, 1)))
                    me.sync()
                    me(pool.tensor_tensor(S0[:, :, :], S0[:, :, :], tA[:, 0:TP].rearrange("p (b n) -> p b n", b=NS), ALU.add), sn_ready)
                elif kind == "qs":
                    pool.wait_ge(ex_a8, c + 1)
                    me(pool.tensor_tensor(Qs[:, :], Qs[:, :], Q[c % 2][:, 0:TP], ALU.mult), qs_ready)
                elif kind == "gelu":
                    pool.wait_ge(g_hi, c + 1)
                    me(split(XL[:, c, :], gel[c % 2], XH[:, c, :]), g_lo)
                elif kind == "mix":
                    pool.wait_ge(m_hi, c + 1)
                    me(split(XL[:, c, :], st[0][:, 0:T] if c < HEADS - 1 else O[:, :], XH[:, c, :]), m_lo)
            for m in range(1, KD, 2):
                pool.wait_ge(x1_hi, m + 1)
                me(split(XL[:, m, :], R[:, m, :], XH[:, m, :]), x1_lo[1])
            n0 = FFN_N
            for q, (j0, nk) in enumerate(PARTS):
                def pair(i, width):
                    for s in range(2):
                        pool.wait_ge(hi_done, n0 + 2 * i + s + 3)
                        pool.tensor_tensor(wl[s][:, 0:width], raw[s][:, 0:width], wh[s][:, 0:width].bitcast(F32), ALU.subtract).then_inc(lo_done, 1)
                    pool.wait_ge(a_hi, j0 + i + 1)
                    a = bass.ds(i, 1)
                    pool.tensor_tensor(AL[:, a, :].rearrange("p a n -> p (a n)"), hb[0][:, :],
                                       AH[:, a, :].rearrange("p a n -> p (a n)").bitcast(F32), ALU.subtract).then_inc(a_lo, 1)
                with pool.Fori(0, nk - 1) as i:
                    pair(i, KD * P)
                pair(nk - 1, nk * P)
                n0 += 2 * nk
                if q + 1 < len(PARTS):
                    with pool.Fori(0, KD // 2 - 1) as i:
                        for s in range(2):
                            pool.wait_ge(hi_done, n0 + 2 * i + s + 3)
                            pool.tensor_tensor(wl[s][:, 0:nk * P], raw[s][:, 0:nk * P], wh[s][:, 0:nk * P].bitcast(F32), ALU.subtract).then_inc(lo_done, 1)
                else:
                    for m in range(KD):
                        if m < KD - 1:
                            pool.wait_ge(evac[m % 2], (n0 + m) // 2 + 1)
                        if 1 <= m < KD - 1:
                            if m > 1:
                                me.sync(summed)
                            summed = me(pool.tensor_tensor(raccs[1], R[:, 0, :] if m == 1 else raccs[1], R[:, m, :], ALU.add),
                                        racc_ready if m == KD - 2 else None)
                        if m + 2 < KD:
                            split_lo(n0 + m + 2, m % 2, nk * P)
                n0 += KD
                if q + 1 < len(PARTS):
                    for s in range(2):
                        pool.wait_ge(hi_done, n0 + s + 1)
                        pool.tensor_tensor(wl[s][:, :], raw[s][:, :], wh[s][:, :].bitcast(F32), ALU.subtract).then_inc(lo_done, 1)

        @block.tensor
        def _(pe):
            def products(slot, k, xh, xl, first, last):
                w_h, w_l = wh[slot][:, k * P:(k + 1) * P], wl[slot][:, k * P:(k + 1) * P]
                for p_, (w, x) in enumerate(((w_h, xh), (w_h, xl), (w_l, xh))):
                    for b in range(NB):
                        ins = nc.tensor.matmul(psum[:, 3 * slot + b, 0:CW], w, x[:, k, CW * b:CW * b + CW],
                                               start=(first and p_ == 0), stop=(last and p_ == 2))
                return ins

            def unit(n, slot, nk, xh, xl, ready=None):
                pe.wait_ge(lo_done, n + 1)
                if not isinstance(n, int) or n >= 2:
                    pe.wait_ge(evac[slot], (n0_half(n)))
                for k in range(nk):
                    if ready:
                        ready(k)
                    last = products(slot, k, xh, xl, k == 0, k == nk - 1)
                last.then_inc(mm_done, 1)

            half = {}

            def n0_half(n):
                return half["v"] if half.get("v") is not None else n // 2

            class Use:
                def __init__(self, name):
                    self.b, k = USES[name]
                    if k:
                        pe.wait_ge(free[self.b], k)
                    self.ps = psum[:, 6 + self.b, :]

                def done(self, ins):
                    ins.then_inc(fill[self.b], 1)

            pe.wait_ge(x_lo, 1)
            for step in ORDER:
                kind, c = step[0], step[1]
                if kind == "part":
                    i, s, rows = step[2], c % 2, rows_of(c)
                    k = rows[i]
                    if i == 0:
                        pe.wait_ge(lo_done, c + 1)
                        if c >= 2:
                            pe.wait_ge(evac[s], c // 2)
                    if c == 0:
                        pe.wait_ge(x_lo, k + 1)
                    elif c == GLU_N:
                        pe.wait_ge(g_lo, HEADS)
                    elif c >= OUT_N and k >= HEADS:
                        pe.wait_ge(z_lo, HEADS)
                    elif c >= OUT_N:
                        pe.wait_ge(m_lo, k + 1)
                    last = products(s, k, XH, XL, i == 0, i == len(rows) - 1)
                    if i == len(rows) - 1:
                        last.then_inc(mm_done, 1)
                    elif (c, i) == (GLU_N - 1, HEADS - 1):
                        last.then_inc(x_used, 1)
                elif kind == "values":
                    cols = slice(c * P, c * P + P) if c < NC else slice(TP, T)
                    u = Use((kind, c, ""))
                    for k in range(KD):
                        pe.wait_ge(wv_lo, k + 1)
                        for p_, (x, w) in enumerate(((XH, WVH), (XH, WVL), (XL, WVH))):
                            last = nc.tensor.matmul(u.ps[0:P if c < NC else NS, :], x[:, k, cols], w[:, k, :],
                                                    start=(k == 0 and p_ == 0), stop=(k == KD - 1 and p_ == 2))
                    u.done(last)
                elif kind == "s5_k":
                    pe.wait_ge(ca_ready, c + 1)
                    for q in range(2):
                        u = Use((kind, c, q))
                        for r in range(PR):
                            lo = SS * q
                            o = u.ps[0:16, r * P:(r + 1) * P]
                            for i in range(2):
                                last = nc.tensor.matmul(o, bb[i][lo:lo + SS, r, :],
                                                        CA[i][lo:lo + SS, r, 0:L, :].rearrange("p t j -> p (t j)"),
                                                        start=(i == 0), stop=(i == 1))
                        u.done(last)
                elif kind == "s5_w":
                    pe.wait_ge(wb_ready, c + 1)
                    for i in range(2):
                        u = Use((kind, c, i))
                        for r in range(PR):
                            last = nc.tensor.transpose(u.ps[:, r * P:(r + 1) * P], WB[i][:, r, :], ident[:, :])
                        u.done(last)
                elif kind == "s5_d":
                    pe.wait_ge(*freed(("s5_w", c, 0)))
                    pe.wait_ge(*freed(("s5_w", c, 1)))
                    pe.wait_ge(u_in, 160 * (c + 1))
                    for q in (step[2],):
                        for i, x in enumerate(("re", "im")):
                            u = Use((kind, c, f"{x}{q}"))
                            for rr in range(2):
                                for gi in range(2):
                                    r = 2 * q + rr
                                    last = nc.tensor.matmul(u.ps[SS * gi:SS * gi + SS, rr * UC:(rr + 1) * UC],
                                                            BT[i][:, r, SS * gi:SS * gi + SS], U[:, 2 * r + gi, :],
                                                            start=True, stop=True)
                            u.done(last)
                elif kind == "s5_y":
                    pe.wait_ge(h5_ready, c + 1)
                    pe.wait_ge(t_in, 16 * L * (c + 1))
                    for q in range(4):
                        u = Use((kind, c, q))
                        for i, g in enumerate(Y_GROUPS[q]):
                            r, lo = g // 2, SS * (g % 2)
                            o = u.ps[:, i * (NS + NL):(i + 1) * (NS + NL)]
                            nc.tensor.matmul(o, TM[:, g, :], U[:, g, 0:NS + NL], start=True, stop=False)
                            for i in range(2):
                                last = nc.tensor.matmul(o, CA[i][lo:lo + SS, r, 1:L + 1, :].rearrange("p t j -> p (t j)"),
                                                        H5[i][lo:lo + SS, r, 0:NS + NL], start=False, stop=(i == 1))
                        u.done(last)
                elif kind == "level":
                    l = step[2]
                    if l == 0:
                        pe.wait_ge(b_ready, c + 1)
                    else:
                        pe.wait_ge(lv_ready, 8 * c + l)
                    for b in range(1 if l else 2):
                        u = Use((kind, c, l, b))
                        for i in range(NC if l else 4):
                            t = slice((4 * b + i) * CH, (4 * b + i + 1) * CH)
                            if l == 0:
                                last = nc.tensor.matmul(u.ps[:, i * CH:(i + 1) * CH], K[c % 2][:, t], Q[c % 2][:, t],
                                                        start=True, stop=True)
                            else:
                                e, hh = EL[(l - 1) % 3], LEVELS[l - 1]
                                last = nc.tensor.matmul(u.ps[:, i * CH // 2:(i + 1) * CH // 2].rearrange("p (b x) -> p b x", x=hh),
                                                        e[:, t], e[:, t].rearrange("p (b two x) -> p b two x", two=2, x=hh)[:, :, 1, :],
                                                        start=True, stop=True)
                        u.done(last)
                elif kind == "kt":
                    pe.wait_ge(lv_ready, 8 * c + 8)
                    e = EL[7 % 3]
                    for b in range(2):
                        u = Use((kind, c, b))
                        for i in range(4):
                            t = slice((4 * b + i) * CH, (4 * b + i + 1) * CH)
                            last = nc.tensor.transpose(u.ps[:, i * CH:(i + 1) * CH], e[:, t], ident[:, :])
                        u.done(last)
                elif kind == "kv":
                    for b in range(2):
                        pe.wait_ge(*freed(("kt", c, b)))
                        u = Use((kind, c, b))
                        for i in range(4):
                            last = nc.tensor.matmul(u.ps[:, i * P:(i + 1) * P], KT[:, 4 * b + i, :],
                                                    V[:, 4 * b + i, c * P:(c + 1) * P], start=True, stop=True)
                        u.done(last)
                elif kind == "vb":
                    pe.wait_ge(consts, 2)
                    for b in range(2):
                        u = Use((kind, c, b))
                        for i in range(4):
                            last = nc.tensor.matmul(u.ps[:, i * P:(i + 1) * P], sel[:, 4 * b + i, :],
                                                    Vs[:, c * P:(c + 1) * P], start=True, stop=True)
                        u.done(last)
                elif kind == "o":
                    pe.wait_ge(*freed(("level", c, len(LEVELS), 0)))
                    pe.wait_ge(qs_ready, c + 1)
                    for b in range(2):
                        pe.wait_ge(*freed(("kv", c, b)))
                        u = Use((kind, c, b))
                        for i in range(4):
                            k = 4 * b + i
                            o = u.ps[:, i * CH:(i + 1) * CH]
                            nc.tensor.matmul(o, V[:, k, c * P:(c + 1) * P], SC[:, k, :], start=True, stop=False)
                            last = nc.tensor.matmul(o, S_all[:, k, :], Qs[:, k * CH:(k + 1) * CH], start=False, stop=True)
                        u.done(last)
                    pe.wait_ge(sn_ready, c + 1)
                    u = Use((kind, c, "s"))
                    for b in range(NS):
                        last = nc.tensor.matmul(u.ps[:, b:b + 1], S0[:, b, :], Q[c % 2][:, TP + b:TP + b + 1], start=True, stop=True)
                    u.done(last)
                elif kind == "ms":
                    pe.wait_ge(sq_ready, c + 1)
                    for b in range(NB):
                        u = Use((kind, c, b))
                        u.done(nc.tensor.matmul(u.ps[:, 0:CW], ones_rms[:, :], KTQ[:, CW * b:CW * b + CW], start=True, stop=True))

            def layer_norm(w, n_units):
                pe.wait_ge(racc_ready, w + 1)
                pe.wait_ge(evac[0], n_units // 2)
                for b in range(NB):
                    nc.tensor.matmul(psum[:, b, 0:CW], ones_ln[:, :], raccs[w][:, CW * b:CW * b + CW], start=True, stop=False)
                pe.wait_ge(evac[1], n_units // 2)
                for b in range(NB):
                    last = nc.tensor.matmul(psum[:, b, 0:CW], ones_ln[:, :], R[:, KD - 1, CW * b:CW * b + CW], start=False, stop=True)
                last.then_inc(mean_mm, 1)
                for m in range(KD):
                    pe.wait_ge(sq_done, KD * w + m + 1)
                    for b in range(NB):
                        last = nc.tensor.matmul(psum[:, 3 + b, 0:CW], ones_ln[:, :], sq[m % 2][:, CW * b:CW * b + CW],
                                                start=(m == 0), stop=(m == KD - 1))
                    last.then_inc(sq_mm, 1)

            layer_norm(0, FFN_N)
            n0 = FFN_N
            for q, (j0, nk) in enumerate(PARTS):
                def pair(i):
                    for s in range(2):
                        half["v"] = n0 // 2 + i
                        unit(n0 + 2 * i + s, s, KD, XH, XL)

                def staggered(parts, nk, xh, xl, ready):
                    for s, k in parts:
                        if k == 0:
                            pe.wait_ge(lo_done, n0 + s + 1)
                            pe.wait_ge(evac[s], n0 // 2)
                        pe.wait_ge(*ready(k))
                        last = products(s, k, xh, xl, k == 0, k == nk - 1)
                        if k == nk - 1:
                            last.then_inc(mm_done, 1)

                a = 0
                if q == 0:
                    pe.wait_ge(var_e, 1)
                    parts = [(s, k) for k in range(4) for s in range(2)] + [(0, k) for k in range(4, KD)] + [(1, k) for k in range(4, KD)]
                    staggered(parts, KD, XH, XL, lambda k: (x1_lo[k % 2], k // 2 + 1))
                    a = 1
                with pe.Fori(a, nk) as i:
                    pair(i)
                n0 += 2 * nk

                def down(i):
                    for s in range(2):
                        half["v"] = n0 // 2 + i
                        unit(n0 + 2 * i + s, s, nk, AH, AL)
                parts = [(0, k) for k in range(nk - 1)] + [(1, k) for k in range(3)] + [(0, nk - 1)] + [(1, k) for k in range(3, nk)]
                staggered(parts, nk, AH, AL, lambda k: (a_lo, j0 + k + 1))
                with pe.Fori(1, KD // 2) as i:
                    down(i)
                n0 += KD
            half["v"] = None
            layer_norm(1, n0)

        @block.vector
        def _(dve):
            me = Lane(dve, dve_own)
            TT, TS, STT = dve.tensor_tensor, dve.tensor_scalar, dve.scalar_tensor_tensor

            def use(name):
                b, k = USES[name]
                dve.wait_ge(fill[b], k + 1)
                return psum[:, 6 + b, :], (free[b], k + 1)

            me(dve.memset(ones_rms[:, :], 1.0 / P))
            me(dve.memset(ones_ln[:, :], 1.0 / D))
            me(dve.memset(one[:, :], 1.0))
            me(dve.memset(eps_rms[:, :], RMS_EPS))
            me(dve.memset(eps_ln[:, :], LN_EPS), dconsts)
            def do(ins, event=None):
                me(ins, event)
                me.sync()

            def S(i):
                return sm[:, i, :]

            def powers(A, top):
                m, n = 1, A.shape[2]
                while m < top:
                    w = min(m, top - m)
                    src = A[:, :, :, 1:1 + w]
                    f = [A[:, i, :, m:m + 1].unsqueeze(1).to_broadcast([P, 2, n, w]) for i in range(2)]
                    u_ = [x[:, 0:2 * n * w].rearrange("p (i r n) -> p i r n", i=2, r=n) for x in (ta5, tb5)]
                    me(TT(u_[0], src, f[0], ALU.mult))
                    do(TT(u_[1], src, f[1], ALU.mult))
                    me(TT(A[:, 0, :, m + 1:m + 1 + w], u_[0][:, 0], u_[1][:, 1], ALU.subtract))
                    do(TT(A[:, 1, :, m + 1:m + 1 + w], u_[0][:, 1], u_[1][:, 0], ALU.add))
                    m *= 2

            def s5_angle():
                dve.wait_ge(p_dt, 1)
                dve.wait_ge(lam_in, 16)
                do(TS(S(8), lam[:, 0, :], -1e-4, None, ALU.min))
                me(TT(S(9), lam[:, 1, :], S(0), ALU.mult))
                do(TT(S(1), S(8), S(0), ALU.mult), p_e)
                do(TS(S(10), S(9), INV_TWO_PI, ROUND, ALU.mult, ALU.add))
                do(TS(S(10), S(10), ROUND, None, ALU.subtract))
                do(STT(S(9), S(10), -TWO_PI_1, S(9), ALU.mult, ALU.add))
                do(STT(S(9), S(10), -TWO_PI_2, S(9), ALU.mult, ALU.add))
                do(STT(S(9), S(10), -TWO_PI_3, S(9), ALU.mult, ALU.add))
                me(TS(S(4), S(9), PI_SAFE, -PI_SAFE, ALU.min, ALU.max))
                do(TS(S(11), S(9), 1.5707963267948966, None, ALU.add))
                do(TS(S(12), S(11), 3.141592653589793, -6.283185307179586, ALU.is_gt, ALU.mult))
                do(TT(S(11), S(11), S(12), ALU.add))
                do(TS(S(5), S(11), PI_SAFE, -PI_SAFE, ALU.min, ALU.max), p_ang)

            def s5_param():
                dve.wait_ge(p_sin, 1)
                lim, sin, cos, mag = lam[:, 1, :], S(6), S(7), S(2)
                me(TT(PW[:, 0, :, 1], mag, cos, ALU.mult))
                me(TT(PW[:, 1, :, 1], mag, sin, ALU.mult))
                me(dve.memset(PW[:, 0, :, 0], 1.0))
                me(dve.memset(PW[:, 1, :, 0], 0.0))
                me(dve.memset(E[:, 0, :, 0], 1.0))
                me(dve.memset(E[:, 1, :, 0], 0.0))
                me(TT(S(14), S(8), S(8), ALU.mult))
                do(TT(S(15), lim, lim, ALU.mult))
                ar, ai = PW[:, 0, :, 1], PW[:, 1, :, 1]
                me(TS(S(13), ar, -1.0, None, ALU.add))
                do(TT(S(14), S(14), S(15), ALU.add))
                me(dve.reciprocal(S(14), S(14)))
                me(TT(S(15), S(13), S(8), ALU.mult))
                me(TT(S(16), ai, lim, ALU.mult))
                me(TT(S(17), ai, S(8), ALU.mult))
                do(TT(S(18), S(13), lim, ALU.mult))
                me(TT(S(15), S(15), S(16), ALU.add))
                do(TT(S(17), S(17), S(18), ALU.subtract))
                me(TT(S(5), S(17), S(14), ALU.mult))
                do(TT(S(4), S(15), S(14), ALU.mult))
                x, y = cos, sin
                for i in range(3):
                    ox, oy = S(19 + 2 * i), S(20 + 2 * i)
                    me(TT(S(25), x, x, ALU.mult))
                    me(TT(S(26), y, y, ALU.mult))
                    do(TT(S(27), x, y, ALU.mult))
                    me(TT(ox, S(25), S(26), ALU.subtract))
                    do(TS(oy, S(27), 2.0, None, ALU.mult))
                    x, y = ox, oy
                powers(PW[:, :, :, :], L)

            for k in range(KD):
                dve.wait_ge(x_hi, k + 1)
                me(TT(XL[:, k, :], st[k % 3][:, 0:T], XH[:, k, :].bitcast(F32), ALU.subtract), x_lo)

            dve.wait_ge(small_in, 64)
            me(TT(lbt[:, 1, :], lbt[:, 0, :], lbt[:, 0, :], ALU.subtract), lbd)
            dve.wait_ge(lbe, 1)
            me(dve.reciprocal(lbt[:, 2, :], lbt[:, 1, :]))
            me.sync()
            me(TT(lbt[:, 2, :], lbt[:, 2, :], lbt[:, 1, :], ALU.mult))
            me.sync()
            me(TT(lb[:, :], lbt[:, 2, :], lbt[:, 2, :], ALU.subtract))
            me.sync()
            me(TS(oml[:, :], lb[:, :], -1.0, 1.0, ALU.mult, ALU.add))
            def s5_prep(c):
                p5, r4 = prm[c % 2], slice(PR * c, PR * c + PR)
                bre, bim, cre, cim = (p5[:, 64 * i:64 * i + 64].rearrange("p (r j) -> p r j", j=16) for i in range(4))
                PWv = PW[:, :, r4, :]
                dve.wait_ge(prm_in[c % 2], 16 * (c // 2 + 1))
                bc = lambda a: a[:, r4].unsqueeze(2).to_broadcast([P, PR, 16])
                t0, t1 = ([x[:, 64 * i:64 * i + 64].rearrange("p (r j) -> p r j", j=16) for i in range(2)] for x in (ta5, tb5))
                for i, (x, y) in enumerate(((bre, bim), (bim, bre))):
                    me(TT(t0[i], x, bc(S(4)), ALU.mult))
                    me(TT(t1[i], y, bc(S(5)), ALU.mult))
                me.sync()
                if c:
                    dve.wait_ge(*filled(("s5_y", c - 1, 3)))
                me(TT(bb[0][:, :, :], t0[0], t1[0], ALU.subtract))
                do(TT(bb[1][:, :, :], t0[1], t1[1], ALU.add))
                bt = lambda a: a.unsqueeze(3).to_broadcast([P, PR, L + 1, 16])
                bj = lambda a: a.unsqueeze(2).to_broadcast([P, PR, L + 1, 16])
                u0, u1 = (x[:, 0:PR * (L + 1) * 16].rearrange("p (r t j) -> p r t j", r=PR, t=L + 1) for x in (ta5, tb5))
                me(TT(u0, bj(cre), bt(PWv[:, 0]), ALU.mult))
                do(TT(u1, bj(cim), bt(PWv[:, 1]), ALU.mult))
                do(TT(CA[0][:, :, :, :], u0, u1, ALU.subtract))
                me(TT(u0, bj(cre), bt(PWv[:, 1]), ALU.mult))
                do(TT(u1, bj(cim), bt(PWv[:, 0]), ALU.mult))
                do(STT(CA[1][:, :, :, :].rearrange("p r t j -> p (r t j)"), ta5[:, 0:PR * (L + 1) * 16], -1.0,
                       tb5[:, 0:PR * (L + 1) * 16], ALU.mult, ALU.subtract), ca_ready)
                bt = lambda a: a.unsqueeze(3).to_broadcast([P, PR, L, 16])
                bj = lambda a: a.unsqueeze(2).to_broadcast([P, PR, L, 16])
                u0, u1 = (x[:, 0:PR * L * 16].rearrange("p (r t j) -> p r t j", r=PR, t=L) for x in (ta5, tb5))
                if c == 0:
                    dve.wait_ge(consts, 1)
                for i, op in ((0, ALU.subtract), (1, ALU.add)):
                    me(TT(u0, bj(bb[i][:, :, :]), bt(PWv[:, 0, :, 0:L]), ALU.mult))
                    do(TT(u1, bj(bb[1 - i][:, :, :]), bt(PWv[:, 1, :, 0:L]), ALU.mult))
                    do(TT(WB[i].rearrange("p r (t j) -> p r t j", j=16), u0, u1, op), wb_ready if i else None)

            def s5_k(c):
                for q in range(2):
                    ps, fr = use(("s5_k", c, q))
                    if c:
                        dve.wait_ge(t_in, 16 * L * c)
                    me(dve.tensor_copy(KS[:, q:GC:2, :], ps[0:16, :].rearrange("p (g n) -> p g n", g=4)), fr)
                    v = KS[:, q:GC:2, 0:16]
                    tv = ta5[0:16, 0:64].rearrange("p (g n) -> p g n", g=4)
                    do(TT(tv, ident[0:16, 0:16].unsqueeze(1).to_broadcast([16, 4, 16]),
                          dk[:, GC * c + q:GC * c + GC:2].unsqueeze(2).to_broadcast([16, 4, 16]), ALU.mult))
                    do(TT(v, v, tv, ALU.add), k_ready)
                r4 = slice(PR * c, PR * c + PR)
                me(dve.tensor_copy(E[:, 0, :, 1], S(23)[:, r4]))
                do(dve.tensor_copy(E[:, 1, :, 1], S(24)[:, r4]))
                powers(E[:, :, :, :], NL - 1)

            def s5_d(c):
                r4 = slice(PR * c, PR * c + PR)
                if c == 0:
                    dve.wait_ge(wv_lo, KD)
                for q in range(2):
                    (pr, fr), (pi, fi) = use(("s5_d", c, f"re{q}")), use(("s5_d", c, f"im{q}"))
                    vr, vi = (x[:, 0:2 * UC].rearrange("p (r n) -> p r n", r=2) for x in (pr, pi))
                    cs, sn = E[:, 0, 2 * q:2 * q + 2, :], E[:, 1, 2 * q:2 * q + 2, :]
                    x0, x1 = (x[:, 0:2 * NL].rearrange("p (r n) -> p r n", r=2) for x in (ta5, tb5))
                    x2, x3 = (x[:, 512:512 + 2 * NL].rearrange("p (r n) -> p r n", r=2) for x in (ta5, tb5))
                    r2 = slice(2 * q, 2 * q + 2)
                    pr_, pi_ = vr[:, :, NS:NS + NL], vi[:, :, NS:NS + NL]
                    me(TT(x0, pr_, cs, ALU.mult))
                    me(TT(x1, pi_, sn, ALU.mult))
                    me(TT(x2, pi_, cs, ALU.mult))
                    me(TT(x3, pr_, sn, ALU.mult))
                    me(dve.tensor_copy(ds_[0][:, r2, :], vr[:, :, NS + NL:UC]), fr)
                    me(dve.tensor_copy(ds_[1][:, r2, :], vi[:, :, NS + NL:UC]), fi)
                    me.sync()
                    me(TT(G5[0][:, r2, :], x0, x1, ALU.add))
                    me(TT(G5[1][:, r2, :], x2, x3, ALU.subtract))
                    me.sync()
                for i in range(2):
                    for r in range(PR):
                        me(dve.tensor_tensor_scan((ta5, tb5)[i][:, r * NL:(r + 1) * NL], sm[:, 3, PR * c + r:PR * c + r + 1].to_broadcast([P, NL]),
                                                  G5[i][:, r, :], 0.0, ALU.mult, ALU.add))
                me.sync()
                gr, gi = (x[:, 0:PR * NL].rearrange("p (r n) -> p r n", r=PR) for x in (ta5, tb5))
                y2, y3 = (x[:, 512:1024].rearrange("p (r n) -> p r n", r=PR) for x in (ta5, tb5))
                cs, sn = E[:, 0, :, :], E[:, 1, :, :]
                me(TT(G5[0][:, :, :], gr, cs, ALU.mult))
                me(TT(G5[1][:, :, :], gi, sn, ALU.mult))
                me(TT(y2, gr, sn, ALU.mult))
                me(TT(y3, gi, cs, ALU.mult))
                me.sync()
                dve.wait_ge(*freed(("s5_w", c, 1)))
                h0 = [prm[c % 2][:, 256 + 32 * i:288 + 32 * i].rearrange("p (r b) -> p r b", b=NS) for i in range(2)]
                me(dve.tensor_copy(H5[0][:, :, 0:NS], h0[0]))
                me(dve.tensor_copy(H5[1][:, :, 0:NS], h0[1]))
                me(TT(H5[0][:, :, NS + 1:HC], G5[0][:, :, :], G5[1][:, :, :], ALU.subtract))
                me(TT(H5[1][:, :, NS + 1:HC], y2, y3, ALU.add), h5_ready)
                me.sync()
                if c:
                    dve.wait_ge(s5_out, 16 * c)
                for i in range(2):
                    me(dve.tensor_copy(s5o[:, i, :, NS:NS + 1], H5[i][:, :, HC - 1:HC]))
                t4 = [x[:, 32 * i:32 * i + 32].rearrange("p (r b) -> p r b", b=NS) for i, x in enumerate((ta5, ta5, ta5, ta5))]
                ar, ai = (PW[:, i, r4, 1:2].to_broadcast([P, PR, NS]) for i in range(2))
                me(TT(t4[0], h0[0], ar, ALU.mult))
                me(TT(t4[1], h0[1], ai, ALU.mult))
                me(TT(t4[2], h0[0], ai, ALU.mult))
                me(TT(t4[3], h0[1], ar, ALU.mult))
                me.sync()
                me(TT(t4[0], t4[0], t4[1], ALU.subtract))
                me(TT(t4[2], t4[2], t4[3], ALU.add))
                me.sync()
                me(TT(s5o[:, 0, :, 0:NS], t4[0], ds_[0][:, :, :], ALU.add))
                me(TT(s5o[:, 1, :, 0:NS], t4[2], ds_[1][:, :, :], ALU.add), s5_full)
                me.sync()

            def hp_a(h):
                fz = FZ[h % 2]
                dve.wait_ge(sig_done, 2 * h + 1)
                if h:
                    dve.wait_ge(sn_ready, h)
                me(TS(fz[:, :], fz[:, :], oml[:, h:h + 1], lb[:, h:h + 1], ALU.mult, ALU.add))
                me(TS(K[h % 2][:, :], K[h % 2][:, :], oml[:, h:h + 1], None, ALU.mult))
                me.sync()
                me(TS(tB[:, 0:TP], fz[:, 0:TP], TWO60, F_FLOOR * TWO60, ALU.mult, ALU.max))
                me(TS(tA[:, 0:TP], fz[:, 0:TP], 1.0 / TWO60, None, ALU.max))
                me(TS(fz[:, TP:T], fz[:, TP:T], F_FLOOR, None, ALU.max))
                me.sync()
                me(TS(tB[:, 0:TP], tB[:, 0:TP], 1.0, None, ALU.min), lnarg)

            def hp_b(h):
                dve.wait_ge(ln_done, h + 1)
                me(TT(tA[:, 0:TP], tA[:, 0:TP], tB[:, 0:TP], ALU.add))
                me.sync()
                for k in range(NC):
                    t = slice(k * CH, (k + 1) * CH)
                    me(dve.tensor_tensor_scan(B[h % 2][:, t], one[:, 0:1].to_broadcast([P, CH]), tA[:, t], 0.0, ALU.mult, ALU.add),
                       b_ready if k == NC - 1 else None)
                me.sync()

            def halves(ap, hh):
                v = ap[:, 0:TP].rearrange("p (b two x) -> p b two x", two=2, x=hh)
                return v[:, :, 0, :], v[:, :, 1, :], v[:, :, 0, hh - 1:hh].to_broadcast([P, TP // (2 * hh), hh])

            def sub(h, l):
                if l > 3:
                    dve.wait_ge(*filled(("level", h, l - 3, 0)))
                elif h:
                    dve.wait_ge(*filled({1: ("level", h - 1, 7, 0), 2: ("kt", h - 1, 1), 3: ("level", h - 1, 6, 0)}[l]))
                if l == 8:
                    ev = EL[7 % 3][:, 0:TP].rearrange("p (c n) -> p c n", c=NC)
                    bv = B[h % 2][:, 0:TP].rearrange("p (c n) -> p c n", c=NC)
                    me(TT(ev, bv[:, :, CH - 1:CH].to_broadcast([P, NC, CH]), bv, ALU.subtract), ex_arg)
                    return
                hh = LEVELS[l - 1]
                e0, e1, _ = halves(EL[(l - 1) % 3], hh)
                b0, b1, mid = halves(B[h % 2], hh)
                me(TT(e0, mid, b0, ALU.subtract))
                me(TT(e1, b1, mid, ALU.subtract), ex_arg)

            def mul(h, l):
                dve.wait_ge(ex_done, 8 * h + l)
                e = EL[(l - 1) % 3]
                if l == 8:
                    me(TT(e[:, 0:TP], e[:, 0:TP], K[h % 2][:, 0:TP], ALU.mult), lv_ready)
                    return
                hh = LEVELS[l - 1]
                e0, e1, _ = halves(e, hh)
                me(TT(e0, e0, halves(K[h % 2], hh)[0], ALU.mult))
                me(TT(e1, e1, halves(Q[h % 2], hh)[1], ALU.mult), lv_ready)

            def level(h, l):
                if l:
                    hh = LEVELS[l - 1]
                    half2 = lambda a: a.rearrange("p c (b two x) -> p c b two x", two=2, x=hh)[:, :, :, 1, :]
                    ps, fr = use(("level", h, l, 0))
                    me(dve.copy_predicated(half2(SC[:, :, :]), half2(masks[:, l:l + 1, :]).to_broadcast([P, NC, CH // (2 * hh), hh]),
                                           ps.rearrange("p (c b x) -> p c b x", c=NC, x=hh)), fr)
                    me.sync()
                    return
                for b in range(2):
                    ps, fr = use(("level", h, l, b))
                    me(dve.copy_predicated(SC[:, 4 * b:4 * b + 4, :], masks[:, l:l + 1, :].to_broadcast([P, 4, CH]),
                                           ps.rearrange("p (c n) -> p c n", c=4)), fr)
                me.sync()

            def kv(h):
                dve.wait_ge(ex_a8, h + 1)
                if h:
                    dve.wait_ge(hp_saved, 16 * h)
                for b in range(2):
                    ps, fr = use(("kv", h, b))
                    for i in range(4):
                        k = 4 * b + i
                        me.sync()
                        me(STT(S_all[:, k + 1, :], S_all[:, k, :], A8[:, k:k + 1], ps[:, i * P:(i + 1) * P], ALU.mult, ALU.add),
                           fr if i == 3 else None)
                me.sync()

            def vb(h):
                tv = tA[:, 0:TP].rearrange("p (b n) -> p b n", b=NS)
                for b in range(2):
                    ps, fr = use(("vb", h, b))
                    me(TT(tv[:, 4 * b:4 * b + 4, :], ps.rearrange("p (b n) -> p b n", b=4),
                          K[h % 2][:, TP + 4 * b:TP + 4 * b + 4].unsqueeze(2).to_broadcast([P, 4, P]), ALU.mult), fr)

            def fin(h):
                dve.wait_ge(rms_e, h + 1)
                me(TT(O[:, :], O[:, :], tB[:, :], ALU.mult))
                me.sync()
                dve.wait_ge(sig_done, 2 * h + 2)
                me(STT(O[:, :], O[:, :], ng[:, :], SG[h % 2][:, :], ALU.mult, ALU.mult), o_full)

            first_level = True
            for step in ORDER:
                kind, c = step[0], step[1]
                if kind == "s5_param":
                    s5_angle()
                    s5_param()
                elif kind == "s5_prep":
                    s5_prep(c)
                elif kind == "s5_k":
                    s5_k(c)
                elif kind == "s5_d" and step[2] == 0:
                    s5_d(c)
                elif kind == "hp_a":
                    if c == 0:
                        dve.wait_ge(*filled(("s5_y", HEADS - 1, 3)))
                    hp_a(c)
                elif kind == "hp_b":
                    hp_b(c)
                elif kind == "sub":
                    sub(c, step[2])
                elif kind == "mul":
                    mul(c, step[2])
                elif kind == "level":
                    if first_level:
                        dve.wait_ge(consts, 2)
                        first_level = False
                    level(c, step[2])
                elif kind == "kv":
                    kv(c)
                elif kind == "vb":
                    vb(c)
                elif kind == "fin":
                    fin(c)
                elif kind == "z":
                    m = c
                    dve.wait_ge(*evacuated(GLU_N + m))
                    if m:
                        dve.wait_ge(z_lo, m)
                    me(TT(st[2][:, 0:T], XH[:, m, :].bitcast(F32), XL[:, m, :].bitcast(F32), ALU.add))
                    me.sync()
                    me(TT(st[2][:, 0:T], st[2][:, 0:T], st[1][:, 0:T], ALU.mult), z_ready)
                elif kind == "unit" and c >= OUT_N:
                    m = c - OUT_N
                    dve.wait_ge(mm_done, c + 1)
                    dve.wait_ge(xt_in[m % 2], 16 * (m // 2 + 1))
                    if m == 0:
                        dve.wait_ge(o_out, 16 * (HEADS - 1))
                        dve.wait_ge(hp_saved, 16 * HEADS)
                        dve.wait_ge(hs_saved, 16 * HEADS)
                        dve.wait_ge(m_lo, HEADS)
                    me(STT(b3(R[:, m, :]), b3(xt[m % 2][:, :]), ALPHA, banks(c % 2), ALU.mult, ALU.add), evacuated(c))

            def layer_norm(w):
                dve.wait_ge(mean_mm, w + 1)
                for m in range(KD):
                    me(TT(b3(R[:, m, :]), b3(R[:, m, :]), banks(0), ALU.subtract), xc_ready)
                dve.wait_ge(var_e, w + 1)
                def low(m):
                    dve.wait_ge(x1_hi, m + 1)
                    me(TT(XL[:, m, :], R[:, m, :], XH[:, m, :].bitcast(F32), ALU.subtract), x1_lo[0])

                for m in range(KD):
                    me(TT(R[:, m, :], R[:, m, :], rstd[:, :], ALU.mult), t_ready)
                    if w == 0 and m % 2:
                        low(m - 1)

            layer_norm(0)
            dve.wait_ge(x1_lo[1], KD // 2)
            me(dve.memset(ub[0][:, 0:2], 0.0))
            me(dve.memset(ub[1][:, 0:2], 0.0), halo)
            n0 = FFN_N
            tick = 0
            for q, (j0, nk) in enumerate(PARTS):
                def pair(i):
                    for s in range(2):
                        jj = 2 * (j0 + i) + s
                        dve.wait_ge(evac[s], (n0 // 2) + i + 1)
                        dve.wait_ge(u_full, jj + 1)
                        dve.wait_ge(cp_in[s], 16 * (j0 + i + 1))
                        h_, u_, w = hb[s], ub[s], cp[s]
                        STT(h_[:, 0:TP], u_[:, 1:1 + TP], w[:, 1:2], h_[:, 0:TP], ALU.mult, ALU.add)
                        STT(h_[:, TP:T], w[:, 12:20], w[:, 1:2], h_[:, TP:T], ALU.mult, ALU.add).then_inc(h0_ready, 1)
                        dve.wait_ge(h0_ready, jj + 1)
                        STT(h_[:, 0:TP], u_[:, 0:TP], w[:, 0:1], h_[:, 0:TP], ALU.mult, ALU.add)
                        STT(h_[:, TP:T], w[:, 4:12], w[:, 0:1], h_[:, TP:T], ALU.mult, ALU.add).then_inc(conv_done, 1)
                    dve.wait_ge(silu_done, j0 + i + 1)
                    TT(hb[0][:, :], hb[0][:, :], hb[1][:, :], ALU.mult).then_inc(a_ready, 1)
                with dve.Fori(0, nk) as i:
                    pair(i)
                n0 += 2 * nk

                def down(i):
                    for s in range(2):
                        m = bass.ds(2 * i + s, 1)
                        n = n0 + 2 * i + s
                        dve.wait_ge(mm_done, n + 1)
                        r = R[:, m, :].rearrange("p a n -> p (a n)")
                        if q == 0:
                            STT(b3(r), b3(r), ALPHA, banks(s), ALU.mult, ALU.add).then_inc(evac[s], 1)
                        else:
                            TT(b3(r), b3(r), banks(s), ALU.add).then_inc(evac[s], 1)
                with dve.Fori(0, KD // 2) as i:
                    down(i)
                n0 += KD
            dve.wait_ge(evac[0], n0 // 2)
            dve.wait_ge(evac[1], n0 // 2)
            layer_norm(1)


_OUTS = [((KD, P, T), "yT"), ((HEADS, P, P), "hp"), ((HEADS, P, 2, PR, NS + 1), "s5st"),
         ((2 * JT, P, 2 + NS), "cache_new"), ((NS, HEADS, P, P), "hs"), ((NS, 2 * FF), "cache_row0")]


def _layout(x_prompt, x_sample, state_hgrn, state_s5_re, state_s5_im, cache_ffn_conv, w_in, hgrn_lb_logits, hgrn_norm_g,
            s5_lambda_re, s5_lambda_im, s5_log_dt, s5_b_re, s5_b_im, s5_c_re, s5_c_im, s5_d, w_glu, w_out, ln1_g, ln1_b,
            w_ffn_up, ffn_conv_w, ffn_conv_b, w_ffn_down, ln2_g, ln2_b):
    import numpy as np

    def tiles(w, kt, nt):
        return w.reshape(kt, P, nt, P).transpose(2, 1, 0, 3).reshape(nt, P, kt * P)

    x = np.concatenate([x_prompt[0], x_sample[:, 0]], axis=0)
    win = tiles(w_in[0], KD, 20)
    order_in = [16 + c for c in range(4)] + [b + h for h in range(4) for b in (4, 0, 12)]
    up = [t + JT * s for t in range(JT) for s in range(2)]

    def per_group(a):
        a = a.reshape((HEADS, PR, 2, SS) + a.shape[2:])
        return np.moveaxis(a, 1, 3).reshape((HEADS, P, -1))

    ldt = np.broadcast_to(s5_log_dt[0][:, None], (G, SS))
    s5q = np.stack([per_group(a) for a in (s5_lambda_re[0], s5_lambda_im[0], ldt)]).transpose(2, 0, 1, 3).reshape(P, -1)
    s5p = np.concatenate([per_group(a) for a in (
        s5_b_re[0], s5_b_im[0],
        s5_c_re[0].transpose(0, 2, 1), s5_c_im[0].transpose(0, 2, 1),
        state_s5_re[0].transpose(1, 2, 0), state_s5_im[0].transpose(1, 2, 0))], axis=2)
    cache = cache_ffn_conv[0]
    by_tile = lambda a: a.reshape(-1, 2 * JT, P).transpose(1, 2, 0)[up]
    convp = np.concatenate([by_tile(ffn_conv_w[0]), by_tile(ffn_conv_b), by_tile(cache[:, 0]), by_tile(cache[:, 1])], axis=2)
    d = dict(
        xT=x.T.reshape(KD, P, T), w_units=win[order_in], w_v=w_in[0][:, 1024:1536].reshape(KD, P, 512),
        w_glu=tiles(w_glu[0], HEADS, HEADS), w_out=tiles(w_out[0], KD, KD), w_up=tiles(w_ffn_up[0], KD, 2 * JT)[up],
        w_dn=tiles(w_ffn_down[0], JT, KD), s5q=s5q, s5p=s5p, dskip=s5_d[0].reshape(G, 16).T,
        lbl=hgrn_lb_logits[0].reshape(HEADS, P).T, normg=hgrn_norm_g.T,
        lnp=np.stack([a.reshape(KD, P).T for a in (ln1_g[0], ln1_b[0], ln2_g[0], ln2_b[0])], axis=1),
        convp=convp, s0=state_hgrn[0], cache_old=cache)
    return {k: np.ascontiguousarray(v) for k, v in d.items()}


def kernel(**inputs):
    import numpy as np
    import concourse.bacc as bacc
    from concourse.bass_utils import run_bass_kernel_spmd

    nc = bacc.Bacc("TRN2", target_bir_lowering=False, num_devices=1)
    arrays = _layout(**{k: np.asarray(v) for k, v in inputs.items()})
    args = [nc.dram_tensor(f"in_{k}", a.shape, F32, kind="ExternalInput").ap() for k, a in arrays.items()]
    args += [nc.dram_tensor(f"out_{k}", shape, F32, kind="ExternalOutput").ap() for shape, k in _OUTS]
    layer(nc, *args)
    r = run_bass_kernel_spmd(nc, [{f"in_{k}": a for k, a in arrays.items()}], core_ids=[0]).results[0]
    yT, hp, s5st, cn, hs, row0 = (r[f"out_{k}"] for _, k in _OUTS)
    y = yT.reshape(D, T).T
    s5 = s5st.reshape(HEADS, 2, SS, 2, PR, NS + 1).transpose(3, 5, 0, 4, 1, 2).reshape(2, NS + 1, G, SS)
    down = [2 * t + s for s in range(2) for t in range(JT)]
    rows = cn[down].reshape(2 * FF, 2 + NS).T
    return (np.ascontiguousarray(y[:TP])[None], np.ascontiguousarray(y[TP:])[:, None], hp[None, None],
            np.ascontiguousarray(s5[0, NS:])[None], np.ascontiguousarray(s5[1, NS:])[None],
            np.ascontiguousarray(rows[:2])[None, None], hs[None],
            np.ascontiguousarray(s5[0, :NS])[None], np.ascontiguousarray(s5[1, :NS])[None],
            np.stack([row0, rows[2:]], axis=1)[None])
```
